# Optimizing a Trainium2 kernel written in Bass

```python
import math
import jax, jax.numpy as jnp
from jax import lax
import numpy as np

D_MODEL = 2048
BATCH = 1
SEQ = 256
DEPTH = 1

HEAD_DIM = 64
SWA_HEADS = 16
SWA_KV_HEADS = 2
SWA_WINDOW = 128
DSA_HEADS = 8
DSA_KV_RANK = 128
IDX_HEADS = 8
IDX_DIM = 64
DSA_TOPK_MAX = 256
QBLOCK = 128
RET_HEADS = 8
RET_CHUNK = 128
A_WIDTH = SWA_HEADS * HEAD_DIM
B_WIDTH = DSA_HEADS * HEAD_DIM
C_WIDTH = RET_HEADS * HEAD_DIM
MIX_WIDTH = A_WIDTH + B_WIDTH + C_WIDTH
MIX_COLS = (
    A_WIDTH, SWA_KV_HEADS * HEAD_DIM, SWA_KV_HEADS * HEAD_DIM,
    B_WIDTH, DSA_KV_RANK, IDX_HEADS * IDX_DIM, IDX_DIM, IDX_HEADS,
    C_WIDTH, C_WIDTH, C_WIDTH, C_WIDTH,
)
MIX_IN_WIDTH = sum(MIX_COLS)
MIX_SPLITS = [int(v) for v in np.cumsum(MIX_COLS)[:-1]]
D_FF = 5504
N_MOD = 9
EPS = 1e-6

kernel_name = "hymba_style_swa_dsa_retention_macaron"

def rms_norm(x, g):
    xf = x.astype(jnp.float32)
    y = xf * lax.rsqrt(jnp.mean(xf * xf, axis=-1, keepdims=True) + EPS)
    return (y * g.astype(jnp.float32)).astype(x.dtype)

def alibi_slopes(n):
    return jnp.asarray(2.0 ** (-8.0 * np.arange(1, n + 1) / n), dtype=jnp.float32)

def swiglu(h, w_in, w_out):
    gate, up = jnp.split(h @ w_in, 2, axis=-1)
    return (jax.nn.silu(gate) * up) @ w_out

def swa_attention(q, k, v, sinks):
    b, s, _, dh = q.shape
    w = SWA_WINDOW
    nb = s // w
    g = SWA_HEADS // SWA_KV_HEADS
    f32 = jnp.float32
    qb = q.reshape(b, nb, w, SWA_KV_HEADS, g, dh)

    def band(t):
        prev = jnp.pad(t, ((0, 0), (w, 0), (0, 0), (0, 0)))[:, :s]
        return jnp.concatenate([prev.reshape(b, nb, w, SWA_KV_HEADS, dh),
                                t.reshape(b, nb, w, SWA_KV_HEADS, dh)], axis=2)

    kb, vb = band(k), band(v)
    i = jnp.arange(w)[:, None]
    j = jnp.arange(2 * w)[None, :]
    dist = i - j + w
    key_pos = jnp.arange(nb)[:, None, None] * w - w + j[None]
    valid = (dist >= 0) & (dist < w) & (key_pos >= 0)
    slopes = alibi_slopes(SWA_HEADS).reshape(SWA_KV_HEADS, g)[:, :, None, None, None]
    scores = jnp.einsum('bnihgd,bnjhd->bhgnij', qb, kb).astype(f32) * dh ** -0.5
    scores = jnp.where(valid, scores - slopes * dist.astype(f32), -jnp.inf)
    sink = sinks.astype(f32).reshape(SWA_KV_HEADS, g)[:, :, None, None, None]
    m = jnp.maximum(scores.max(axis=-1, keepdims=True), sink)
    e = jnp.exp(scores - m)
    p = e / (e.sum(axis=-1, keepdims=True) + jnp.exp(sink - m))
    out = jnp.einsum('bhgnij,bnjhd->bnihgd', p.astype(v.dtype), vb)
    return out.reshape(b, s, SWA_HEADS * dh)

def dsa_attention(q, ckv, iq, ik, iw, w_uk, w_uv):
    b, s, _, dh = q.shape
    f32 = jnp.float32
    topk = min(DSA_TOPK_MAX, s // 4)
    nb = s // QBLOCK
    slopes = alibi_slopes(DSA_HEADS)[None, :, None, None]
    q_lat = jnp.einsum('bshd,rhd->bshr', q, w_uk)
    key_pos = jnp.arange(s)

    def to_blocks(t):
        return jnp.moveaxis(t.reshape((b, nb, QBLOCK) + t.shape[2:]), 1, 0)

    def one_block(args):
        blk, ql, iqb, iwb = args
        t = blk * QBLOCK + jnp.arange(QBLOCK)
        logit = jnp.einsum('bthd,bsd->bths', iqb, ik).astype(f32) * IDX_DIM ** -0.5
        score = jnp.einsum('bth,bths->bts', iwb.astype(f32) * IDX_HEADS ** -0.5, jax.nn.relu(logit))
        score = jnp.where(key_pos[None, None, :] <= t[None, :, None], score, -jnp.inf)
        _, idx = lax.top_k(score, topk)
        c_sel = jax.vmap(lambda cc, ii: cc[ii])(ckv, idx)
        att = jnp.einsum('bthr,btkr->bhtk', ql, c_sel).astype(f32) * dh ** -0.5
        dist = (t[:, None] - idx).astype(f32)
        att = att - slopes * dist[:, None]
        att = jnp.where((idx <= t[:, None])[:, None], att, -jnp.inf)
        p = jax.nn.softmax(att, axis=-1)
        return jnp.einsum('bhtk,btkr->bthr', p.astype(c_sel.dtype), c_sel)

    o = lax.map(one_block, (jnp.arange(nb), to_blocks(q_lat), to_blocks(iq), to_blocks(iw)))
    o = jnp.moveaxis(o, 0, 1).reshape(b, s, DSA_HEADS, DSA_KV_RANK)
    return jnp.einsum('bshr,rhd->bshd', o, w_uv).reshape(b, s, DSA_HEADS * dh)

def retention(q, k, v, gate, norm_g):
    b, s, h, dh = q.shape
    f32 = jnp.float32
    cs = RET_CHUNK
    nc = s // cs
    lg = jnp.log(1.0 - 2.0 ** (-5.0 - jnp.arange(h, dtype=f32)))
    i = jnp.arange(cs, dtype=f32)
    diff = i[:, None] - i[None, :]
    inner_decay = jnp.where(diff >= 0, jnp.exp(lg[:, None, None] * jnp.maximum(diff, 0.0)), 0.0)
    q_decay = jnp.exp(lg[None, :] * (i[:, None] + 1.0))[None, :, :, None]
    k_decay = jnp.exp(lg[None, :] * (cs - 1.0 - i[:, None]))[None, :, :, None]
    chunk_decay = jnp.exp(lg * cs)[None, :, None, None]

    def to_chunks(t):
        return jnp.moveaxis(t.reshape(b, nc, cs, h, dh), 1, 0)

    def step(state, xs):
        qc, kc, vc = (t.astype(f32) for t in xs)
        kc = kc * dh ** -0.5
        inner = jnp.einsum('bihd,bjhd->bhij', qc, kc) * inner_decay
        out = jnp.einsum('bhij,bjhd->bihd', inner, vc)
        out = out + jnp.einsum('bihd,bhde->bihe', qc, state) * q_decay
        state = state * chunk_decay + jnp.einsum('bjhd,bjhe->bhde', kc * k_decay, vc)
        return state, out

    state0 = jnp.zeros((b, h, dh, dh), f32)
    _, o = lax.scan(step, state0, (to_chunks(q), to_chunks(k), to_chunks(v)))
    o = jnp.moveaxis(o, 0, 1).reshape(b, s, h, dh)
    mu = jnp.mean(o, axis=-1, keepdims=True)
    var = jnp.mean(jnp.square(o - mu), axis=-1, keepdims=True)
    o = ((o - mu) * lax.rsqrt(var + EPS)).reshape(b, s, h * dh) * norm_g.astype(f32)
    return (o * jax.nn.silu(gate.astype(f32))).astype(q.dtype)

def token_mixer(h, w_in, w_out, sinks, kv_norm, w_uk, w_uv, ret_norm):
    b, s, _ = h.shape
    aq, ak, av, bq, bkv, biq, bik, biw, cq, ck, cv, cg = jnp.split(h @ w_in, MIX_SPLITS, axis=-1)

    def heads(t, n):
        return t.reshape(b, s, n, HEAD_DIM)

    oa = swa_attention(heads(aq, SWA_HEADS), heads(ak, SWA_KV_HEADS), heads(av, SWA_KV_HEADS), sinks)
    ob = dsa_attention(heads(bq, DSA_HEADS), rms_norm(bkv, kv_norm),
                       biq.reshape(b, s, IDX_HEADS, IDX_DIM), bik, biw, w_uk, w_uv)
    oc = retention(heads(cq, RET_HEADS), heads(ck, RET_HEADS), heads(cv, RET_HEADS), cg, ret_norm)
    return jnp.concatenate([oa, ob, oc], axis=-1) @ w_out

def sandwich(x, fn, g_pre, g_post, shift, scale, gate, res_w):
    h = rms_norm(x, g_pre) * (1.0 + scale[:, None]) + shift[:, None]
    y = rms_norm(fn(h), g_post)
    return x + res_w * gate[:, None] * y

def setup_inputs(seed: int = 0) -> dict:
    key = jax.random.key(seed)
    ks = jax.random.split(key, 17)
    f32 = jnp.float32
    nrm = lambda k, shp, sc: jax.random.normal(k, shp, f32) * sc
    return {
        "x": nrm(ks[0], (BATCH, SEQ, D_MODEL), 1.0),
        "c": nrm(ks[1], (BATCH, D_MODEL), 1.0),
        "ada_w": nrm(ks[2], (DEPTH, D_MODEL, N_MOD * D_MODEL), 0.5 * D_MODEL ** -0.5),
        "ada_b": nrm(ks[3], (DEPTH, N_MOD * D_MODEL), 0.01),
        "norm_g": 1.0 + nrm(ks[4], (DEPTH, 6, D_MODEL), 0.05),
        "ffn1_w_in": nrm(ks[5], (DEPTH, D_MODEL, 2 * D_FF), D_MODEL ** -0.5),
        "ffn1_w_out": nrm(ks[6], (DEPTH, D_FF, D_MODEL), D_FF ** -0.5),
        "ffn2_w_in": nrm(ks[7], (DEPTH, D_MODEL, 2 * D_FF), D_MODEL ** -0.5),
        "ffn2_w_out": nrm(ks[8], (DEPTH, D_FF, D_MODEL), D_FF ** -0.5),
        "mix_w_in": nrm(ks[9], (DEPTH, D_MODEL, MIX_IN_WIDTH), D_MODEL ** -0.5),
        "mix_w_out": nrm(ks[10], (DEPTH, MIX_WIDTH, D_MODEL), MIX_WIDTH ** -0.5),
        "swa_sinks": nrm(ks[11], (DEPTH, SWA_HEADS), 1.0),
        "dsa_kv_norm": 1.0 + nrm(ks[12], (DEPTH, DSA_KV_RANK), 0.05),
        "dsa_w_uk": nrm(ks[13], (DEPTH, DSA_KV_RANK, DSA_HEADS, HEAD_DIM), DSA_KV_RANK ** -0.5),
        "dsa_w_uv": nrm(ks[14], (DEPTH, DSA_KV_RANK, DSA_HEADS, HEAD_DIM), DSA_KV_RANK ** -0.5),
        "ret_norm": 1.0 + nrm(ks[15], (DEPTH, C_WIDTH), 0.05),
    }

def reference(x, c, ada_w, ada_b, norm_g, ffn1_w_in, ffn1_w_out, ffn2_w_in, ffn2_w_out,
              mix_w_in, mix_w_out, swa_sinks, dsa_kv_norm, dsa_w_uk, dsa_w_uv, ret_norm):
    cond = jax.nn.silu(c)
    for l in range(DEPTH):
        mod = cond @ ada_w[l] + ada_b[l]
        sh1, sc1, gt1, sh2, sc2, gt2, sh3, sc3, gt3 = jnp.split(mod, N_MOD, axis=-1)
        x = sandwich(x, lambda h: swiglu(h, ffn1_w_in[l], ffn1_w_out[l]),
                     norm_g[l, 0], norm_g[l, 1], sh1, sc1, gt1, 0.5)
        x = sandwich(x, lambda h: token_mixer(h, mix_w_in[l], mix_w_out[l], swa_sinks[l], dsa_kv_norm[l],
                                              dsa_w_uk[l], dsa_w_uv[l], ret_norm[l]),
                     norm_g[l, 2], norm_g[l, 3], sh2, sc2, gt2, 1.0)
        x = sandwich(x, lambda h: swiglu(h, ffn2_w_in[l], ffn2_w_out[l]),
                     norm_g[l, 4], norm_g[l, 5], sh3, sc3, gt3, 0.5)
    return x


_drawn_inputs = setup_inputs


def setup_inputs(seed=0):
    import zlib

    import numpy as np

    out = dict(_drawn_inputs(seed))
    spreads = {}
    factors = {}
    for name, (base, spread) in spreads.items():
        noise = np.random.default_rng([zlib.crc32(name.encode()), seed]).standard_normal(out[name].shape)
        drawn = base * np.exp(spread * noise) if base else spread * noise
        out[name] = __import__('jax').numpy.asarray(drawn.astype(out[name].dtype))
    for name, factor in factors.items():
        out[name] = (out[name] * factor).astype(out[name].dtype)
    return out
```

```python
from contextlib import ExitStack

import numpy as np

import concourse.bass as bass
from concourse import mybir

ALU = mybir.AluOpType
ACT = mybir.ActivationFunctionType
F32 = mybir.dt.float32
F32R = mybir.dt.float32r
AX_X = mybir.AxisListType.X

P = 128
SEQ, D, DFF = 256, 2048, 5504
TILES = SEQ // P
KD = D // P
NB = 512
HD = 64
A_HEADS, A_KV, B_HEADS, C_HEADS = 16, 2, 8, 8
KV_RANK = 128
EPS = 1e-6
BIG = 1e30

COLS = (A_HEADS * HD, A_KV * HD, A_KV * HD, B_HEADS * HD, KV_RANK, B_HEADS * HD, HD, B_HEADS,
        C_HEADS * HD, C_HEADS * HD, C_HEADS * HD, C_HEADS * HD)
AQ, AK, AV, BQ, BKV, BIQ, BIK, BIW, CQ, CK, CV, CG = [sum(COLS[:i]) for i in range(len(COLS))]
MIX_IN = sum(COLS)
TOPK = min(256, SEQ // 4)

FBLOCKS = -(-DFF // NB)
TAIL = DFF - (FBLOCKS - 1) * NB
LOOP = 8
PBLOCKS = -(-MIX_IN // NB)
PTAIL = MIX_IN - (PBLOCKS - 1) * NB

FFN_GROUPS = 3 * FBLOCKS
G_FFN = (0, FFN_GROUPS + PBLOCKS + 4)
G_IN = FFN_GROUPS
G_OUT = G_IN + PBLOCKS
Y_FFN = (0, 4 * FBLOCKS + 16)
Y_OUT = 4 * FBLOCKS
PRE_USES = 8
ADA_PRE = 32
ADA_FFN = (ADA_PRE, ADA_PRE + 64 + 32)
ADA_IN = ADA_PRE + 64
MODS_PRE = ((0, 1), (1, 2))
MODS_FFN = (((2, 1), (3, 2), (4, 3), (5, 0)), ((8, 3),))
MODS_IN = ((6, 1), (7, 2))


def need(eng, sem, value):
    if isinstance(value, int) and value <= 0:
        return
    eng.wait_ge(sem, value)


def build(nc, x_in, c_in, ada_w, ada_b, norm_g, f1_in, f1_out, f2_in, f2_out, m_in, m_out, sinks_in,
          kvn_in, uk_in, uv_in, rn_in, consts, out):
    ctx = ExitStack()
    with ctx:
        def sb(name, shape, dt=F32):
            return ctx.enter_context(nc.sbuf_tensor(name, shape, dt))

        def sem(name):
            return ctx.enter_context(nc.semaphore(name))

        x_sb = sb("x_sb", [P, TILES, D])
        xT_hi = sb("xT_hi", [P, KD, SEQ], F32R)
        xT_lo = sb("xT_lo", [P, KD, SEQ], F32R)
        w_raw = sb("w_raw", [P, 4, 4, NB])
        w_hi = sb("w_hi", [P, 4, 2, NB], F32R)
        w_lo = sb("w_lo", [P, 4, 2, NB], F32R)
        hT_hi = sb("hT_hi", [P, 4, SEQ], F32R)
        hT_lo = sb("hT_lo", [P, 4, SEQ], F32R)
        ada_raw = sb("ada_raw", [P, 2, D])
        work_w = 7056
        arena = sb("arena", [P, 4 * D + work_w])
        acc = arena[:, 0:4 * D].rearrange("p (m d) -> p m d", m=4)
        work = arena[:, 4 * D:4 * D + work_w]
        yacc = work[:, 0:TILES * D].rearrange("p (t d) -> p t d", t=TILES)
        silu = work[:, 4096:5120].rearrange("p (t n) -> p t n", t=TILES)
        hbuf = work[:, 5120:6144].rearrange("p (t n) -> p t n", t=TILES)
        junk = work[:, 4096:6144]
        proj = arena[:, 3 * D:3 * D + TILES * MIX_IN].rearrange("p (t n) -> p t n", t=TILES)
        assert 3 * D + TILES * MIX_IN <= 4 * D + work_w
        ident = sb("ident", [P, P])
        ones = sb("ones", [P, P])
        dist_a = sb("dist_a", [P, 3 * P])
        dist_b = sb("dist_b", [P, 3 * P])
        kvg = sb("kvg", [P, KV_RANK])
        rows64 = sb("rows64", [4 * KD, P])
        cond = sb("cond", [P, KD])
        gpre = sb("gpre", [P, 3, KD])
        modcol = sb("modcol", [P, 3, 2, KD])
        sink = sb("sink", [P, A_HEADS])
        negsink = sb("negsink", [P, A_HEADS])
        iws = sb("iws", [P, TILES, B_HEADS])
        ss = sb("ss", [P, 8])
        rstd = sb("rstd", [P, 8])
        neghalf = sb("neghalf", [P, 16])
        stat = sb("stat", [P, 2, 12])
        rstat = sb("rstat", [P, 4, 16])
        top8 = sb("top8", [P, TILES, 8])
        t1 = arena[:, D:3 * D]
        t2 = ada_raw[:, :, :].rearrange("p a n -> p (a n)")
        t3 = w_raw[:, 2:4].rearrange("p a b n -> p (a b n)")
        qT_a = t1[:, 0:2048].rearrange("p (c n) -> p c n", n=SEQ)
        qlatT = w_raw[:, 1].rearrange("p b n -> p (b n)").rearrange("p (c n) -> p c n", n=SEQ)
        qT_b = t1[:, 2048:3072].rearrange("p (c n) -> p c n", n=SEQ)
        iqT = t1[:, 3072:4096].rearrange("p (c n) -> p c n", n=SEQ)
        cqT, ckT = qT_b, iqT
        sc = t2[:, 0:768].rearrange("p (b n) -> p b n", b=2)
        pr = t2[:, 768:1536].rearrange("p (b n) -> p b n", b=2)
        pT = t2[:, 1536:2304].rearrange("p (b n) -> p b n", b=2)
        akT = t2[:, 2304:2816].rearrange("p (c n) -> p c n", n=SEQ)
        ikT = t2[:, 2816:3072]
        ckvT = t2[:, 3072:3328]
        ckv = t2[:, 3328:3584].rearrange("p (t n) -> p t n", t=TILES)
        olatT = t2[:, 3584:4096].rearrange("p (b n) -> p b n", b=2)
        w_uk = t3[:, 0:512]
        w_uv = t3[:, 512:1024]
        w_ukT = t3[:, 1024:1536].rearrange("p (c n) -> p c n", n=P)
        score = t3[:, 1536:1920]
        pick = t3[:, 1920:2304]
        dist_sel = t3[:, 2304:2688]
        rw = t3[:, 2688:3072]
        kdup = t3[:, 3072:3840].rearrange("p (t s n) -> p t s n", t=TILES, s=3)
        decay = t1[:, 0:2048].rearrange("p (h n) -> p h n", n=SEQ)
        rnorm = w_raw[:, 0, 0, :]
        ro = w_raw[:, 0, 1:3, :]
        cent = t1[:, 0:1024].rearrange("p (t n) -> p t n", t=TILES)
        csq = t1[:, 1024:2048].rearrange("p (t n) -> p t n", t=TILES)
        cgate = t2[:, 3072:4096].rearrange("p (t n) -> p t n", t=TILES)

        ps_g = ctx.enter_context(nc.psum_tensor("ps_g", [P, 2, NB], F32))
        ps_u = ctx.enter_context(nc.psum_tensor("ps_u", [P, 2, NB], F32))
        ps_t = ctx.enter_context(nc.psum_tensor("ps_t", [P, 2, NB], F32))
        ps_y = ctx.enter_context(nc.psum_tensor("ps_y", [P, 2, NB], F32))

        w_landed = [sem(f"w_landed{s}") for s in range(4)]
        ada_landed = [sem(f"ada_landed{s}") for s in range(2)]
        c_landed, x_landed, const_landed = sem("c_landed"), sem("x_landed"), sem("const_landed")
        gpost_landed, tab_landed, out_landed = sem("gpost_landed"), sem("tab_landed"), sem("out_landed")
        decay_landed, uv_done, ro_done_head = sem("decay_landed"), sem("uv_done"), sem("ro_done_head")
        bias_landed = sem("bias_landed")
        ident_landed, small_done = sem("ident_landed"), sem("small_done")
        cond_ready, acc_zero, consts_set = sem("cond_ready"), sem("acc_zero"), sem("consts_set")
        yacc_zero = sem("yacc_zero")
        hi_done, lo_done, pe_used = sem("hi_done"), sem("lo_done"), sem("pe_used")
        ada_done = sem("ada_done")
        gate_done, silu_done, up_done, h_done = sem("gate_done"), sem("silu_done"), sem("up_done"), sem("h_done")
        ht_done, ht_hi_done, ht_lo_done = sem("ht_done"), sem("ht_hi_done"), sem("ht_lo_done")
        y_done, y_added = sem("y_done"), sem("y_added")
        in_done, proj_done = sem("in_done"), sem("proj_done")
        cols_done, modcol_done = sem("cols_done"), sem("modcol_done")
        gbc_done, gates_ready = sem("gbc_done"), sem("gates_ready")
        ysq_done, xsq_done, var_ready, rstd_ready = sem("ysq_done"), sem("xsq_done"), sem("var_ready"), sem("rstd_ready")
        x_new, xn_ready = sem("x_new"), sem("xn_ready")
        xt_done, xt_hi_done, xt_lo_done = sem("xt_done"), sem("xt_hi_done"), sem("xt_lo_done")
        dve_chain, act_chain = sem("dve_chain"), sem("act_chain")
        kdup_done, ckvsq_done, tp_done, tp_copied = sem("kdup_done"), sem("ckvsq_done"), sem("tp_done"), sem("tp_copied")
        ukT_done, ukT_copied = sem("ukT_done"), sem("ukT_copied")
        ql_done, ql_copied = sem("ql_done"), sem("ql_copied")
        lg_done, lg_used = sem("lg_done"), sem("lg_used")
        s_done, s_biased, e_done, p_ready = sem("s_done"), sem("s_biased"), sem("e_done"), sem("p_ready")
        pt_done, pt_copied, pv_done = sem("pt_done"), sem("pt_copied"), sem("pv_done")
        ol_done, ol_copied = sem("ol_done"), sem("ol_copied")
        oh_done, o_hi_done, o_lo_done = sem("oh_done"), sem("o_hi_done"), sem("o_lo_done")
        r_done, r_decayed, ro_done, ro_copied = sem("r_done"), sem("r_decayed"), sem("ro_done"), sem("ro_copied")
        cent_ready, csq_done, rvar_ready, rrstd_ready = sem("cent_ready"), sem("csq_done"), sem("rvar_ready"), sem("rrstd_ready")
        cgate_done, oc_ready, oct_done = sem("cgate_done"), sem("oc_ready"), sem("oct_done")
        mix_ready = sem("mix_ready")

        win_v = [w[0].rearrange("(k p) n -> p k n", p=P) for w in (f1_in, f2_in)]
        wout_v = [w[0].rearrange("(k p) n -> p k n", p=P) for w in (f1_out, f2_out)]
        min_v = m_in[0].rearrange("(k p) n -> p k n", p=P)
        mout_v = m_out[0].rearrange("(k p) n -> p k n", p=P)
        ada_v = ada_w[0].rearrange("(k p) n -> k p n", p=P)

        def cols_of(a):
            return lambda t: proj[:, t, a:a + P]

        TP = [((cols_of(AQ + 2 * P * b), cols_of(AQ + 2 * P * b + P)), qT_a[:, 2 * b:2 * b + 2, :]) for b in range(4)]
        TP += [((lambda t: kdup[:, t, 0, :], lambda t: kdup[:, t, 1, :]), akT[:, 0:2, :])]
        TP += [((cols_of(BQ + 2 * P * b), cols_of(BQ + 2 * P * b + P)), qT_b[:, 2 * b:2 * b + 2, :]) for b in range(2)]
        TP += [((cols_of(BIQ + 2 * P * b), cols_of(BIQ + 2 * P * b + P)), iqT[:, 2 * b:2 * b + 2, :]) for b in range(2)]
        TP += [((lambda t: kdup[:, t, 2, :], lambda t: ckv[:, t, :]), t2[:, 2816:3328].rearrange("p (c n) -> p c n", n=SEQ))]
        TP_AB = len(TP)
        TP += [((cols_of(CQ + 2 * P * b), cols_of(CQ + 2 * P * b + P)), cqT[:, 2 * b:2 * b + 2, :]) for b in range(2)]
        TP += [((cols_of(CK + 2 * P * b), cols_of(CK + 2 * P * b + P)), ckT[:, 2 * b:2 * b + 2, :]) for b in range(2)]

        HEADS = A_HEADS + B_HEADS
        STEPS = HEADS + 7

        def pair_step(q):
            return 2 * q + (5 if q < A_HEADS // 2 else 7)

        slope = [2.0 ** (-8.0 * (i + 1) / A_HEADS) for i in range(A_HEADS)]
        slope += [2.0 ** (-8.0 * (i + 1) / B_HEADS) for i in range(B_HEADS)]

        def ada_after_lo(n, total, a):
            return (a + 1) * total // n - 1

        def ada_after_w(n, total, a):
            return min(a * total // n + 1, total - 1)

        block = ctx.enter_context(nc.Block())

        @block.sync
        def _(sp):
            def load_group(g, src_of, hooks=None, first=0):
                for s in range(4):
                    dst, src = src_of(s)
                    if isinstance(g, int) and g == 0:
                        sp.wait_ge(ada_done, ADA_PRE - 4 + s + 1)
                    else:
                        sp.wait_ge(lo_done, 8 * g - 8 + 2 * s + 2)
                    sp.dma_start(dst, src).then_inc(w_landed[s], 16)
                    if hooks:
                        hooks(first + s)

            def in_cols(view, col, width):
                return lambda s: (w_raw[:, s, :, 0:width], view[:, 4 * s:4 * s + 4, bass.ds(col, width)])

            def out_rows(view, chunk, chunks):
                return lambda s: (w_raw[:, s, 0:chunks, :], view[:, bass.ds(chunk, chunks), s * NB:(s + 1) * NB])

            def ada_hook(mods, base, i, weights):
                n = 2 * len(mods)

                def hook(at):
                    for a in range(n):
                        if ada_after_w(n, weights, a) != at:
                            continue
                        kk, m = divmod(a, len(mods))
                        count = base + n * i + a
                        sp.wait_ge(ada_done, count - 1)
                        sp.dma_start(ada_raw[:, a % 2, :],
                                     ada_v[bass.ds(2 * i + kk, 1), :, mods[m][0] * D:(mods[m][0] + 1) * D]
                                     .rearrange("k p n -> p (k n)")).then_inc(ada_landed[a % 2], 16)
                return hook

            def ffn_loads(f):
                g0, win, wout = G_FFN[f], win_v[f], wout_v[f]
                load_group(g0, in_cols(win, 0, NB))
                load_group(g0 + 1, in_cols(win, DFF, NB))

                def hidden(j, g, width, hooks):
                    load_group(g, in_cols(win, j * NB, width), hooks, 0)
                    load_group(g + 1, in_cols(win, j * NB + DFF, width), hooks, 4)
                    load_group(g + 2, out_rows(wout, (j - 1) * 4, 4), hooks, 8)

                hidden(1, g0 + 2, NB, None)
                with sp.Fori(0, LOOP) as i:
                    hidden(i + 2, g0 + 5 + 3 * i, NB, ada_hook(MODS_FFN[f], ADA_FFN[f], i, 12))
                hidden(FBLOCKS - 1, g0 + 5 + 3 * LOOP, TAIL, None)
                load_group(g0 + 8 + 3 * LOOP, out_rows(wout, (FBLOCKS - 1) * 4, TAIL // P))

            def load_gpost(n, ada_count):
                sp.wait_ge(ada_done, ada_count)
                sp.dma_start(ada_raw[:, 0, :], norm_g[0, 2 * n + 1:2 * n + 2, :].broadcast_to((P, D))).then_inc(gpost_landed, 16)

            sp.dma_start(rows64[3 * KD:4 * KD, :], c_in[0].rearrange("(k p) -> k p", p=P)).then_inc(c_landed, 16)
            for n in range(3):
                sp.dma_start(rows64[n * KD:(n + 1) * KD, :], norm_g[0, 2 * n].rearrange("(k p) -> k p", p=P)).then_inc(c_landed, 16)
            def first_ada(i, wait):
                for a in range(4):
                    kk, m = divmod(a, 2)
                    if wait:
                        sp.wait_ge(ada_done, 4 * i + a - 3)
                    sp.dma_start(w_raw[:, a].rearrange("p b n -> p (b n)"),
                                 ada_v[bass.ds(2 * i + kk, 1), :, m * D:(m + 1) * D].rearrange("k p n -> p (k n)")
                                 ).then_inc(w_landed[a], 16)

            first_ada(0, False)
            with sp.Fori(1, PRE_USES) as i:
                first_ada(i, True)
            ffn_loads(0)
            load_gpost(0, ADA_IN)
            def pair(i, g, hooks):
                load_group(g, in_cols(min_v, 2 * NB * i, NB), hooks, 0)
                load_group(g + 1, in_cols(min_v, 2 * NB * i + NB, NB), hooks, 4)

            def in_hook(i):
                def hook(at):
                    for a in range(8):
                        if ada_after_w(8, 8, a) != at:
                            continue
                        kk, m = divmod(a, 2)
                        sp.wait_ge(ada_done, ADA_IN + 8 * i + a - 1)
                        sp.dma_start(ada_raw[:, a % 2, :],
                                     ada_v[bass.ds(4 * i + kk, 1), :, MODS_IN[m][0] * D:(MODS_IN[m][0] + 1) * D]
                                     .rearrange("k p n -> p (k n)")).then_inc(ada_landed[a % 2], 16)
                return hook

            def first_hook(at):
                if at == 1:
                    sp.wait_ge(gates_ready, 1)
                in_hook(0)(at)

            pair(0, G_IN, first_hook)
            with sp.Fori(1, PBLOCKS // 2) as i:
                pair(i, G_IN + 2 * i, in_hook(i))
            load_group(G_IN + PBLOCKS - 1, in_cols(min_v, (PBLOCKS - 1) * NB, PTAIL))
            sp.wait_ge(lo_done, 8 * G_OUT)
            sp.dma_start(w_uk, uk_in[0].rearrange("r h d -> r (h d)")).then_inc(tab_landed, 16)
            sp.dma_start(w_uv, uv_in[0].rearrange("r h d -> r (h d)")).then_inc(tab_landed, 16)
            sp.dma_start(rnorm, rn_in[0:1, :].broadcast_to((P, NB))).then_inc(tab_landed, 16)
            sp.wait_ge(s_done, A_HEADS)
            sp.dma_start(decay.rearrange("p h n -> p (h n)"), consts[:, 896:896 + 2048]).then_inc(decay_landed, 16)
            sp.wait_ge(mix_ready, 1)
            for g in range(4):
                load_group(G_OUT + g, out_rows(mout_v, 4 * g, 4))
            load_gpost(1, ADA_FFN[1])
            sp.wait_ge(gates_ready, 2)
            ffn_loads(1)
            load_gpost(2, ADA_FFN[1] + 16)
            for t in range(TILES):
                sp.wait_ge(x_new, 2 * TILES + t + 1)
                sp.dma_start(out[0, t * P:(t + 1) * P, :], x_sb[:, t, :]).then_inc(out_landed, 16)
            sp.wait_ge(out_landed, 16 * TILES)

        @block.gpsimd
        def _(pool):
            nc.gpsimd.memset(ones[:, :], 1.0).then_inc(consts_set, 1)
            nc.gpsimd.memset(neghalf[:, :], -0.5).then_inc(consts_set, 1)
            pool.wait_ge(consts_set, 2)
            count = [0]

            def start_acc(mod, pos):
                nc.gpsimd.memset(acc[:, pos, :], 0.0).then_inc(acc_zero, 1)
                count[0] += 1
                pool.wait_ge(acc_zero, count[0])
                pool.dma_start(acc[0:1, pos, :], ada_b[0:1, mod * D:(mod + 1) * D]).then_inc(bias_landed, 16)
                pool.wait_ge(bias_landed, 16 * count[0])

            powers = [0]

            def power(lo, hi):
                powers[0] += 1
                pool.wait_ge(var_ready, powers[0])
                nc.gpsimd.tensor_tensor(rstd[:, lo:hi], ss[:, lo:hi], neghalf[:, 0:hi - lo], ALU.pow).then_inc(rstd_ready, 1)

            for mod, pos in MODS_PRE:
                start_acc(mod, pos)
            start_acc(4, 3)
            start_acc(5, 0)
            power(2, 4)
            pool.wait_ge(modcol_done, 1)
            start_acc(2, 1)
            start_acc(3, 2)
            pool.wait_ge(xt_done, 8)
            nc.gpsimd.memset(yacc, 0.0).then_inc(yacc_zero, 1)
            power(0, 2)
            power(2, 4)
            pool.wait_ge(x_new, TILES)
            start_acc(6, 1)
            start_acc(7, 2)
            power(4, 6)
            pool.wait_ge(rvar_ready, 1)
            nc.gpsimd.tensor_tensor(rstat[:, 2, :], rstat[:, 1, :], neghalf[:, 0:16], ALU.pow).then_inc(rrstd_ready, 1)
            pool.wait_ge(mix_ready, 1)
            nc.gpsimd.memset(yacc, 0.0).then_inc(yacc_zero, 1)
            start_acc(8, 3)
            power(0, 2)
            power(2, 4)
            pool.wait_ge(xt_done, 24)
            nc.gpsimd.memset(yacc, 0.0).then_inc(yacc_zero, 1)
            power(0, 2)

        @block.scalar
        def _(act):
            act.dma_start(ident[:, :], consts[:, 0:128]).then_inc(ident_landed, 16)
            act.dma_start(x_sb[:, :, :], x_in[0].rearrange("(t p) d -> p t d", p=P)).then_inc(x_landed, 16)
            act.dma_start(dist_a[:, :], consts[:, 128:512]).then_inc(const_landed, 16)
            act.dma_start(dist_b[:, :], consts[:, 512:896]).then_inc(const_landed, 16)
            act.dma_start(kvg[:, :], kvn_in[0:1, :].broadcast_to((P, KV_RANK))).then_inc(const_landed, 16)
            act.dma_start(sink[:, :], sinks_in[0:1, :].broadcast_to((P, A_HEADS))).then_inc(const_landed, 16)
            act.wait_ge(small_done, 1)
            nc.scalar.activation(gpre[:, :, :], ps_y[:, 0, 0:3 * KD].rearrange("p (n k) -> p n k", k=KD), ACT.Copy)
            nc.scalar.activation(cond[:, :], ps_y[:, 0, 3 * KD:4 * KD], ACT.Silu).then_inc(cond_ready, 1)

            chain = [0]

            def link(ins):
                chain[0] += 1
                ins.then_inc(act_chain, 1)
                act.wait_ge(act_chain, chain[0])

            def hi_group(g, chunks, width, hooks=None):
                for s in range(4):
                    act.wait_ge(w_landed[s], 16 * PRE_USES + 16 + 16 * g)
                    for hf in range(2):
                        v = 8 * g + 2 * s + hf
                        n = min(2, chunks - 2 * hf)
                        need(act, pe_used, v - 3)
                        nc.scalar.activation(w_hi[:, (2 * s + hf) % 4, 0:n, 0:width],
                                             w_raw[:, s, 2 * hf:2 * hf + n, 0:width], ACT.Copy).then_inc(hi_done, 1)
                        if hooks and (2 * s + hf) in hooks:
                            for h in hooks[2 * s + hf]:
                                h()

            def silu_of(j, width):
                def f():
                    act.wait_ge(gate_done, j + 1)
                    need(act, h_done, j)
                    nc.scalar.activation(silu[:, :, 0:width], ps_g[:, :, 0:width], ACT.Silu).then_inc(silu_done, 1)
                return f

            def ht_hi(j, ybase, chunks):
                def f():
                    act.wait_ge(ht_done, j + 1)
                    need(act, y_done, ybase)
                    nc.scalar.activation(hT_hi[:, 0:chunks, :],
                                         ps_t[:, :, :].rearrange("p b (c n) -> p (b c) n", n=SEQ)[:, 0:chunks, :],
                                         ACT.Copy).then_inc(ht_hi_done, 1)
                return f

            def ffn_act(f):
                g0, j0, y0 = G_FFN[f], f * FBLOCKS, Y_FFN[f]
                hi_group(g0, 4, NB)
                hi_group(g0 + 1, 4, NB, {2: [silu_of(j0, NB)]})

                def hidden(j, g, width):
                    hi_group(g, 4, width)
                    hi_group(g + 1, 4, width, {2: [silu_of(j0 + j, width)],
                                               3: [ht_hi(j0 + j - 1, y0 + 4 * (j - 1), 4)]})
                    hi_group(g + 2, 4, NB)

                hidden(1, g0 + 2, NB)
                with act.Fori(0, LOOP) as i:
                    hidden(i + 2, g0 + 5 + 3 * i, NB)
                hidden(FBLOCKS - 1, g0 + 5 + 3 * LOOP, TAIL)
                last = FBLOCKS - 1
                hi_group(g0 + 8 + 3 * LOOP, TAIL // P, NB, {3: [ht_hi(j0 + last, y0 + 4 * last, TAIL // P)]})

            def sum_squares(src, col, done, before, ready, ready0, per_tile=1):
                for t in range(TILES):
                    if ready is not None:
                        act.wait_ge(ready, ready0 + per_tile * t)
                    nc.scalar.activation(junk, src[:, t, :], ACT.Square, accum_out=ss[:, col + t:col + t + 1]).then_inc(done, 1)
                    act.wait_ge(done, before + t + 1)

            def xt_hi(n):
                act.wait_ge(modcol_done, n + 1)
                for b in range(8):
                    act.wait_ge(xt_done, 8 * n + b + 1)
                    for c in range(2):
                        k = 2 * b + c
                        nc.scalar.activation(xT_hi[:, k, :], banks[b][:, c * SEQ:(c + 1) * SEQ], ACT.Identity,
                                             bias=modcol[:, n, 1, k:k + 1], scale=modcol[:, n, 0, k:k + 1]).then_inc(xt_hi_done, 1)

            banks = [q[:, i, :] for q in (ps_g, ps_u, ps_t, ps_y) for i in range(2)]

            act.wait_ge(x_landed, 16)
            sum_squares(x_sb, 2, xsq_done, 0, None, 0)
            xt_hi(0)
            ffn_act(0)
            sum_squares(yacc, 0, ysq_done, 0, y_added, 4 * FBLOCKS, 0)
            sum_squares(x_sb, 2, xsq_done, 2, x_new, 1)
            xt_hi(1)

            def proj_out(b, pairs, width):
                def f():
                    act.wait_ge(in_done, b + 1)
                    nc.scalar.activation(proj[:, :, bass.ds(b * NB, width)], pairs[:, :, 0:width], ACT.Copy).then_inc(proj_done, 1)
                return f

            hi_group(G_IN, 4, NB)
            hi_group(G_IN + 1, 4, NB, {2: [proj_out(0, ps_g, NB)]})
            with act.Fori(1, PBLOCKS // 2) as i:
                hi_group(G_IN + 2 * i, 4, NB, {2: [proj_out(2 * i - 1, ps_u, NB)]})
                hi_group(G_IN + 2 * i + 1, 4, NB, {2: [proj_out(2 * i, ps_g, NB)]})
            hi_group(G_IN + PBLOCKS - 1, 4, PTAIL, {2: [proj_out(PBLOCKS - 2, ps_u, NB)]})
            proj_out(PBLOCKS - 1, ps_g, PTAIL)()

            act.wait_ge(proj_done, PBLOCKS)
            act.wait_ge(modcol_done, 3)
            for t in range(TILES):
                act.wait_ge(ada_done, ADA_FFN[1])
                nc.scalar.activation(sc[:, t, 0:KV_RANK], proj[:, t, BKV:BKV + KV_RANK], ACT.Square,
                                     accum_out=ss[:, 4 + t:5 + t]).then_inc(ckvsq_done, 1)

            def copy_transposes(b0, b1):
                for b in range(b0, b1):
                    act.wait_ge(tp_done, b + 1)
                    nc.scalar.activation(TP[b][1], ps_y[:, b % 2, :].rearrange("p (c n) -> p c n", n=SEQ), ACT.Copy).then_inc(tp_copied, 1)

            copy_transposes(0, TP_AB)
            act.wait_ge(ukT_done, 1)
            nc.scalar.activation(w_ukT, ps_y[:, 0, :].rearrange("p (c n) -> p c n", n=P), ACT.Copy).then_inc(ukT_copied, 1)
            for h in range(B_HEADS):
                act.wait_ge(ql_done, h + 1)
                nc.scalar.activation(qlatT[:, h, :], ps_y[:, h % 2, 0:SEQ], ACT.Copy).then_inc(ql_copied, 1)

            def pair_hi(q):
                act.wait_ge(oh_done, q + 1)
                nc.scalar.activation(xT_hi[:, q, :], ps_t[:, q % 2, 0:SEQ], ACT.Copy).then_inc(o_hi_done, 1)

            for step in range(STEPS):
                h = step
                if h < HEADS:
                    st = stat[:, h % 2, :]
                    act.wait_ge(s_biased, h + 1)
                    need(act, pt_done, h - 1)
                    nc.scalar.activation(pr[:, h % 2, 0:P], sc[:, h % 2, 0:P], ACT.Exp, bias=st[:, 2:3], scale=HD ** -0.5,
                                         accum_out=st[:, 4:5])
                    if h < A_HEADS:
                        nc.scalar.activation(st[:, 6:8], st[:, 2:4], ACT.Exp, bias=sink[:, h:h + 1])
                    nc.scalar.activation(pr[:, h % 2, P:], sc[:, h % 2, P:], ACT.Exp, bias=st[:, 3:4], scale=HD ** -0.5,
                                         accum_out=st[:, 5:6]).then_inc(e_done, 1)
                h = step - 2
                if 0 <= h < HEADS:
                    act.wait_ge(pt_done, h + 1)
                    need(act, pv_done, h - 1)
                    nc.scalar.activation(pT[:, h % 2, :], ps_u[:, h % 2, 0:3 * P], ACT.Copy).then_inc(pt_copied, 1)
                h = step - 4 - A_HEADS
                if 0 <= h < B_HEADS:
                    act.wait_ge(ol_done, h + 1)
                    need(act, uv_done, h - 1)
                    nc.scalar.activation(olatT[:, h % 2, :], ps_y[:, h % 2, 0:SEQ], ACT.Copy).then_inc(ol_copied, 1)
                for q in range(HEADS // 2):
                    if step == pair_step(q):
                        pair_hi(q)

            copy_transposes(TP_AB, len(TP))
            nc.scalar.activation(cgate, proj[:, :, CG:CG + NB], ACT.Silu).then_inc(cgate_done, 1)
            act.wait_ge(ro_done, 1)
            nc.scalar.activation(ro, ps_t[:, :, :], ACT.Copy).then_inc(ro_copied, 1)
            act.wait_ge(cent_ready, 1)
            nc.scalar.activation(csq, cent, ACT.Square).then_inc(csq_done, 1)
            for b in range(2):
                act.wait_ge(oct_done, b + 1)
                nc.scalar.activation(xT_hi[:, 12 + 2 * b:14 + 2 * b, :], ps_y[:, b, :].rearrange("p (c n) -> p c n", n=SEQ),
                                     ACT.Copy).then_inc(o_hi_done, 1)

            for g in range(4):
                hi_group(G_OUT + g, 4, NB)
            sum_squares(yacc, 0, ysq_done, 2, y_added, Y_OUT + 16, 0)
            sum_squares(x_sb, 2, xsq_done, 4, x_new, TILES + 1)
            xt_hi(2)
            ffn_act(1)
            sum_squares(yacc, 0, ysq_done, 4, y_added, Y_FFN[1] + 4 * FBLOCKS, 0)

        @block.vector
        def _(dve):
            chain = [0]

            def link(ins):
                chain[0] += 1
                ins.then_inc(dve_chain, 1)
                dve.wait_ge(dve_chain, chain[0])

            def lo_group(g, chunks, width, hooks=None):
                for s in range(4):
                    for hf in range(2):
                        v = 8 * g + 2 * s + hf
                        b = (2 * s + hf) % 4
                        n = min(2, chunks - 2 * hf)
                        dve.wait_ge(hi_done, v + 1)
                        nc.vector.tensor_tensor(w_lo[:, b, 0:n, 0:width], w_raw[:, s, 2 * hf:2 * hf + n, 0:width],
                                                w_hi[:, b, 0:n, 0:width].bitcast(F32), ALU.subtract).then_inc(lo_done, 1)
                        for h in (hooks or {}).get(2 * s + hf, ()):
                            h()

            def ada_unit(raw, landed, count, k, pos, done):
                def f():
                    dve.wait_ge(landed[0], landed[1])
                    dve.wait_ge(ada_done, done)
                    nc.vector.scalar_tensor_tensor(acc[:, pos, :], raw, cond[:, bass.ds(k, 1)], acc[:, pos, :],
                                                   ALU.mult, ALU.add).then_inc(ada_done, 1)
                return f

            def ada_hooks(mods, base, i, units, k0, hooks):
                n = 8 if units == 16 else 2 * len(mods)
                for a in range(n):
                    kk, m = divmod(a, len(mods))
                    count = base + n * i + a
                    use = (base - ADA_PRE) // 2 + (n // 2) * i + a // 2
                    unit = ada_unit(ada_raw[:, a % 2, :], (ada_landed[a % 2], 16 * use + 16), count, k0 + kk, mods[m][1], count)
                    hooks.setdefault(ada_after_lo(n, units, a), []).append(unit)
                return hooks

            def y_add(idx, n):
                ps = ps_t if n % 2 else ps_y

                def f():
                    dve.wait_ge(y_done, idx + 1)
                    need(dve, y_added, idx)
                    cols = yacc[:, :, n * NB:(n + 1) * NB]
                    nc.vector.tensor_tensor(cols, ps[:, :, :], cols, ALU.add).then_inc(y_added, 1)
                return f

            def h_mul(j, width):
                def f():
                    dve.wait_ge(silu_done, j + 1)
                    dve.wait_ge(up_done, j + 1)
                    need(dve, ht_done, j)
                    nc.vector.tensor_tensor(hbuf[:, :, 0:width], ps_u[:, :, 0:width], silu[:, :, 0:width],
                                            ALU.mult).then_inc(h_done, 1)
                return f

            def ht_lo(j, chunks):
                def f():
                    dve.wait_ge(ht_hi_done, j + 1)
                    nc.vector.tensor_tensor(hT_lo[:, 0:chunks, :],
                                            ps_t[:, :, :].rearrange("p b (c n) -> p (b c) n", n=SEQ)[:, 0:chunks, :],
                                            hT_hi[:, 0:chunks, :].bitcast(F32), ALU.subtract).then_inc(ht_lo_done, 1)
                return f

            def mod_cols(n, bank):
                def f():
                    dve.wait_ge(cols_done, n + 1)
                    nc.vector.scalar_tensor_tensor(modcol[:, n, 0, :], bank[:, KD:2 * KD], 1.0, gpre[:, n, :], ALU.add, ALU.mult)
                    nc.vector.tensor_copy(modcol[:, n, 1, :], bank[:, 0:KD]).then_inc(modcol_done, 1)
                return f

            def gates(n, pos, weight):
                def f():
                    dve.wait_ge(gpost_landed, 16 * n + 16)
                    dve.wait_ge(gbc_done, n + 1)
                    for b, ps in enumerate((ps_g, ps_u)):
                        part = slice(2 * b * NB, 2 * (b + 1) * NB)
                        last = nc.vector.scalar_tensor_tensor(
                            acc[:, pos, part], ps[:, :, :].rearrange("p b n -> p (b n)"), weight, ada_raw[:, 0, part],
                            ALU.mult, ALU.mult)
                    last.then_inc(gates_ready, 1)
                return f

            def ffn_dve(f):
                g0, j0, y0 = G_FFN[f], f * FBLOCKS, Y_FFN[f]
                dve.wait_ge(yacc_zero, 1 + 2 * f)
                lo_group(g0, 4, NB)
                lo_group(g0 + 1, 4, NB)

                def hidden(j, g, width, hooks):
                    parts = [{}, {}, {}]
                    for at, work_ in hooks.items():
                        parts[at // 8].setdefault(at % 8, []).extend(work_)
                    parts[0].setdefault(0, []).append(y_add(y0 + 4 * (j - 2) + 2, 2))
                    parts[0].setdefault(2, []).append(y_add(y0 + 4 * (j - 2) + 3, 3))
                    parts[1].setdefault(4, []).append(ht_lo(j0 + j - 1, 4))
                    parts[2].setdefault(2, []).append(h_mul(j0 + j, width))
                    parts[2].setdefault(4, []).append(y_add(y0 + 4 * (j - 1), 0))
                    parts[2].setdefault(6, []).append(y_add(y0 + 4 * (j - 1) + 1, 1))
                    lo_group(g, 4, width, parts[0])
                    lo_group(g + 1, 4, width, parts[1])
                    lo_group(g + 2, 4, NB, parts[2])

                lo_group(g0 + 2, 4, NB, {2: [h_mul(j0, NB)]})
                lo_group(g0 + 3, 4, NB, {4: [ht_lo(j0, 4)]})
                lo_group(g0 + 4, 4, NB, {2: [h_mul(j0 + 1, NB)], 4: [y_add(y0, 0)], 6: [y_add(y0 + 1, 1)]})
                dve.wait_ge(bias_landed, 16 * (6 if f == 0 else 9))
                with dve.Fori(0, LOOP) as i:
                    hidden(i + 2, g0 + 5 + 3 * i, NB, ada_hooks(MODS_FFN[f], ADA_FFN[f], i, 24, 2 * i, {}))
                last = FBLOCKS - 1
                hidden(last, g0 + 5 + 3 * LOOP, TAIL, {})
                yl = y0 + 4 * last
                tail = {0: [y_add(yl - 2, 2)], 2: [y_add(yl - 1, 3)], 3: [ht_lo(j0 + last, TAIL // P)],
                        5: [y_add(yl, 0), gates(0 if f == 0 else 2, 1 if f == 0 else 3, 0.5)], 7: [y_add(yl + 1, 1)]}
                if f == 0:
                    tail[2].append(mod_cols(1, ps_g[:, 0, :]))
                lo_group(g0 + 8 + 3 * LOOP, TAIL // P, NB, tail)
                y_add(yl + 2, 2)()
                y_add(yl + 3, 3)()

            norms = [0]

            def norm_scale(col, width):
                nc.vector.tensor_scalar(ss[:, col:col + 2], ss[:, col:col + 2], 1.0 / width, EPS, ALU.mult, ALU.add).then_inc(var_ready, 1)
                norms[0] += 1
                dve.wait_ge(rstd_ready, norms[0])

            def residual(n, pos):
                dve.wait_ge(ysq_done, 2 * n + 2)
                norm_scale(0, D)
                dve.wait_ge(y_added, (Y_OUT, Y_OUT + 16, Y_FFN[1] + 4 * FBLOCKS)[n])
                for t in range(TILES):
                    link(nc.vector.scalar_tensor_tensor(yacc[:, t, :], yacc[:, t, :], rstd[:, t:t + 1], acc[:, pos, :],
                                                        ALU.mult, ALU.mult))
                    nc.vector.tensor_tensor(x_sb[:, t, :], x_sb[:, t, :], yacc[:, t, :], ALU.add).then_inc(x_new, 1)

            def normed_input(n):
                dve.wait_ge(xsq_done, 2 * n + 2)
                norm_scale(2, D)
                need(dve, x_new, 2 * n)
                for t in range(TILES):
                    nc.vector.tensor_scalar(yacc[:, t, :], x_sb[:, t, :], rstd[:, 2 + t:3 + t], None, ALU.mult).then_inc(xn_ready, 1)

            def xt_lo(n):
                dve.wait_ge(modcol_done, n + 1)
                for b in range(8):
                    dve.wait_ge(xt_hi_done, 16 * n + 2 * b + 2)
                    for c in range(2):
                        k = 2 * b + c
                        full = junk[:, (k % 8) * SEQ:(k % 8 + 1) * SEQ]
                        last = nc.vector.tensor_scalar(full, banks[b][:, c * SEQ:(c + 1) * SEQ], modcol[:, n, 0, k:k + 1],
                                                       modcol[:, n, 1, k:k + 1], ALU.mult, ALU.add)
                    link(last)
                    for c in range(2):
                        k = 2 * b + c
                        full = junk[:, (k % 8) * SEQ:(k % 8 + 1) * SEQ]
                        nc.vector.tensor_tensor(xT_lo[:, k, :], full, xT_hi[:, k, :].bitcast(F32), ALU.subtract).then_inc(xt_lo_done, 1)
                    dve.wait_ge(xt_lo_done, 16 * n + 2 * b + 2)

            banks = [q[:, i, :] for q in (ps_g, ps_u, ps_t, ps_y) for i in range(2)]

            dve.wait_ge(x_landed, 16)
            dve.wait_ge(cond_ready, 1)
            dve.wait_ge(bias_landed, 32)
            dve.wait_ge(const_landed, 16 * 4)
            nc.vector.tensor_scalar(negsink[:, :], sink[:, :], -1.0, None, ALU.mult)
            with dve.Fori(0, PRE_USES) as i:
                for a in range(4):
                    kk, m = divmod(a, 2)
                    dve.wait_ge(w_landed[a], 16 * i + 16)
                    dve.wait_ge(ada_done, 4 * i + a)
                    raw = w_raw[:, a].rearrange("p b n -> p (b n)")
                    pos = MODS_PRE[m][1]
                    nc.vector.scalar_tensor_tensor(acc[:, pos, :], raw, cond[:, bass.ds(2 * i + kk, 1)], acc[:, pos, :],
                                                   ALU.mult, ALU.add).then_inc(ada_done, 1)
            normed_input(0)
            mod_cols(0, ps_g[:, 0, :])()
            xt_lo(0)
            ffn_dve(0)
            residual(0, 1)
            normed_input(1)
            xt_lo(1)

            dve.wait_ge(bias_landed, 16 * 8)

            def in_pair(i):
                hooks = ada_hooks(MODS_IN, ADA_IN, i, 16, 4 * i, {})
                lo_group(G_IN + 2 * i, 4, NB, {k: h for k, h in hooks.items() if k < 8})
                lo_group(G_IN + 2 * i + 1, 4, NB, {k - 8: h for k, h in hooks.items() if k >= 8})

            in_pair(0)
            with dve.Fori(1, PBLOCKS // 2) as i:
                in_pair(i)
            lo_group(G_IN + PBLOCKS - 1, 4, PTAIL)
            mod_cols(2, ps_t[:, 0, :])()

            dve.wait_ge(proj_done, PBLOCKS)
            for n_, a in enumerate((AK, AK + HD, BIK)):
                for dup in range(2):
                    last = nc.vector.tensor_copy(kdup[:, :, n_, dup * HD:(dup + 1) * HD], proj[:, :, a:a + HD])
            last.then_inc(kdup_done, 1)
            nc.vector.tensor_scalar(iws[:, :, :], proj[:, :, BIW:BIW + B_HEADS], B_HEADS ** -0.5, None, ALU.mult)
            dve.wait_ge(ckvsq_done, 2)
            norm_scale(4, KV_RANK)
            for t in range(TILES):
                last = nc.vector.scalar_tensor_tensor(ckv[:, t, :], proj[:, t, BKV:BKV + KV_RANK], rstd[:, 4 + t:5 + t],
                                                      kvg[:, :], ALU.mult, ALU.mult)
            last.then_inc(kdup_done, 1)

            link(nc.vector.tensor_scalar(score, dist_b[:, :], 0.1 * BIG, -1e37, ALU.is_ge, ALU.mult))
            for h in range(B_HEADS):
                dve.wait_ge(lg_done, h + 1)
                nc.vector.tensor_scalar(rw[:, 0:P], ps_g[:, h % 2, 0:P], 0.0, iws[:, 0, h:h + 1], ALU.max, ALU.mult)
                last = nc.vector.tensor_scalar(rw[:, P:3 * P], ps_g[:, h % 2, P:3 * P], 0.0, iws[:, 1, h:h + 1], ALU.max, ALU.mult)
                last.then_inc(lg_used, 1)
                dve.wait_ge(lg_used, h + 1)
                if h == 0:
                    link(nc.vector.tensor_copy(pick, rw))
                else:
                    link(nc.vector.tensor_tensor(pick, pick, rw, ALU.add))
            link(nc.vector.tensor_tensor(pick, pick, score, ALU.add))

            def top_round():
                for t in range(TILES):
                    keys = slice(0, P) if t == 0 else slice(P, 3 * P)
                    last = nc.vector.max(top8[:, t, :], pick[:, keys])
                link(last)
                for t in range(TILES):
                    keys = slice(0, P) if t == 0 else slice(P, 3 * P)
                    last = nc.vector.match_replace(pick[:, keys], top8[:, t, :], pick[:, keys], -3e38)
                link(last)

            def selected_distances():
                link(nc.vector.tensor_scalar(dist_sel, pick, -2e38, BIG, ALU.is_ge, ALU.mult))
                link(nc.vector.tensor_tensor(dist_sel, dist_sel, dist_b[:, :], ALU.max))

            side_work = {s: top_round for s in range(TOPK // 8)}
            side_work[TOPK // 8] = selected_distances

            def pair_lo(q):
                dve.wait_ge(o_hi_done, q + 1)
                nc.vector.tensor_tensor(xT_lo[:, q, :], ps_t[:, q % 2, 0:SEQ], xT_hi[:, q, :].bitcast(F32), ALU.subtract).then_inc(o_lo_done, 1)

            for step in range(STEPS):
                h = step
                if h < HEADS:
                    st = stat[:, h % 2, :]
                    dist = dist_a[:, :] if h < A_HEADS else dist_sel
                    dve.wait_ge(s_done, h + 1)
                    need(dve, e_done, h - 1)
                    link(nc.vector.scalar_tensor_tensor(sc[:, h % 2, :], dist, -slope[h] * HD ** 0.5, ps_g[:, h % 2, 0:3 * P],
                                                        ALU.mult, ALU.add))
                    nc.vector.reduce_max(st[:, 0:1], sc[:, h % 2, 0:P], AX_X)
                    link(nc.vector.reduce_max(st[:, 1:2], sc[:, h % 2, P:3 * P], AX_X))
                    if h < A_HEADS:
                        nc.vector.tensor_scalar(st[:, 2:4], st[:, 0:2], -HD ** -0.5, negsink[:, h:h + 1], ALU.mult, ALU.min).then_inc(s_biased, 1)
                    else:
                        nc.vector.tensor_scalar(st[:, 2:4], st[:, 0:2], -HD ** -0.5, None, ALU.mult).then_inc(s_biased, 1)
                h = step - 1
                if 0 <= h < HEADS:
                    st = stat[:, h % 2, :]
                    dve.wait_ge(e_done, h + 1)
                    if h < A_HEADS:
                        link(nc.vector.tensor_tensor(st[:, 4:6], st[:, 4:6], st[:, 6:8], ALU.add))
                    link(nc.vector.reciprocal(st[:, 8:10], st[:, 4:6]))
                    nc.vector.tensor_scalar(pr[:, h % 2, 0:P], pr[:, h % 2, 0:P], st[:, 8:9], None, ALU.mult)
                    nc.vector.tensor_scalar(pr[:, h % 2, P:], pr[:, h % 2, P:], st[:, 9:10], None, ALU.mult).then_inc(p_ready, 1)
                for q in range(HEADS // 2):
                    if step == pair_step(q):
                        pair_lo(q)
                if step in side_work:
                    side_work[step]()

            dve.wait_ge(decay_landed, 16)
            for h in range(C_HEADS):
                dve.wait_ge(r_done, h + 1)
                need(dve, ro_done_head, h - 1)
                nc.vector.tensor_tensor(sc[:, h % 2, 0:SEQ], ps_g[:, h % 2, 0:SEQ], decay[:, h, :], ALU.mult)
                nc.vector.tensor_tensor(sc[:, h % 2, SEQ:3 * P], ps_g[:, h % 2, SEQ:3 * P], decay[:, h, 0:P], ALU.mult).then_inc(r_decayed, 1)
            dve.wait_ge(r_decayed, C_HEADS)
            dve.wait_ge(ro_copied, 1)

            ro_h = ro.rearrange("p t (h d) -> p (t h) d", d=HD)
            cent_h = cent.rearrange("p t (h d) -> p (t h) d", d=HD)
            link(nc.vector.reduce_sum(rstat[:, 0, :], ro_h, AX_X))
            link(nc.vector.tensor_scalar(rstat[:, 0, :], rstat[:, 0, :], 1.0 / HD, None, ALU.mult))
            nc.vector.tensor_tensor(cent_h, ro_h, rstat[:, 0, :].unsqueeze(2).broadcast_to((P, 16, HD)), ALU.subtract).then_inc(cent_ready, 1)
            dve.wait_ge(csq_done, 1)
            link(nc.vector.reduce_sum(rstat[:, 1, :], csq.rearrange("p t (h d) -> p (t h) d", d=HD), AX_X))
            nc.vector.tensor_scalar(rstat[:, 1, :], rstat[:, 1, :], 1.0 / HD, EPS, ALU.mult, ALU.add).then_inc(rvar_ready, 1)
            dve.wait_ge(tab_landed, 16 * 3)
            dve.wait_ge(rrstd_ready, 1)
            link(nc.vector.tensor_tensor(cent_h, cent_h, rstat[:, 2, :].unsqueeze(2).broadcast_to((P, 16, HD)), ALU.mult))
            for t in range(TILES):
                last = nc.vector.tensor_tensor(cent[:, t, :], cent[:, t, :], rnorm, ALU.mult)
            link(last)
            dve.wait_ge(cgate_done, 1)
            nc.vector.tensor_tensor(cent, cent, cgate, ALU.mult).then_inc(oc_ready, 1)
            for b in range(2):
                dve.wait_ge(o_hi_done, HEADS // 2 + b + 1)
                last = nc.vector.tensor_tensor(xT_lo[:, 12 + 2 * b:14 + 2 * b, :], ps_y[:, b, :].rearrange("p (c n) -> p c n", n=SEQ),
                                               xT_hi[:, 12 + 2 * b:14 + 2 * b, :].bitcast(F32), ALU.subtract)
            last.then_inc(mix_ready, 1)

            dve.wait_ge(yacc_zero, 2)
            for g in range(4):
                y0 = Y_OUT + 4 * g
                hooks = {5: [y_add(y0, 0)], 7: [y_add(y0 + 1, 1)]}
                if g:
                    hooks[0] = [y_add(y0 - 2, 2)]
                    hooks[2] = [y_add(y0 - 1, 3)]
                if g == 3:
                    hooks[4] = [gates(1, 0, 1.0)]
                lo_group(G_OUT + g, 4, NB, hooks)
            y_add(Y_OUT + 14, 2)()
            y_add(Y_OUT + 15, 3)()
            residual(1, 0)
            normed_input(2)
            xt_lo(2)
            ffn_dve(1)
            residual(2, 3)

        @block.tensor
        def _(pe):
            def unit(a_hi, a_lo, chunk0, b, n, width, out_of, first, last_unit):
                for t in range(TILES):
                    rows = slice(t * P, (t + 1) * P)
                    for c in range(n):
                        k = chunk0 + c
                        start, stop = first and c == 0, last_unit and c == n - 1
                        o = out_of(t)
                        nc.tensor.matmul(o, a_hi[:, k, rows], w_hi[:, b, c, 0:width], start=start, stop=False)
                        nc.tensor.matmul(o, a_hi[:, k, rows], w_lo[:, b, c, 0:width], start=False, stop=False)
                        ins = nc.tensor.matmul(o, a_lo[:, k, rows], w_hi[:, b, c, 0:width], start=False, stop=stop)
                return ins

            def in_group(g, width, ps, done):
                for s in range(4):
                    for hf in range(2):
                        pe.wait_ge(lo_done, 8 * g + 2 * s + hf + 1)
                        ins = unit(xT_hi, xT_lo, 4 * s + 2 * hf, (2 * s + hf) % 4, 2, width, lambda t: ps[:, t, 0:width],
                                   s == 0 and hf == 0, s == 3 and hf == 1)
                        ins.then_inc(pe_used, 1)
                pe.wait_ge(pe_used, 8 * g + 8)
                pe.sem_inc(done, 1)

            def out_group(g, a_hi, a_lo, chunk0, chunks, y0):
                for n in range(4):
                    ps = ps_t if n % 2 else ps_y
                    need(pe, y_added, y0 + n - 1)
                    for hf in range(2):
                        m = min(2, chunks - 2 * hf)
                        pe.wait_ge(lo_done, 8 * g + 2 * n + hf + 1)
                        ins = unit(a_hi, a_lo, chunk0 + 2 * hf, (2 * n + hf) % 4, m, NB, lambda t: ps[:, t, :], hf == 0, hf == 1)
                        ins.then_inc(pe_used, 1)
                    pe.wait_ge(pe_used, 8 * g + 2 * n + 2)
                    pe.sem_inc(y_done, 1)

            def transpose_h(j, chunks, y_before):
                pe.wait_ge(h_done, j + 1)
                need(pe, y_added, y_before)
                for c in range(chunks):
                    for t in range(TILES):
                        col = (c % 2) * SEQ + t * P
                        ins = nc.tensor.transpose(ps_t[:, c // 2, col:col + P], hbuf[:, t, c * P:(c + 1) * P], ident[:, :])
                ins.then_inc(ht_done, 1)

            def mod_columns(shift, scale, bank, count):
                pe.wait_ge(ada_done, count)
                for m, pos in enumerate((shift, scale)):
                    for k in range(KD):
                        ins = nc.tensor.matmul(bank[:, m * KD + k:m * KD + k + 1], acc[:, pos, k * P:(k + 1) * P], ones[:, 0:1],
                                               start=True, stop=True)
                ins.then_inc(cols_done, 1)

            def gate_rows(pos, count):
                pe.wait_ge(ada_done, count)
                for n in range(4):
                    ps = (ps_g, ps_u)[n // 2]
                    ins = nc.tensor.matmul(ps[:, n % 2, :], ones[:, :], acc[:, pos, n * NB:(n + 1) * NB], start=True, stop=True)
                ins.then_inc(gbc_done, 1)

            banks = [q[:, i, :] for q in (ps_g, ps_u, ps_t, ps_y) for i in range(2)]

            def transpose_x(n):
                pe.wait_ge(xn_ready, 2 * n + 2)
                pe.wait_ge(modcol_done, n + 1)
                for b in range(8):
                    for c in range(2):
                        for t in range(TILES):
                            k = 2 * b + c
                            ins = nc.tensor.transpose(banks[b][:, c * SEQ + t * P:c * SEQ + (t + 1) * P],
                                                      yacc[:, t, k * P:(k + 1) * P], ident[:, :])
                    ins.then_inc(xt_done, 1)

            def ffn_pe(f):
                g0, j0, y0 = G_FFN[f], f * FBLOCKS, Y_FFN[f]
                pe.wait_ge(xt_lo_done, 16 + 32 * f)
                in_group(g0, NB, ps_g, gate_done)
                in_group(g0 + 1, NB, ps_u, up_done)

                def hidden(j, g, width):
                    need(pe, silu_done, j0 + j)
                    in_group(g, width, ps_g, gate_done)
                    transpose_h(j0 + j - 1, 4, y0 + 4 * (j - 1))
                    need(pe, h_done, j0 + j)
                    in_group(g + 1, width, ps_u, up_done)
                    pe.wait_ge(ht_lo_done, j0 + j)
                    out_group(g + 2, hT_hi, hT_lo, 0, 4, y0 + 4 * (j - 1))

                hidden(1, g0 + 2, NB)
                with pe.Fori(0, LOOP) as i:
                    hidden(i + 2, g0 + 5 + 3 * i, NB)
                last = FBLOCKS - 1
                hidden(last, g0 + 5 + 3 * LOOP, TAIL)
                pe.wait_ge(h_done, j0 + FBLOCKS)
                if f == 0:
                    mod_columns(2, 3, ps_g[:, 0, :], ADA_IN)
                    pe.wait_ge(modcol_done, 2)
                transpose_h(j0 + last, TAIL // P, y0 + 4 * last)
                pe.wait_ge(ht_lo_done, j0 + FBLOCKS)
                gate_rows(1 if f == 0 else 3, ADA_IN if f == 0 else ADA_FFN[1] + 16)
                out_group(g0 + 8 + 3 * LOOP, hT_hi, hT_lo, 0, TAIL // P, y0 + 4 * last)

            pe.wait_ge(ident_landed, 16)
            pe.wait_ge(c_landed, 16 * 4)
            nc.tensor.transpose(ps_y[:, 0, 0:4 * KD], rows64[:, :], ident[0:4 * KD, 0:4 * KD]).then_inc(small_done, 1)
            pe.wait_ge(consts_set, 1)
            mod_columns(1, 2, ps_g[:, 0, :], ADA_PRE)
            transpose_x(0)
            ffn_pe(0)
            transpose_x(1)

            pe.wait_ge(xt_lo_done, 32)
            in_group(G_IN, NB, ps_g, in_done)
            in_group(G_IN + 1, NB, ps_u, in_done)
            with pe.Fori(1, PBLOCKS // 2) as i:
                pe.wait_ge(proj_done, 2 * i - 1)
                in_group(G_IN + 2 * i, NB, ps_g, in_done)
                pe.wait_ge(proj_done, 2 * i)
                in_group(G_IN + 2 * i + 1, NB, ps_u, in_done)
            pe.wait_ge(proj_done, PBLOCKS - 2)
            in_group(G_IN + PBLOCKS - 1, PTAIL, ps_g, in_done)
            mod_columns(1, 2, ps_t[:, 0, :], ADA_FFN[1])

            def transposes(b0, b1):
                for b in range(b0, b1):
                    need(pe, tp_copied, b - 1)
                    if b == 4:
                        pe.wait_ge(kdup_done, 1)
                    if b == TP_AB - 1:
                        pe.wait_ge(kdup_done, 2)
                    for c in range(2):
                        for t in range(TILES):
                            col = c * SEQ + t * P
                            ins = nc.tensor.transpose(ps_y[:, b % 2, col:col + P], TP[b][0][c](t), ident[:, :])
                    ins.then_inc(tp_done, 1)

            pe.wait_ge(proj_done, PBLOCKS)
            transposes(0, TP_AB)
            pe.wait_ge(tab_landed, 16 * 3)
            pe.wait_ge(tp_copied, TP_AB)
            for c in range(4):
                ins = nc.tensor.transpose(ps_y[:, 0, c * P:(c + 1) * P], w_uk[:, c * P:(c + 1) * P], ident[:, :])
            ins.then_inc(ukT_done, 1)
            pe.wait_ge(ukT_copied, 1)
            for h in range(B_HEADS):
                need(pe, ql_copied, h - 1)
                rows = slice((h % 2) * HD, (h % 2 + 1) * HD)
                nc.tensor.matmul(ps_y[:, h % 2, 0:SEQ], w_ukT[rows, h // 2, :], qT_b[rows, h // 2, :],
                                 start=True, stop=True).then_inc(ql_done, 1)

            def two_tiles(bank, q_of, keys):
                nc.tensor.matmul(bank[:, 0:P], q_of(0), keys[:, 0:P], start=True, stop=True)
                return nc.tensor.matmul(bank[:, P:3 * P], q_of(1), keys, start=True, stop=True)

            for h in range(B_HEADS):
                rows = slice((h % 2) * HD, (h % 2 + 1) * HD)
                need(pe, lg_used, h - 1)
                two_tiles(ps_g[:, h % 2, :], lambda t: iqT[rows, h // 2, t * P:(t + 1) * P], ikT[rows, :]).then_inc(lg_done, 1)
            pe.wait_ge(lg_used, B_HEADS)
            pe.wait_ge(ql_copied, B_HEADS)
            pe.wait_ge(modcol_done, 3)

            for step in range(STEPS):
                h = step
                if h < HEADS:
                    need(pe, s_biased, h - 1)
                    if h < A_HEADS:
                        rows = slice((h % 2) * HD, (h % 2 + 1) * HD)
                        ins = two_tiles(ps_g[:, h % 2, :], lambda t: qT_a[rows, h // 2, t * P:(t + 1) * P],
                                        akT[rows, h // (A_HEADS // A_KV), :])
                    else:
                        ins = two_tiles(ps_g[:, h % 2, :], lambda t: qlatT[:, h - A_HEADS, t * P:(t + 1) * P], ckvT)
                    ins.then_inc(s_done, 1)
                h = step - 2
                if 0 <= h < HEADS:
                    pe.wait_ge(p_ready, h + 1)
                    need(pe, pt_copied, h - 1)
                    for c in range(2):
                        nc.tensor.transpose(ps_u[:, h % 2, c * P:(c + 1) * P], pr[:, h % 2, c * P:(c + 1) * P], ident[:, :])
                    nc.tensor.transpose(ps_u[:, h % 2, 2 * P:3 * P], pr[:, h % 2, 2 * P:3 * P], ident[:, :]).then_inc(pt_done, 1)
                h = step - 3
                if 0 <= h < HEADS:
                    pe.wait_ge(pt_copied, h + 1)
                    if h < A_HEADS:
                        q = h // 2
                        need(pe, o_lo_done, q - 1)
                        kv = AV + (h // (A_HEADS // A_KV)) * HD
                        o = ps_t[(h % 2) * HD:(h % 2 + 1) * HD, q % 2, 0:SEQ]
                        values = [proj[:, t, kv:kv + HD] for t in range(TILES)]
                    else:
                        need(pe, ol_copied, h - A_HEADS - 1)
                        o = ps_y[:, h % 2, 0:SEQ]
                        values = [ckv[:, t, :] for t in range(TILES)]
                    nc.tensor.matmul(o, values[0], pT[:, h % 2, 0:SEQ], start=True, stop=False)
                    ins = nc.tensor.matmul(o[:, P:SEQ], values[1], pT[:, h % 2, SEQ:3 * P], start=False, stop=True)
                    ins.then_inc(pv_done, 1)
                    if h < A_HEADS and h % 2:
                        pe.wait_ge(pv_done, h + 1)
                        pe.sem_inc(oh_done, 1)
                    if h >= A_HEADS:
                        pe.wait_ge(pv_done, h + 1)
                        pe.sem_inc(ol_done, 1)
                h = step - 5
                if A_HEADS <= h < HEADS:
                    q = h // 2
                    pe.wait_ge(ol_copied, h - A_HEADS + 1)
                    pe.wait_ge(o_lo_done, q - 1)
                    ins = nc.tensor.matmul(ps_t[(h % 2) * HD:(h % 2 + 1) * HD, q % 2, 0:SEQ],
                                           w_uv[:, (h - A_HEADS) * HD:(h - A_HEADS + 1) * HD], olatT[:, h % 2, :], start=True, stop=True)
                    ins.then_inc(uv_done, 1)
                    if h % 2:
                        pe.wait_ge(uv_done, h - A_HEADS + 1)
                        pe.sem_inc(oh_done, 1)

            pe.wait_ge(ol_copied, B_HEADS)
            transposes(TP_AB, len(TP))
            pe.wait_ge(tp_copied, len(TP))
            pe.wait_ge(o_lo_done, HEADS // 2)
            for step in range(C_HEADS + 1):
                h = step
                if h < C_HEADS:
                    rows = slice((h % 2) * HD, (h % 2 + 1) * HD)
                    need(pe, r_decayed, h - 1)
                    nc.tensor.matmul(ps_g[:, h % 2, 0:SEQ], ckT[rows, h // 2, 0:P], cqT[rows, h // 2, :], start=True, stop=True)
                    nc.tensor.matmul(ps_g[:, h % 2, SEQ:3 * P], ckT[rows, h // 2, P:SEQ], cqT[rows, h // 2, P:SEQ],
                                     start=True, stop=True).then_inc(r_done, 1)
                h = step - 1
                if h >= 0:
                    pe.wait_ge(r_decayed, h + 1)
                    v = [proj[:, t, CV + h * HD:CV + (h + 1) * HD] for t in range(TILES)]
                    cols = slice(h * HD, (h + 1) * HD)
                    nc.tensor.matmul(ps_t[:, 0, cols], sc[:, h % 2, 0:P], v[0], start=True, stop=True)
                    nc.tensor.matmul(ps_t[:, 1, cols], sc[:, h % 2, P:SEQ], v[0], start=True, stop=False)
                    nc.tensor.matmul(ps_t[:, 1, cols], sc[:, h % 2, SEQ:3 * P], v[1], start=False, stop=True).then_inc(ro_done_head, 1)
            pe.wait_ge(ro_done_head, C_HEADS)
            pe.sem_inc(ro_done, 1)
            pe.wait_ge(oc_ready, 1)
            for b in range(2):
                for c in range(2):
                    for t in range(TILES):
                        k = 2 * b + c
                        ins = nc.tensor.transpose(ps_y[:, b, c * SEQ + t * P:c * SEQ + (t + 1) * P], cent[:, t, k * P:(k + 1) * P], ident[:, :])
                ins.then_inc(oct_done, 1)

            pe.wait_ge(mix_ready, 1)
            for g in range(4):
                if g == 3:
                    gate_rows(0, ADA_IN)
                out_group(G_OUT + g, xT_hi, xT_lo, 4 * g, 4, Y_OUT + 4 * g)
            transpose_x(2)
            ffn_pe(1)


_INS = ["x", "c", "ada_w", "ada_b", "norm_g", "ffn1_w_in", "ffn1_w_out", "ffn2_w_in", "ffn2_w_out", "mix_w_in", "mix_w_out",
        "swa_sinks", "dsa_kv_norm", "dsa_w_uk", "dsa_w_uv", "ret_norm"]


def shape_constants():
    i = np.arange(P)[:, None].astype(np.float64)
    j = np.arange(P)[None, :].astype(np.float64)
    own = np.where(j <= i, i - j, BIG)
    window = np.where(j > i, i - j + P, BIG)
    gamma = 1.0 - 2.0 ** (-5.0 - np.arange(C_HEADS))
    q = np.arange(SEQ)[None, None, :]
    diff = q - np.arange(P)[:, None, None]
    decays = np.where(diff >= 0, gamma[None, :, None] ** np.maximum(diff, 0), 0.0) * HD ** -0.5
    parts = [np.eye(P), own, window, own, own, i - j + P, own, decays.reshape(P, -1)]
    return np.concatenate(parts, axis=1).astype(np.float32)


def kernel(**inputs):
    import concourse.bacc as _bacc
    from concourse.bass_utils import run_bass_kernel_spmd as _run

    nc = _bacc.Bacc("TRN2", target_bir_lowering=False, num_devices=1)
    arrays, args = {}, []
    given = {name: np.ascontiguousarray(inputs[name]) for name in _INS}
    given["consts"] = shape_constants()
    for name, a in given.items():
        arrays[f"in_{name}"] = a
        args.append(nc.dram_tensor(f"in_{name}", a.shape, mybir.dt.from_np(a.dtype), kind="ExternalInput").ap())
    args.append(nc.dram_tensor("out", (1, SEQ, D), F32, kind="ExternalOutput").ap())
    build(nc, *args)
    r = _run(nc, [arrays], core_ids=[0])
    return r.results[0]["out"]
```

```python
from contextlib import ExitStack

import numpy as np

import concourse.bass as bass
from concourse import mybir

ALU = mybir.AluOpType
ACT = mybir.ActivationFunctionType
F32 = mybir.dt.float32
F32R = mybir.dt.float32r
AX_X = mybir.AxisListType.X

P = 128
SEQ, D, DFF = 256, 2048, 5504
TILES = SEQ // P
KD = D // P
NB = 512
HD = 64
A_HEADS, A_KV, B_HEADS, C_HEADS = 16, 2, 8, 8
KV_RANK = 128
EPS = 1e-6
BIG = 1e30

COLS = (A_HEADS * HD, A_KV * HD, A_KV * HD, B_HEADS * HD, KV_RANK, B_HEADS * HD, HD, B_HEADS,
        C_HEADS * HD, C_HEADS * HD, C_HEADS * HD, C_HEADS * HD)
AQ, AK, AV, BQ, BKV, BIQ, BIK, BIW, CQ, CK, CV, CG = [sum(COLS[:i]) for i in range(len(COLS))]
MIX_IN = sum(COLS)
TOPK = min(256, SEQ // 4)

FBLOCKS = -(-DFF // NB)
TAIL = DFF - (FBLOCKS - 1) * NB
LOOP = 8
PBLOCKS = -(-MIX_IN // NB)
PTAIL = MIX_IN - (PBLOCKS - 1) * NB

FFN_GROUPS = 3 * FBLOCKS
G_FFN = (0, FFN_GROUPS + PBLOCKS + 4)
G_IN = FFN_GROUPS
G_OUT = G_IN + PBLOCKS
Y_FFN = (0, 4 * FBLOCKS + 16)
Y_OUT = 4 * FBLOCKS
PRE_USES = 8
ADA_PRE = 32
ADA_FFN = (ADA_PRE, ADA_PRE + 64 + 32)
ADA_IN = ADA_PRE + 64
MODS_PRE = ((0, 1), (1, 2))
MODS_FFN = (((2, 1), (3, 2), (4, 3), (5, 0)), ((8, 3),))
MODS_IN = ((6, 1), (7, 2))


def need(eng, sem, value):
    if isinstance(value, int) and value <= 0:
        return
    eng.wait_ge(sem, value)


def build(nc, x_in, c_in, ada_w, ada_b, norm_g, f1_in, f1_out, f2_in, f2_out, m_in, m_out, sinks_in,
          kvn_in, uk_in, uv_in, rn_in, consts, out):
    ctx = ExitStack()
    with ctx:
        def sb(name, shape, dt=F32):
            return ctx.enter_context(nc.sbuf_tensor(name, shape, dt))

        def sem(name):
            return ctx.enter_context(nc.semaphore(name))

        x_sb = sb("x_sb", [P, TILES, D])
        xT_hi = sb("xT_hi", [P, KD, SEQ], F32R)
        xT_lo = sb("xT_lo", [P, KD, SEQ], F32R)
        w_raw = sb("w_raw", [P, 4, 4, NB])
        w_hi = sb("w_hi", [P, 4, 2, NB], F32R)
        w_lo = sb("w_lo", [P, 4, 2, NB], F32R)
        hT_hi = sb("hT_hi", [P, 4, SEQ], F32R)
        hT_lo = sb("hT_lo", [P, 4, SEQ], F32R)
        ada_raw = sb("ada_raw", [P, 2, D])
        work_w = 7056
        arena = sb("arena", [P, 4 * D + work_w])
        acc = arena[:, 0:4 * D].rearrange("p (m d) -> p m d", m=4)
        work = arena[:, 4 * D:4 * D + work_w]
        yacc = work[:, 0:TILES * D].rearrange("p (t d) -> p t d", t=TILES)
        silu = work[:, 4096:5120].rearrange("p (t n) -> p t n", t=TILES)
        hbuf = work[:, 5120:6144].rearrange("p (t n) -> p t n", t=TILES)
        junk = work[:, 4096:6144]
        proj = arena[:, 3 * D:3 * D + TILES * MIX_IN].rearrange("p (t n) -> p t n", t=TILES)
        assert 3 * D + TILES * MIX_IN <= 4 * D + work_w
        ident = sb("ident", [P, P])
        ones = sb("ones", [P, P])
        dist_a = sb("dist_a", [P, 3 * P])
        dist_b = sb("dist_b", [P, 3 * P])
        kvg = sb("kvg", [P, KV_RANK])
        rows64 = sb("rows64", [4 * KD, P])
        cond = sb("cond", [P, KD])
        gpre = sb("gpre", [P, 3, KD])
        modcol = sb("modcol", [P, 3, 2, KD])
        sink = sb("sink", [P, A_HEADS])
        negsink = sb("negsink", [P, A_HEADS])
        iws = sb("iws", [P, TILES, B_HEADS])
        ss = sb("ss", [P, 8])
        ssy = sb("ssy", [P, TILES, 4])
        diag = sb("diag", [P, TILES, P])
        rbc = sb("rbc", [P, SEQ])
        rstd = sb("rstd", [P, 8])
        neghalf = sb("neghalf", [P, 16])
        stat = sb("stat", [P, 2, 12])
        rstat = sb("rstat", [P, 4, 16])
        top8 = sb("top8", [P, TILES, 8])
        t1 = arena[:, D:3 * D]
        t2 = ada_raw[:, :, :].rearrange("p a n -> p (a n)")
        t3 = w_raw[:, 2:4].rearrange("p a b n -> p (a b n)")
        qT_a = t1[:, 0:2048].rearrange("p (c n) -> p c n", n=SEQ)
        qlatT = w_raw[:, 1].rearrange("p b n -> p (b n)").rearrange("p (c n) -> p c n", n=SEQ)
        qT_b = t1[:, 2048:3072].rearrange("p (c n) -> p c n", n=SEQ)
        iqT = t1[:, 3072:4096].rearrange("p (c n) -> p c n", n=SEQ)
        cqT, ckT = qT_b, iqT
        sc = t2[:, 0:768].rearrange("p (b n) -> p b n", b=2)
        pr = t2[:, 768:1536].rearrange("p (b n) -> p b n", b=2)
        pT = t2[:, 1536:2304].rearrange("p (b n) -> p b n", b=2)
        akT = t2[:, 2304:2816].rearrange("p (c n) -> p c n", n=SEQ)
        ikT = t2[:, 2816:3072]
        ckvT = t2[:, 3072:3328]
        ckv = t2[:, 3328:3584].rearrange("p (t n) -> p t n", t=TILES)
        olatT = t2[:, 3584:4096].rearrange("p (b n) -> p b n", b=2)
        w_uk = t3[:, 0:512]
        w_uv = t3[:, 512:1024]
        w_ukT = t3[:, 1024:1536].rearrange("p (c n) -> p c n", n=P)
        score = t3[:, 1536:1920]
        pick = t3[:, 1920:2304]
        dist_sel = t3[:, 2304:2688]
        rw = t3[:, 2688:3072]
        kdup = t3[:, 3072:3840].rearrange("p (t s n) -> p t s n", t=TILES, s=3)
        decay = t1[:, 0:2048].rearrange("p (h n) -> p h n", n=SEQ)
        rnorm = w_raw[:, 0, 0, :]
        ro = w_raw[:, 0, 1:3, :]
        cent = t1[:, 0:1024].rearrange("p (t n) -> p t n", t=TILES)
        csq = t1[:, 1024:2048].rearrange("p (t n) -> p t n", t=TILES)
        cgate = t2[:, 3072:4096].rearrange("p (t n) -> p t n", t=TILES)

        ps_g = ctx.enter_context(nc.psum_tensor("ps_g", [P, 2, NB], F32))
        ps_u = ctx.enter_context(nc.psum_tensor("ps_u", [P, 2, NB], F32))
        ps_t = ctx.enter_context(nc.psum_tensor("ps_t", [P, 2, NB], F32))
        ps_y = ctx.enter_context(nc.psum_tensor("ps_y", [P, 2, NB], F32))

        w_landed = [sem(f"w_landed{s}") for s in range(4)]
        ada_landed = [sem(f"ada_landed{s}") for s in range(2)]
        c_landed, x_landed, const_landed = sem("c_landed"), sem("x_landed"), sem("const_landed")
        gpost_landed, tab_landed, out_landed = sem("gpost_landed"), sem("tab_landed"), sem("out_landed")
        decay_landed, uv_done, ro_done_head = sem("decay_landed"), sem("uv_done"), sem("ro_done_head")
        bias_landed = sem("bias_landed")
        ident_landed, small_done = sem("ident_landed"), sem("small_done")
        cond_ready, acc_zero, consts_set = sem("cond_ready"), sem("acc_zero"), sem("consts_set")
        yacc_zero = sem("yacc_zero")
        hi_done, lo_done, pe_used = sem("hi_done"), sem("lo_done"), sem("pe_used")
        ada_done = sem("ada_done")
        silu_done, h_done = sem("silu_done"), sem("h_done")
        ht_done, ht_hi_done, ht_lo_done = sem("ht_done"), sem("ht_hi_done"), sem("ht_lo_done")
        y_added, y_gated, proj_done = sem("y_added"), sem("y_gated"), sem("proj_done")
        cols_done, modcol_done = sem("cols_done"), sem("modcol_done")
        gbc_done, gates_ready = sem("gbc_done"), sem("gates_ready")
        ysq_done, xsq_done, var_ready, rstd_ready = sem("ysq_done"), sem("xsq_done"), sem("var_ready"), sem("rstd_ready")
        x_new, diag_ready, rb_done, rb_copied = sem("x_new"), sem("diag_ready"), sem("rb_done"), sem("rb_copied")
        xt_done, xt_scaled, xt_hi_done, xt_lo_done = sem("xt_done"), sem("xt_scaled"), sem("xt_hi_done"), sem("xt_lo_done")
        dve_chain, act_chain = sem("dve_chain"), sem("act_chain")
        kdup_done, ckvsq_done, tp_done, tp_copied = sem("kdup_done"), sem("ckvsq_done"), sem("tp_done"), sem("tp_copied")
        ukT_done, ukT_copied = sem("ukT_done"), sem("ukT_copied")
        ql_done, ql_copied = sem("ql_done"), sem("ql_copied")
        lg_done, lg_used = sem("lg_done"), sem("lg_used")
        s_done, s_biased, e_done, p_ready = sem("s_done"), sem("s_biased"), sem("e_done"), sem("p_ready")
        pt_done, pt_copied, pv_done = sem("pt_done"), sem("pt_copied"), sem("pv_done")
        ol_copied, o_hi_done, o_lo_done = sem("ol_copied"), sem("o_hi_done"), sem("o_lo_done")
        r_done, r_decayed, ro_copied = sem("r_done"), sem("r_decayed"), sem("ro_copied")
        cent_ready, csq_done, rvar_ready, rrstd_ready = sem("cent_ready"), sem("csq_done"), sem("rvar_ready"), sem("rrstd_ready")
        cgate_done, oc_ready, oct_done = sem("cgate_done"), sem("oc_ready"), sem("oct_done")
        mix_ready = sem("mix_ready")

        win_v = [w[0].rearrange("(k p) n -> p k n", p=P) for w in (f1_in, f2_in)]
        wout_v = [w[0].rearrange("(k p) n -> p k n", p=P) for w in (f1_out, f2_out)]
        min_v = m_in[0].rearrange("(k p) n -> p k n", p=P)
        mout_v = m_out[0].rearrange("(k p) n -> p k n", p=P)
        ada_v = ada_w[0].rearrange("(k p) n -> k p n", p=P)

        def cols_of(a):
            return lambda t: proj[:, t, a:a + P]

        TP = [((cols_of(AQ + 2 * P * b), cols_of(AQ + 2 * P * b + P)), qT_a[:, 2 * b:2 * b + 2, :]) for b in range(4)]
        TP += [((lambda t: kdup[:, t, 0, :], lambda t: kdup[:, t, 1, :]), akT[:, 0:2, :])]
        TP += [((cols_of(BQ + 2 * P * b), cols_of(BQ + 2 * P * b + P)), qT_b[:, 2 * b:2 * b + 2, :]) for b in range(2)]
        TP += [((cols_of(BIQ + 2 * P * b), cols_of(BIQ + 2 * P * b + P)), iqT[:, 2 * b:2 * b + 2, :]) for b in range(2)]
        TP += [((lambda t: kdup[:, t, 2, :], lambda t: ckv[:, t, :]), t2[:, 2816:3328].rearrange("p (c n) -> p c n", n=SEQ))]
        TP_AB = len(TP)
        TP += [((cols_of(CQ + 2 * P * b), cols_of(CQ + 2 * P * b + P)), cqT[:, 2 * b:2 * b + 2, :]) for b in range(2)]
        TP += [((cols_of(CK + 2 * P * b), cols_of(CK + 2 * P * b + P)), ckT[:, 2 * b:2 * b + 2, :]) for b in range(2)]

        HEADS = A_HEADS + B_HEADS
        STEPS = HEADS + 7

        def pair_step(q):
            return 2 * q + (5 if q < A_HEADS // 2 else 7)

        slope = [2.0 ** (-8.0 * (i + 1) / A_HEADS) for i in range(A_HEADS)]
        slope += [2.0 ** (-8.0 * (i + 1) / B_HEADS) for i in range(B_HEADS)]

        def ada_after_lo(n, total, a):
            return (a + 1) * total // n - 1

        def ada_after_w(n, total, a):
            return min(a * total // n + 1, total - 1)

        block = ctx.enter_context(nc.Block())

        @block.sync
        def _(sp):
            def load_group(g, src_of, hooks=None, first=0):
                for s in range(4):
                    dst, src = src_of(s)
                    if isinstance(g, int) and g == 0:
                        sp.wait_ge(ada_done, ADA_PRE - 4 + s + 1)
                    else:
                        sp.wait_ge(lo_done, 8 * g - 8 + 2 * s + 2)
                    sp.dma_start(dst, src).then_inc(w_landed[s], 16)
                    if hooks:
                        hooks(first + s)

            def in_cols(view, col, width):
                return lambda s: (w_raw[:, s, :, 0:width], view[:, 4 * s:4 * s + 4, bass.ds(col, width)])

            def out_rows(view, chunk, chunks):
                return lambda s: (w_raw[:, s, 0:chunks, :], view[:, bass.ds(chunk, chunks), s * NB:(s + 1) * NB])

            def ada_hook(mods, base, i, weights):
                n = 2 * len(mods)

                def hook(at):
                    for a in range(n):
                        if ada_after_w(n, weights, a) != at:
                            continue
                        kk, m = divmod(a, len(mods))
                        count = base + n * i + a
                        sp.wait_ge(ada_done, count - 1)
                        sp.dma_start(ada_raw[:, a % 2, :],
                                     ada_v[bass.ds(2 * i + kk, 1), :, mods[m][0] * D:(mods[m][0] + 1) * D]
                                     .rearrange("k p n -> p (k n)")).then_inc(ada_landed[a % 2], 16)
                return hook

            def ffn_loads(f):
                g0, win, wout = G_FFN[f], win_v[f], wout_v[f]
                load_group(g0, in_cols(win, 0, NB))
                load_group(g0 + 1, in_cols(win, DFF, NB))

                def hidden(j, g, width, hooks):
                    load_group(g, in_cols(win, j * NB, width), hooks, 0)
                    load_group(g + 1, in_cols(win, j * NB + DFF, width), hooks, 4)
                    load_group(g + 2, out_rows(wout, (j - 1) * 4, 4), hooks, 8)

                hidden(1, g0 + 2, NB, None)
                if f == 1:
                    sp.wait_ge(gates_ready, 2)
                with sp.Fori(0, LOOP) as i:
                    hidden(i + 2, g0 + 5 + 3 * i, NB, ada_hook(MODS_FFN[f], ADA_FFN[f], i, 12))
                hidden(FBLOCKS - 1, g0 + 5 + 3 * LOOP, TAIL, None)
                load_group(g0 + 8 + 3 * LOOP, out_rows(wout, (FBLOCKS - 1) * 4, TAIL // P))

            def load_gpost(n, ada_count):
                sp.wait_ge(ada_done, ada_count)
                sp.dma_start(ada_raw[:, 0, :], norm_g[0, 2 * n + 1:2 * n + 2, :].broadcast_to((P, D))).then_inc(gpost_landed, 16)

            sp.dma_start(rows64[3 * KD:4 * KD, :], c_in[0].rearrange("(k p) -> k p", p=P)).then_inc(c_landed, 16)
            for n in range(3):
                sp.dma_start(rows64[n * KD:(n + 1) * KD, :], norm_g[0, 2 * n].rearrange("(k p) -> k p", p=P)).then_inc(c_landed, 16)
            def first_ada(m, i, wait):
                for a in range(4):
                    if wait:
                        sp.wait_ge(ada_done, 16 * m + 4 * i + a - 3)
                    sp.dma_start(w_raw[:, a].rearrange("p b n -> p (b n)"),
                                 ada_v[bass.ds(4 * i + a, 1), :, m * D:(m + 1) * D].rearrange("k p n -> p (k n)")
                                 ).then_inc(w_landed[a], 16)

            first_ada(0, 0, False)
            with sp.Fori(1, 4) as i:
                first_ada(0, i, True)
            with sp.Fori(0, 4) as i:
                first_ada(1, i, True)
            ffn_loads(0)
            load_gpost(0, ADA_IN)
            def pair(i, g, hooks):
                load_group(g, in_cols(min_v, 2 * NB * i, NB), hooks, 0)
                load_group(g + 1, in_cols(min_v, 2 * NB * i + NB, NB), hooks, 4)

            def in_hook(i):
                def hook(at):
                    for a in range(8):
                        if ada_after_w(8, 8, a) != at:
                            continue
                        kk, m = divmod(a, 2)
                        sp.wait_ge(ada_done, ADA_IN + 8 * i + a - 1)
                        sp.dma_start(ada_raw[:, a % 2, :],
                                     ada_v[bass.ds(4 * i + kk, 1), :, MODS_IN[m][0] * D:(MODS_IN[m][0] + 1) * D]
                                     .rearrange("k p n -> p (k n)")).then_inc(ada_landed[a % 2], 16)
                return hook

            def first_hook(at):
                if at == 1:
                    sp.wait_ge(gates_ready, 1)
                    sp.wait_ge(modcol_done, 4)
                in_hook(0)(at)

            pair(0, G_IN, first_hook)
            with sp.Fori(1, PBLOCKS // 2) as i:
                pair(i, G_IN + 2 * i, in_hook(i))
            load_group(G_IN + PBLOCKS - 1, in_cols(min_v, (PBLOCKS - 1) * NB, PTAIL))
            sp.wait_ge(lo_done, 8 * G_OUT)
            sp.dma_start(w_uk, uk_in[0].rearrange("r h d -> r (h d)")).then_inc(tab_landed, 16)
            sp.dma_start(w_uv, uv_in[0].rearrange("r h d -> r (h d)")).then_inc(tab_landed, 16)
            sp.dma_start(rnorm, rn_in[0:1, :].broadcast_to((P, NB))).then_inc(tab_landed, 16)
            sp.wait_ge(s_done, A_HEADS)
            sp.dma_start(decay.rearrange("p h n -> p (h n)"), consts[:, 896:896 + 2048]).then_inc(decay_landed, 16)
            sp.wait_ge(mix_ready, 1)
            for g in range(4):
                load_group(G_OUT + g, out_rows(mout_v, 4 * g, 4))
            load_gpost(1, ADA_FFN[1])
            ffn_loads(1)
            load_gpost(2, ADA_FFN[1] + 16)
            for t in range(TILES):
                sp.wait_ge(x_new, 2 * TILES + t + 1)
                sp.dma_start(out[0, t * P:(t + 1) * P, :], x_sb[:, t, :]).then_inc(out_landed, 16)
            sp.wait_ge(out_landed, 16 * TILES)

        @block.gpsimd
        def _(pool):
            nc.gpsimd.memset(ones[:, :], 1.0).then_inc(consts_set, 1)
            nc.gpsimd.memset(neghalf[:, :], -0.5).then_inc(consts_set, 1)
            pool.wait_ge(consts_set, 2)
            count = [0]

            def start_acc(mod, pos):
                nc.gpsimd.memset(acc[:, pos, :], 0.0).then_inc(acc_zero, 1)
                count[0] += 1
                pool.wait_ge(acc_zero, count[0])
                pool.dma_start(acc[0:1, pos, :], ada_b[0:1, mod * D:(mod + 1) * D]).then_inc(bias_landed, 16)
                pool.wait_ge(bias_landed, 16 * count[0])

            powers = [0]

            def power(lo, hi):
                powers[0] += 1
                pool.wait_ge(var_ready, powers[0])
                nc.gpsimd.tensor_tensor(rstd[:, lo:hi], ss[:, lo:hi], neghalf[:, 0:hi - lo], ALU.pow).then_inc(rstd_ready, 1)

            for mod, pos in MODS_PRE:
                start_acc(mod, pos)
            nc.gpsimd.memset(yacc, 0.0).then_inc(yacc_zero, 1)
            start_acc(4, 3)
            start_acc(5, 0)
            power(2, 4)
            pool.wait_ge(modcol_done, 2)
            start_acc(2, 1)
            start_acc(3, 2)
            power(0, 2)
            power(2, 4)
            pool.wait_ge(x_new, TILES)
            start_acc(6, 1)
            start_acc(7, 2)
            power(4, 6)
            pool.wait_ge(rvar_ready, 1)
            nc.gpsimd.tensor_tensor(rstat[:, 2, :], rstat[:, 1, :], neghalf[:, 0:16], ALU.pow).then_inc(rrstd_ready, 1)
            pool.wait_ge(mix_ready, 1)
            nc.gpsimd.memset(yacc, 0.0).then_inc(yacc_zero, 1)
            start_acc(8, 3)
            power(0, 2)
            power(2, 4)
            pool.wait_ge(x_new, 2 * TILES)
            nc.gpsimd.memset(yacc, 0.0).then_inc(yacc_zero, 1)
            power(0, 2)

        @block.scalar
        def _(act):
            act.dma_start(ident[:, :], consts[:, 0:128]).then_inc(ident_landed, 16)
            act.dma_start(x_sb[:, :, :], x_in[0].rearrange("(t p) d -> p t d", p=P)).then_inc(x_landed, 16)
            act.dma_start(dist_a[:, :], consts[:, 128:512]).then_inc(const_landed, 16)
            act.dma_start(dist_b[:, :], consts[:, 512:896]).then_inc(const_landed, 16)
            act.dma_start(kvg[:, :], kvn_in[0:1, :].broadcast_to((P, KV_RANK))).then_inc(const_landed, 16)
            act.dma_start(sink[:, :], sinks_in[0:1, :].broadcast_to((P, A_HEADS))).then_inc(const_landed, 16)
            act.wait_ge(small_done, 1)
            nc.scalar.activation(gpre[:, :, :], ps_y[:, 0, 0:3 * KD].rearrange("p (n k) -> p n k", k=KD), ACT.Copy)
            nc.scalar.activation(cond[:, :], ps_y[:, 0, 3 * KD:4 * KD], ACT.Silu).then_inc(cond_ready, 1)

            chain = [0]

            def link(ins):
                chain[0] += 1
                ins.then_inc(act_chain, 1)
                act.wait_ge(act_chain, chain[0])

            def hi_group(g, chunks, width, hooks=None, units=range(8)):
                for u in units:
                    s, hf = divmod(u, 2)
                    if hf == 0:
                        act.wait_ge(w_landed[s], 16 * PRE_USES + 16 + 16 * g)
                    n = min(2, chunks - 2 * hf)
                    need(act, pe_used, 8 * g + u - 3)
                    nc.scalar.activation(w_hi[:, u % 4, 0:n, 0:width],
                                         w_raw[:, s, 2 * hf:2 * hf + n, 0:width], ACT.Copy).then_inc(hi_done, 1)
                    for h in (hooks or {}).get(u, ()):
                        h()

            def silu_of(j, g, width):
                def f():
                    act.wait_ge(pe_used, 8 * g + 8)
                    need(act, h_done, j)
                    nc.scalar.activation(silu[:, :, 0:width], ps_g[:, :, 0:width], ACT.Silu).then_inc(silu_done, 1)
                return f

            def ht_hi(j, chunks):
                def f():
                    act.wait_ge(ht_done, j + 1)
                    nc.scalar.activation(hT_hi[:, 0:chunks, :],
                                         ps_t[:, :, :].rearrange("p b (c n) -> p (b c) n", n=SEQ)[:, 0:chunks, :],
                                         ACT.Copy).then_inc(ht_hi_done, 1)
                return f

            def ffn_act(f):
                g0, j0 = G_FFN[f], f * FBLOCKS
                hi_group(g0, 4, NB, xt_hooks(2 * f), range(4, 8))
                hi_group(g0 + 1, 4, NB, {2: [silu_of(j0, g0, NB)]})

                def hidden(j, g, width):
                    hi_group(g, 4, width)
                    hi_group(g + 1, 4, width, {2: [silu_of(j0 + j, g, width)], 3: [ht_hi(j0 + j - 1, 4)]})
                    hi_group(g + 2, 4, NB)

                hidden(1, g0 + 2, NB)
                with act.Fori(0, LOOP) as i:
                    hidden(i + 2, g0 + 5 + 3 * i, NB)
                hidden(FBLOCKS - 1, g0 + 5 + 3 * LOOP, TAIL)
                hi_group(g0 + 8 + 3 * LOOP, TAIL // P, NB, {3: [ht_hi(j0 + FBLOCKS - 1, TAIL // P)]})

            def y_squares(n, y0):
                for b in range(4):
                    act.wait_ge(y_added, y0 + b + 1)
                    if b >= 2:
                        act.wait_ge(ysq_done, 4 * n + b - 1)
                    for t in range(TILES):
                        ins = nc.scalar.activation(junk[:, (2 * b + t) % 4 * NB:((2 * b + t) % 4 + 1) * NB],
                                                   yacc[:, t, b * NB:(b + 1) * NB], ACT.Square, accum_out=ssy[:, t, b:b + 1])
                    ins.then_inc(ysq_done, 1)

            def x_squares(n):
                for t in range(TILES):
                    if n == 0:
                        act.wait_ge(x_landed, 16)
                    else:
                        act.wait_ge(x_new, TILES * (n - 1) + t + 1)
                        act.wait_ge(ysq_done, 4 * n)
                    nc.scalar.activation(junk, x_sb[:, t, :], ACT.Square, accum_out=ss[:, 2 + t:3 + t]).then_inc(xsq_done, 1)
                    act.wait_ge(xsq_done, 2 * n + t + 1)

            def row_scale(n):
                act.wait_ge(rb_done, n + 1)
                nc.scalar.activation(rbc[:, :], ps_y[:, 1, 0:SEQ], ACT.Copy).then_inc(rb_copied, 1)

            def xt_hi(n, b):
                def f():
                    act.wait_ge(xt_scaled, 8 * n + b + 1)
                    for c in range(2):
                        k = 2 * b + c
                        ins = nc.scalar.activation(xT_hi[:, k, :], junk[:, (k % 8) * SEQ:(k % 8 + 1) * SEQ], ACT.Identity,
                                                   bias=modcol[:, n, 1, k:k + 1])
                    ins.then_inc(xt_hi_done, 1)
                return f

            def xt_hooks(n):
                return {4: [xt_hi(n, 3)], 5: [xt_hi(n, 4)], 6: [xt_hi(n, 5)], 7: [xt_hi(n, 6), xt_hi(n, 7)]}

            def into_part(n, g):
                hi_group(g, 4, NB, None, range(4))
                x_squares(n)
                row_scale(n)
                for b in range(3):
                    xt_hi(n, b)()

            x_squares(0)
            row_scale(0)
            hi_group(0, 4, NB, None, range(4))
            for b in range(3):
                xt_hi(0, b)()
            ffn_act(0)
            y_squares(0, Y_FFN[0] + 4 * FBLOCKS - 4)
            into_part(1, G_IN)

            def proj_out(b, pairs, width):
                def f():
                    act.wait_ge(pe_used, 8 * (G_IN + b) + 8)
                    nc.scalar.activation(proj[:, :, bass.ds(b * NB, width)], pairs[:, :, 0:width], ACT.Copy).then_inc(proj_done, 1)
                return f

            hi_group(G_IN, 4, NB, xt_hooks(1), range(4, 8))
            hi_group(G_IN + 1, 4, NB, {2: [proj_out(0, ps_g, NB)]})
            with act.Fori(1, PBLOCKS // 2) as i:
                hi_group(G_IN + 2 * i, 4, NB, {2: [proj_out(2 * i - 1, ps_u, NB)]})
                hi_group(G_IN + 2 * i + 1, 4, NB, {2: [proj_out(2 * i, ps_g, NB)]})
            hi_group(G_IN + PBLOCKS - 1, 4, PTAIL, {2: [proj_out(PBLOCKS - 2, ps_u, NB)]})
            proj_out(PBLOCKS - 1, ps_g, PTAIL)()

            act.wait_ge(proj_done, PBLOCKS)
            act.wait_ge(modcol_done, 6)
            for t in range(TILES):
                act.wait_ge(ada_done, ADA_FFN[1])
                nc.scalar.activation(sc[:, t, 0:KV_RANK], proj[:, t, BKV:BKV + KV_RANK], ACT.Square,
                                     accum_out=ss[:, 4 + t:5 + t]).then_inc(ckvsq_done, 1)

            def copy_transposes(b0, b1):
                for b in range(b0, b1):
                    act.wait_ge(tp_done, b + 1)
                    nc.scalar.activation(TP[b][1], ps_y[:, b % 2, :].rearrange("p (c n) -> p c n", n=SEQ), ACT.Copy).then_inc(tp_copied, 1)

            copy_transposes(0, TP_AB)
            act.wait_ge(ukT_done, 1)
            nc.scalar.activation(w_ukT, ps_y[:, 0, :].rearrange("p (c n) -> p c n", n=P), ACT.Copy).then_inc(ukT_copied, 1)
            for h in range(B_HEADS):
                act.wait_ge(ql_done, h + 1)
                nc.scalar.activation(qlatT[:, h, :], ps_y[:, h % 2, 0:SEQ], ACT.Copy).then_inc(ql_copied, 1)

            def pair_hi(q):
                if q < A_HEADS // 2:
                    act.wait_ge(pv_done, 2 * q + 2)
                else:
                    act.wait_ge(uv_done, 2 * q + 2 - A_HEADS)
                nc.scalar.activation(xT_hi[:, q, :], ps_t[:, q % 2, 0:SEQ], ACT.Copy).then_inc(o_hi_done, 1)

            for step in range(STEPS):
                h = step
                if h < HEADS:
                    st = stat[:, h % 2, :]
                    act.wait_ge(s_biased, h + 1)
                    need(act, pt_done, h - 1)
                    nc.scalar.activation(pr[:, h % 2, 0:P], sc[:, h % 2, 0:P], ACT.Exp, bias=st[:, 2:3], scale=HD ** -0.5,
                                         accum_out=st[:, 4:5])
                    if h < A_HEADS:
                        nc.scalar.activation(st[:, 6:8], st[:, 2:4], ACT.Exp, bias=sink[:, h:h + 1])
                    nc.scalar.activation(pr[:, h % 2, P:], sc[:, h % 2, P:], ACT.Exp, bias=st[:, 3:4], scale=HD ** -0.5,
                                         accum_out=st[:, 5:6]).then_inc(e_done, 1)
                h = step - 2
                if 0 <= h < HEADS:
                    act.wait_ge(pt_done, h + 1)
                    need(act, pv_done, h - 1)
                    nc.scalar.activation(pT[:, h % 2, :], ps_u[:, h % 2, 0:3 * P], ACT.Copy).then_inc(pt_copied, 1)
                h = step - 4 - A_HEADS
                if 0 <= h < B_HEADS:
                    act.wait_ge(pv_done, A_HEADS + h + 1)
                    need(act, uv_done, h - 1)
                    nc.scalar.activation(olatT[:, h % 2, :], ps_y[:, h % 2, 0:SEQ], ACT.Copy).then_inc(ol_copied, 1)
                for q in range(HEADS // 2):
                    if step == pair_step(q):
                        pair_hi(q)

            copy_transposes(TP_AB, len(TP))
            nc.scalar.activation(cgate, proj[:, :, CG:CG + NB], ACT.Silu).then_inc(cgate_done, 1)
            act.wait_ge(ro_done_head, C_HEADS)
            nc.scalar.activation(ro, ps_t[:, :, :], ACT.Copy).then_inc(ro_copied, 1)
            act.wait_ge(cent_ready, 1)
            nc.scalar.activation(csq, cent, ACT.Square).then_inc(csq_done, 1)
            for b in range(2):
                act.wait_ge(oct_done, b + 1)
                nc.scalar.activation(xT_hi[:, 12 + 2 * b:14 + 2 * b, :], ps_y[:, b, :].rearrange("p (c n) -> p c n", n=SEQ),
                                     ACT.Copy).then_inc(o_hi_done, 1)

            for g in range(4):
                hi_group(G_OUT + g, 4, NB)
            y_squares(1, Y_OUT + 12)
            into_part(2, G_FFN[1])
            ffn_act(1)
            y_squares(2, Y_FFN[1] + 4 * FBLOCKS - 4)

        @block.vector
        def _(dve):
            chain = [0]

            def link(ins):
                chain[0] += 1
                ins.then_inc(dve_chain, 1)
                dve.wait_ge(dve_chain, chain[0])

            def lo_group(g, chunks, width, hooks=None, units=range(8)):
                for u in units:
                    s, hf = divmod(u, 2)
                    n = min(2, chunks - 2 * hf)
                    dve.wait_ge(hi_done, 8 * g + u + 1)
                    nc.vector.tensor_tensor(w_lo[:, u % 4, 0:n, 0:width], w_raw[:, s, 2 * hf:2 * hf + n, 0:width],
                                            w_hi[:, u % 4, 0:n, 0:width].bitcast(F32), ALU.subtract).then_inc(lo_done, 1)
                    for h in (hooks or {}).get(u, ()):
                        h()

            def ada_unit(raw, landed, count, k, pos, done):
                def f():
                    dve.wait_ge(landed[0], landed[1])
                    dve.wait_ge(ada_done, done)
                    nc.vector.scalar_tensor_tensor(acc[:, pos, :], raw, cond[:, bass.ds(k, 1)], acc[:, pos, :],
                                                   ALU.mult, ALU.add).then_inc(ada_done, 1)
                return f

            def ada_hooks(mods, base, i, units, k0, hooks):
                n = 8 if units == 16 else 2 * len(mods)
                for a in range(n):
                    kk, m = divmod(a, len(mods))
                    count = base + n * i + a
                    use = (base - ADA_PRE) // 2 + (n // 2) * i + a // 2
                    unit = ada_unit(ada_raw[:, a % 2, :], (ada_landed[a % 2], 16 * use + 16), count, k0 + kk, mods[m][1], count)
                    hooks.setdefault(ada_after_lo(n, units, a), []).append(unit)
                return hooks

            def y_add(g, idx, n):
                ps = ps_t if n % 2 else ps_y

                def f():
                    dve.wait_ge(pe_used, 8 * g + 2 * n + 2)
                    need(dve, y_added, idx)
                    cols = yacc[:, :, n * NB:(n + 1) * NB]
                    nc.vector.tensor_tensor(cols, ps[:, :, :], cols, ALU.add).then_inc(y_added, 1)
                return f

            def h_mul(j, g, width):
                def f():
                    dve.wait_ge(silu_done, j + 1)
                    dve.wait_ge(pe_used, 8 * g + 8)
                    need(dve, ht_done, j)
                    nc.vector.tensor_tensor(hbuf[:, :, 0:width], ps_u[:, :, 0:width], silu[:, :, 0:width],
                                            ALU.mult).then_inc(h_done, 1)
                return f

            def ht_lo(j, chunks):
                def f():
                    dve.wait_ge(ht_hi_done, j + 1)
                    nc.vector.tensor_tensor(hT_lo[:, 0:chunks, :],
                                            ps_t[:, :, :].rearrange("p b (c n) -> p (b c) n", n=SEQ)[:, 0:chunks, :],
                                            hT_hi[:, 0:chunks, :].bitcast(F32), ALU.subtract).then_inc(ht_lo_done, 1)
                return f

            def mod_cols(n, which, pairs):
                def f():
                    for b, ps in enumerate(pairs):
                        dve.wait_ge(cols_done, 4 * n + 2 * which + b + 1)
                        picked = ada_raw[:, 1, b * 1024:(b + 1) * 1024].rearrange("p (k q) -> p k q", q=P)
                        link(nc.vector.tensor_tensor(picked, ps[:, :, :].rearrange("p b (k q) -> p (b k) q", q=P),
                                                     ident[:, :].unsqueeze(1).broadcast_to((P, 8, P)), ALU.mult))
                        ins = nc.vector.reduce_sum(modcol[:, n, 1 - which, 8 * b:8 * b + 8], picked, AX_X)
                        if b == 0 or which == 1:
                            link(ins)
                    if which == 1:
                        ins = nc.vector.scalar_tensor_tensor(modcol[:, n, 0, :], modcol[:, n, 0, :], 1.0, gpre[:, n, :], ALU.add, ALU.mult)
                    ins.then_inc(modcol_done, 1)
                return f

            def gates(n, pos, weight):
                def f():
                    dve.wait_ge(gpost_landed, 16 * n + 16)
                    dve.wait_ge(gbc_done, n + 1)
                    for b, ps in enumerate((ps_g, ps_u)):
                        part = slice(2 * b * NB, 2 * (b + 1) * NB)
                        last = nc.vector.scalar_tensor_tensor(
                            acc[:, pos, part], ps[:, :, :].rearrange("p b n -> p (b n)"), weight, ada_raw[:, 0, part],
                            ALU.mult, ALU.mult)
                    last.then_inc(gates_ready, 1)
                return f

            def ffn_dve(f):
                g0, j0, y0 = G_FFN[f], f * FBLOCKS, Y_FFN[f]
                dve.wait_ge(yacc_zero, 1 + 2 * f)
                lo_group(g0, 4, NB, xt_hooks(2 * f), range(4, 8))
                lo_group(g0 + 1, 4, NB)

                def hidden(j, g, width, hooks):
                    parts = [{}, {}, {}]
                    for at, work_ in hooks.items():
                        parts[at // 8].setdefault(at % 8, []).extend(work_)
                    parts[0].setdefault(0, []).append(y_add(g - 1, y0 + 4 * (j - 2) + 2, 2))
                    parts[0].setdefault(2, []).append(y_add(g - 1, y0 + 4 * (j - 2) + 3, 3))
                    parts[1].setdefault(4, []).append(ht_lo(j0 + j - 1, 4))
                    parts[2].setdefault(2, []).append(h_mul(j0 + j, g + 1, width))
                    parts[2].setdefault(4, []).append(y_add(g + 2, y0 + 4 * (j - 1), 0))
                    parts[2].setdefault(6, []).append(y_add(g + 2, y0 + 4 * (j - 1) + 1, 1))
                    lo_group(g, 4, width, parts[0])
                    lo_group(g + 1, 4, width, parts[1])
                    lo_group(g + 2, 4, NB, parts[2])

                lo_group(g0 + 2, 4, NB, {2: [h_mul(j0, g0 + 1, NB)]})
                lo_group(g0 + 3, 4, NB, {4: [ht_lo(j0, 4)]})
                lo_group(g0 + 4, 4, NB, {2: [h_mul(j0 + 1, g0 + 3, NB)], 4: [y_add(g0 + 4, y0, 0)], 6: [y_add(g0 + 4, y0 + 1, 1)]})
                dve.wait_ge(bias_landed, 16 * (6 if f == 0 else 9))
                with dve.Fori(0, LOOP) as i:
                    hidden(i + 2, g0 + 5 + 3 * i, NB, ada_hooks(MODS_FFN[f], ADA_FFN[f], i, 24, 2 * i, {}))
                last = FBLOCKS - 1
                hidden(last, g0 + 5 + 3 * LOOP, TAIL, {})
                yl, gy = y0 + 4 * last, g0 + 8 + 3 * LOOP
                tail = {0: [y_add(gy - 1, yl - 2, 2)], 2: [y_add(gy - 1, yl - 1, 3)], 3: [ht_lo(j0 + last, TAIL // P)],
                        4: [gates(2 * f, 1 if f == 0 else 3, 0.5)], 5: [y_add(gy, yl, 0)], 7: [y_add(gy, yl + 1, 1)]}
                if f == 0:
                    tail[6] = [mod_cols(1, 0, (ps_g, ps_u))]
                    tail[7].append(mod_cols(1, 1, (ps_g, ps_u)))
                lo_group(gy, TAIL // P, NB, tail)

            norms = [0]

            def norm_scale(col, width):
                nc.vector.tensor_scalar(ss[:, col:col + 2], ss[:, col:col + 2], 1.0 / width, EPS, ALU.mult, ALU.add).then_inc(var_ready, 1)
                norms[0] += 1
                dve.wait_ge(rstd_ready, norms[0])

            def residual(n, pos, g, y0):
                def gated(b):
                    dve.wait_ge(ysq_done, 4 * n + b + 1)
                    cols = slice(b * NB, (b + 1) * NB)
                    nc.vector.tensor_tensor(yacc[:, :, cols], yacc[:, :, cols],
                                            acc[:, pos, cols].unsqueeze(1).broadcast_to((P, TILES, NB)), ALU.mult).then_inc(y_gated, 1)

                y_add(g, y0 + 2, 2)()
                gated(0)
                y_add(g, y0 + 3, 3)()
                gated(1)
                gated(2)
                dve.wait_ge(ysq_done, 4 * n + 4)
                link(nc.vector.reduce_sum(ss[:, 0:2], ssy[:, :, :], AX_X))
                nc.vector.tensor_scalar(ss[:, 0:2], ss[:, 0:2], 1.0 / D, EPS, ALU.mult, ALU.add).then_inc(var_ready, 1)
                norms[0] += 1
                gated(3)
                dve.wait_ge(rstd_ready, norms[0])
                dve.wait_ge(y_gated, 4 * n + 4)
                for t in range(TILES):
                    nc.vector.scalar_tensor_tensor(x_sb[:, t, :], yacc[:, t, :], rstd[:, t:t + 1], x_sb[:, t, :],
                                                   ALU.mult, ALU.add).then_inc(x_new, 1)

            def input_scale(n):
                dve.wait_ge(xsq_done, 2 * n + 2)
                norm_scale(2, D)
                for t in range(TILES):
                    last = nc.vector.tensor_scalar(diag[:, t, :], ident[:, :], rstd[:, 2 + t:3 + t], None, ALU.mult)
                last.then_inc(diag_ready, 1)

            def xt_scale(n, b):
                def f():
                    if b == 0:
                        dve.wait_ge(rb_copied, n + 1)
                        dve.wait_ge(modcol_done, 2 * n + 2)
                    dve.wait_ge(xt_done, 8 * n + b + 1)
                    need(dve, xt_lo_done, 8 * n + b - 3 if b >= 4 else 0)
                    for c in range(2):
                        k = 2 * b + c
                        last = nc.vector.scalar_tensor_tensor(junk[:, (k % 8) * SEQ:(k % 8 + 1) * SEQ], banks[b][:, c * SEQ:(c + 1) * SEQ],
                                                              modcol[:, n, 0, k:k + 1], rbc[:, :], ALU.mult, ALU.mult)
                    last.then_inc(xt_scaled, 1)
                return f

            def xt_lo(n, b):
                def f():
                    dve.wait_ge(xt_hi_done, 8 * n + b + 1)
                    dve.wait_ge(xt_scaled, 8 * n + b + 1)
                    for c in range(2):
                        k = 2 * b + c
                        last = nc.vector.scalar_tensor_tensor(xT_lo[:, k, :], junk[:, (k % 8) * SEQ:(k % 8 + 1) * SEQ], modcol[:, n, 1, k:k + 1],
                                                              xT_hi[:, k, :].bitcast(F32), ALU.add, ALU.subtract)
                    last.then_inc(xt_lo_done, 1)
                return f

            def xt_hooks(n):
                return {4: [xt_scale(n, 4), xt_lo(n, 3)], 5: [xt_scale(n, 5), xt_lo(n, 4)], 6: [xt_scale(n, 6), xt_lo(n, 5)],
                        7: [xt_scale(n, 7), xt_lo(n, 6), xt_lo(n, 7)]}

            def into_part(n, g):
                lo_group(g, 4, NB, None, range(4))
                input_scale(n)
                for b in range(3):
                    xt_scale(n, b)()
                    if b:
                        xt_lo(n, b - 1)()
                xt_scale(n, 3)()
                xt_lo(n, 2)()

            banks = [q[:, i, :] for q in (ps_g, ps_u, ps_t, ps_y) for i in range(2)]

            dve.wait_ge(cond_ready, 1)
            dve.wait_ge(bias_landed, 32)
            dve.wait_ge(const_landed, 16 * 4)
            dve.wait_ge(ident_landed, 16)
            nc.vector.tensor_scalar(negsink[:, :], sink[:, :], -1.0, None, ALU.mult)

            def first_ada(m, i):
                for a in range(4):
                    dve.wait_ge(w_landed[a], 64 * m + 16 * i + 16)
                    dve.wait_ge(ada_done, 16 * m + 4 * i + a)
                    raw = w_raw[:, a].rearrange("p b n -> p (b n)")
                    pos = MODS_PRE[m][1]
                    nc.vector.scalar_tensor_tensor(acc[:, pos, :], raw, cond[:, bass.ds(4 * i + a, 1)], acc[:, pos, :],
                                                   ALU.mult, ALU.add).then_inc(ada_done, 1)

            with dve.Fori(0, 4) as i:
                first_ada(0, i)
            input_scale(0)
            mod_cols(0, 0, (ps_t, ps_y))()
            with dve.Fori(0, 4) as i:
                first_ada(1, i)
            mod_cols(0, 1, (ps_t, ps_y))()
            xt_scale(0, 0)()
            xt_scale(0, 1)()
            xt_lo(0, 0)()
            lo_group(0, 4, NB, None, range(2))
            xt_scale(0, 2)()
            xt_lo(0, 1)()
            lo_group(0, 4, NB, None, range(2, 4))
            xt_scale(0, 3)()
            xt_lo(0, 2)()
            ffn_dve(0)
            residual(0, 1, G_IN - 1, Y_OUT - 4)
            into_part(1, G_IN)

            dve.wait_ge(bias_landed, 16 * 8)

            def in_pair(i):
                hooks = ada_hooks(MODS_IN, ADA_IN, i, 16, 4 * i, {})
                first = {k: h for k, h in hooks.items() if k < 8}
                if isinstance(i, int):
                    for k, h in xt_hooks(1).items():
                        first.setdefault(k, []).extend(h)
                lo_group(G_IN + 2 * i, 4, NB, first, range(4 if isinstance(i, int) else 0, 8))
                lo_group(G_IN + 2 * i + 1, 4, NB, {k - 8: h for k, h in hooks.items() if k >= 8})

            early = ada_hooks(MODS_IN, ADA_IN, 0, 16, 0, {})
            for k in range(4):
                for h in early.get(k, ()):
                    h()
            in_pair(0)
            with dve.Fori(1, PBLOCKS // 2) as i:
                in_pair(i)
            lo_group(G_IN + PBLOCKS - 1, 4, PTAIL)
            mod_cols(2, 0, (ps_t, ps_y))()
            mod_cols(2, 1, (ps_t, ps_y))()

            dve.wait_ge(proj_done, PBLOCKS)
            for n_, a in enumerate((AK, AK + HD, BIK)):
                for dup in range(2):
                    last = nc.vector.tensor_copy(kdup[:, :, n_, dup * HD:(dup + 1) * HD], proj[:, :, a:a + HD])
            last.then_inc(kdup_done, 1)
            nc.vector.tensor_scalar(iws[:, :, :], proj[:, :, BIW:BIW + B_HEADS], B_HEADS ** -0.5, None, ALU.mult)
            dve.wait_ge(ckvsq_done, 2)
            norm_scale(4, KV_RANK)
            for t in range(TILES):
                last = nc.vector.scalar_tensor_tensor(ckv[:, t, :], proj[:, t, BKV:BKV + KV_RANK], rstd[:, 4 + t:5 + t],
                                                      kvg[:, :], ALU.mult, ALU.mult)
            last.then_inc(kdup_done, 1)

            link(nc.vector.tensor_scalar(score, dist_b[:, :], 0.1 * BIG, -1e37, ALU.is_ge, ALU.mult))
            for h in range(B_HEADS):
                dve.wait_ge(lg_done, h + 1)
                nc.vector.tensor_scalar(rw[:, 0:P], ps_g[:, h % 2, 0:P], 0.0, iws[:, 0, h:h + 1], ALU.max, ALU.mult)
                last = nc.vector.tensor_scalar(rw[:, P:3 * P], ps_g[:, h % 2, P:3 * P], 0.0, iws[:, 1, h:h + 1], ALU.max, ALU.mult)
                last.then_inc(lg_used, 1)
                dve.wait_ge(lg_used, h + 1)
                if h == 0:
                    link(nc.vector.tensor_copy(pick, rw))
                else:
                    link(nc.vector.tensor_tensor(pick, pick, rw, ALU.add))
            link(nc.vector.tensor_tensor(pick, pick, score, ALU.add))

            def top_round():
                for t in range(TILES):
                    keys = slice(0, P) if t == 0 else slice(P, 3 * P)
                    last = nc.vector.max(top8[:, t, :], pick[:, keys])
                link(last)
                for t in range(TILES):
                    keys = slice(0, P) if t == 0 else slice(P, 3 * P)
                    last = nc.vector.match_replace(pick[:, keys], top8[:, t, :], pick[:, keys], -3e38)
                link(last)

            def selected_distances():
                link(nc.vector.tensor_scalar(dist_sel, pick, -2e38, BIG, ALU.is_ge, ALU.mult))
                link(nc.vector.tensor_tensor(dist_sel, dist_sel, dist_b[:, :], ALU.max))

            side_work = {s: top_round for s in range(TOPK // 8)}
            side_work[TOPK // 8] = selected_distances

            def pair_lo(q):
                dve.wait_ge(o_hi_done, q + 1)
                nc.vector.tensor_tensor(xT_lo[:, q, :], ps_t[:, q % 2, 0:SEQ], xT_hi[:, q, :].bitcast(F32), ALU.subtract).then_inc(o_lo_done, 1)

            for step in range(STEPS):
                h = step
                if h < HEADS:
                    st = stat[:, h % 2, :]
                    dist = dist_a[:, :] if h < A_HEADS else dist_sel
                    dve.wait_ge(s_done, h + 1)
                    need(dve, e_done, h - 1)
                    link(nc.vector.scalar_tensor_tensor(sc[:, h % 2, :], dist, -slope[h] * HD ** 0.5, ps_g[:, h % 2, 0:3 * P],
                                                        ALU.mult, ALU.add))
                    nc.vector.reduce_max(st[:, 0:1], sc[:, h % 2, 0:P], AX_X)
                    link(nc.vector.reduce_max(st[:, 1:2], sc[:, h % 2, P:3 * P], AX_X))
                    if h < A_HEADS:
                        nc.vector.tensor_scalar(st[:, 2:4], st[:, 0:2], -HD ** -0.5, negsink[:, h:h + 1], ALU.mult, ALU.min).then_inc(s_biased, 1)
                    else:
                        nc.vector.tensor_scalar(st[:, 2:4], st[:, 0:2], -HD ** -0.5, None, ALU.mult).then_inc(s_biased, 1)
                h = step - 1
                if 0 <= h < HEADS:
                    st = stat[:, h % 2, :]
                    dve.wait_ge(e_done, h + 1)
                    if h < A_HEADS:
                        link(nc.vector.tensor_tensor(st[:, 4:6], st[:, 4:6], st[:, 6:8], ALU.add))
                    link(nc.vector.reciprocal(st[:, 8:10], st[:, 4:6]))
                    nc.vector.tensor_scalar(pr[:, h % 2, 0:P], pr[:, h % 2, 0:P], st[:, 8:9], None, ALU.mult)
                    nc.vector.tensor_scalar(pr[:, h % 2, P:], pr[:, h % 2, P:], st[:, 9:10], None, ALU.mult).then_inc(p_ready, 1)
                for q in range(HEADS // 2):
                    if step == pair_step(q):
                        pair_lo(q)
                if step in side_work:
                    side_work[step]()

            dve.wait_ge(decay_landed, 16)
            for h in range(C_HEADS):
                dve.wait_ge(r_done, h + 1)
                need(dve, ro_done_head, h - 1)
                nc.vector.tensor_tensor(sc[:, h % 2, 0:SEQ], ps_g[:, h % 2, 0:SEQ], decay[:, h, :], ALU.mult)
                nc.vector.tensor_tensor(sc[:, h % 2, SEQ:3 * P], ps_g[:, h % 2, SEQ:3 * P], decay[:, h, 0:P], ALU.mult).then_inc(r_decayed, 1)
            dve.wait_ge(r_decayed, C_HEADS)
            dve.wait_ge(ro_copied, 1)

            ro_h = ro.rearrange("p t (h d) -> p (t h) d", d=HD)
            cent_h = cent.rearrange("p t (h d) -> p (t h) d", d=HD)
            link(nc.vector.reduce_sum(rstat[:, 0, :], ro_h, AX_X))
            link(nc.vector.tensor_scalar(rstat[:, 0, :], rstat[:, 0, :], 1.0 / HD, None, ALU.mult))
            nc.vector.tensor_tensor(cent_h, ro_h, rstat[:, 0, :].unsqueeze(2).broadcast_to((P, 16, HD)), ALU.subtract).then_inc(cent_ready, 1)
            dve.wait_ge(csq_done, 1)
            link(nc.vector.reduce_sum(rstat[:, 1, :], csq.rearrange("p t (h d) -> p (t h) d", d=HD), AX_X))
            nc.vector.tensor_scalar(rstat[:, 1, :], rstat[:, 1, :], 1.0 / HD, EPS, ALU.mult, ALU.add).then_inc(rvar_ready, 1)
            dve.wait_ge(tab_landed, 16 * 3)
            dve.wait_ge(rrstd_ready, 1)
            link(nc.vector.tensor_tensor(cent_h, cent_h, rstat[:, 2, :].unsqueeze(2).broadcast_to((P, 16, HD)), ALU.mult))
            for t in range(TILES):
                last = nc.vector.tensor_tensor(cent[:, t, :], cent[:, t, :], rnorm, ALU.mult)
            link(last)
            dve.wait_ge(cgate_done, 1)
            nc.vector.tensor_tensor(cent, cent, cgate, ALU.mult).then_inc(oc_ready, 1)
            for b in range(2):
                dve.wait_ge(o_hi_done, HEADS // 2 + b + 1)
                last = nc.vector.tensor_tensor(xT_lo[:, 12 + 2 * b:14 + 2 * b, :], ps_y[:, b, :].rearrange("p (c n) -> p c n", n=SEQ),
                                               xT_hi[:, 12 + 2 * b:14 + 2 * b, :].bitcast(F32), ALU.subtract)
            last.then_inc(mix_ready, 1)

            dve.wait_ge(yacc_zero, 2)
            for g in range(4):
                y0 = Y_OUT + 4 * g
                hooks = {5: [y_add(G_OUT + g, y0, 0)], 7: [y_add(G_OUT + g, y0 + 1, 1)]}
                if g:
                    hooks[0] = [y_add(G_OUT + g - 1, y0 - 2, 2)]
                    hooks[2] = [y_add(G_OUT + g - 1, y0 - 1, 3)]
                if g == 3:
                    hooks[4] = [gates(1, 0, 1.0)]
                lo_group(G_OUT + g, 4, NB, hooks)
            residual(1, 0, G_OUT + 3, Y_OUT + 12)
            into_part(2, G_FFN[1])
            ffn_dve(1)
            residual(2, 3, G_FFN[1] + FFN_GROUPS - 1, Y_FFN[1] + 4 * FBLOCKS - 4)

        @block.tensor
        def _(pe):
            def unit(a_hi, a_lo, chunk0, b, n, width, out_of, first, last_unit):
                for t in range(TILES):
                    rows = slice(t * P, (t + 1) * P)
                    for c in range(n):
                        k = chunk0 + c
                        start, stop = first and c == 0, last_unit and c == n - 1
                        o = out_of(t)
                        nc.tensor.matmul(o, a_hi[:, k, rows], w_hi[:, b, c, 0:width], start=start, stop=False)
                        nc.tensor.matmul(o, a_hi[:, k, rows], w_lo[:, b, c, 0:width], start=False, stop=False)
                        ins = nc.tensor.matmul(o, a_lo[:, k, rows], w_hi[:, b, c, 0:width], start=False, stop=stop)
                return ins

            def in_group(g, width, ps, part=None):
                if part is not None:
                    pe.wait_ge(xt_scaled, 8 * part + 2)
                for u in range(8):
                    pe.wait_ge(lo_done, 8 * g + u + 1)
                    if part is not None:
                        pe.wait_ge(xt_lo_done, 8 * part + u + 1)
                    unit(xT_hi, xT_lo, 2 * u, u % 4, 2, width, lambda t: ps[:, t, 0:width], u == 0, u == 7).then_inc(pe_used, 1)

            def out_group(g, a_hi, a_lo, chunk0, chunks, y0, blocks=range(4)):
                for n in blocks:
                    ps = ps_t if n % 2 else ps_y
                    need(pe, y_added, y0 + n - 1)
                    for hf in range(2):
                        m = min(2, chunks - 2 * hf)
                        pe.wait_ge(lo_done, 8 * g + 2 * n + hf + 1)
                        ins = unit(a_hi, a_lo, chunk0 + 2 * hf, (2 * n + hf) % 4, m, NB, lambda t: ps[:, t, :], hf == 0, hf == 1)
                        ins.then_inc(pe_used, 1)

            def transpose_h(j, chunks, y_before):
                pe.wait_ge(h_done, j + 1)
                need(pe, y_added, y_before)
                for c in range(chunks):
                    for t in range(TILES):
                        col = (c % 2) * SEQ + t * P
                        ins = nc.tensor.transpose(ps_t[:, c // 2, col:col + P], hbuf[:, t, c * P:(c + 1) * P], ident[:, :])
                ins.then_inc(ht_done, 1)

            def mod_rows(pos, pairs, free, count):
                pe.wait_ge(ada_done, count)
                for b, ps in enumerate(pairs):
                    pe.wait_ge(*free[b])
                    for n in range(2):
                        col = (2 * b + n) * NB
                        ins = nc.tensor.matmul(ps[:, n, :], ones[:, :], acc[:, pos, col:col + NB], start=True, stop=True)
                    ins.then_inc(cols_done, 1)

            def gate_rows(pos, count):
                pe.wait_ge(ada_done, count)
                for n in range(4):
                    ps = (ps_g, ps_u)[n // 2]
                    ins = nc.tensor.matmul(ps[:, n % 2, :], ones[:, :], acc[:, pos, n * NB:(n + 1) * NB], start=True, stop=True)
                ins.then_inc(gbc_done, 1)

            banks = [q[:, i, :] for q in (ps_g, ps_u, ps_t, ps_y) for i in range(2)]

            def x_transposes(b, t):
                for c in range(2):
                    k = 2 * b + c
                    ins = nc.tensor.transpose(banks[b][:, c * SEQ + t * P:c * SEQ + (t + 1) * P],
                                              x_sb[:, t, k * P:(k + 1) * P], ident[:, :])
                return ins

            def row_scale(n):
                pe.wait_ge(diag_ready, n + 1)
                for t in range(TILES):
                    ins = nc.tensor.matmul(ps_y[:, 1, t * P:(t + 1) * P], ones[:, :], diag[:, t, :], start=True, stop=True)
                ins.then_inc(rb_done, 1)
                pe.wait_ge(rb_copied, n + 1)

            def transpose_x(n):
                for t in range(TILES):
                    pe.wait_ge(x_new, TILES * (n - 1) + t + 1)
                    for b in range(7):
                        ins = x_transposes(b, t)
                        if t == 1:
                            ins.then_inc(xt_done, 1)
                row_scale(n)
                x_transposes(7, 0)
                x_transposes(7, 1).then_inc(xt_done, 1)

            def ffn_pe(f):
                g0, j0, y0 = G_FFN[f], f * FBLOCKS, Y_FFN[f]
                in_group(g0, NB, ps_g, 2 * f)
                in_group(g0 + 1, NB, ps_u)

                def hidden(j, g, width):
                    need(pe, silu_done, j0 + j)
                    in_group(g, width, ps_g)
                    transpose_h(j0 + j - 1, 4, y0 + 4 * (j - 1))
                    need(pe, h_done, j0 + j)
                    in_group(g + 1, width, ps_u)
                    pe.wait_ge(ht_lo_done, j0 + j)
                    out_group(g + 2, hT_hi, hT_lo, 0, 4, y0 + 4 * (j - 1))

                hidden(1, g0 + 2, NB)
                with pe.Fori(0, LOOP) as i:
                    hidden(i + 2, g0 + 5 + 3 * i, NB)
                last = FBLOCKS - 1
                hidden(last, g0 + 5 + 3 * LOOP, TAIL)
                gate_rows(1 if f == 0 else 3, ADA_IN if f == 0 else ADA_FFN[1] + 16)
                transpose_h(j0 + last, TAIL // P, y0 + 4 * last)
                pe.wait_ge(ht_lo_done, j0 + FBLOCKS)
                g, yl = g0 + 8 + 3 * LOOP, y0 + 4 * last
                if f == 0:
                    out_group(g, hT_hi, hT_lo, 0, TAIL // P, yl, range(0, 2))
                    mod_rows(3 - 1, (ps_g, ps_u), ((gates_ready, 1), (gates_ready, 1)), ADA_IN)
                    out_group(g, hT_hi, hT_lo, 0, TAIL // P, yl, range(2, 3))
                    mod_rows(3, (ps_g, ps_u), ((modcol_done, 3), (modcol_done, 3)), ADA_IN)
                    out_group(g, hT_hi, hT_lo, 0, TAIL // P, yl, range(3, 4))
                else:
                    out_group(g, hT_hi, hT_lo, 0, TAIL // P, yl)

            pe.wait_ge(ident_landed, 16)
            pe.wait_ge(c_landed, 16 * 4)
            nc.tensor.transpose(ps_y[:, 0, 0:4 * KD], rows64[:, :], ident[0:4 * KD, 0:4 * KD]).then_inc(small_done, 1)
            pe.wait_ge(x_landed, 16)
            for b in range(4):
                x_transposes(b, 0)
                x_transposes(b, 1).then_inc(xt_done, 1)
            pe.wait_ge(consts_set, 1)
            pe.wait_ge(cond_ready, 1)
            row_scale(0)
            mod_rows(1, (ps_t, ps_y), ((rb_copied, 1), (rb_copied, 1)), 16)
            mod_rows(2, (ps_t, ps_y), ((modcol_done, 1), (modcol_done, 1)), ADA_PRE)
            pe.wait_ge(modcol_done, 2)
            for b in range(4, 8):
                x_transposes(b, 0)
                x_transposes(b, 1).then_inc(xt_done, 1)
            ffn_pe(0)
            transpose_x(1)

            in_group(G_IN, NB, ps_g, 1)
            in_group(G_IN + 1, NB, ps_u)
            with pe.Fori(1, PBLOCKS // 2) as i:
                pe.wait_ge(proj_done, 2 * i - 1)
                in_group(G_IN + 2 * i, NB, ps_g)
                pe.wait_ge(proj_done, 2 * i)
                in_group(G_IN + 2 * i + 1, NB, ps_u)
            pe.wait_ge(proj_done, PBLOCKS - 2)
            in_group(G_IN + PBLOCKS - 1, PTAIL, ps_g)
            mod_rows(1, (ps_t, ps_y), ((xt_scaled, 16), (xt_scaled, 16)), ADA_FFN[1])
            mod_rows(2, (ps_t, ps_y), ((modcol_done, 5), (modcol_done, 5)), ADA_FFN[1])
            pe.wait_ge(modcol_done, 6)

            def transposes(b0, b1):
                for b in range(b0, b1):
                    need(pe, tp_copied, b - 1)
                    if b == 4:
                        pe.wait_ge(kdup_done, 1)
                    if b == TP_AB - 1:
                        pe.wait_ge(kdup_done, 2)
                    for c in range(2):
                        for t in range(TILES):
                            col = c * SEQ + t * P
                            ins = nc.tensor.transpose(ps_y[:, b % 2, col:col + P], TP[b][0][c](t), ident[:, :])
                    ins.then_inc(tp_done, 1)

            pe.wait_ge(proj_done, PBLOCKS)
            transposes(0, TP_AB)
            pe.wait_ge(tab_landed, 16 * 3)
            pe.wait_ge(tp_copied, TP_AB)
            for c in range(4):
                ins = nc.tensor.transpose(ps_y[:, 0, c * P:(c + 1) * P], w_uk[:, c * P:(c + 1) * P], ident[:, :])
            ins.then_inc(ukT_done, 1)
            pe.wait_ge(ukT_copied, 1)
            for h in range(B_HEADS):
                need(pe, ql_copied, h - 1)
                rows = slice((h % 2) * HD, (h % 2 + 1) * HD)
                nc.tensor.matmul(ps_y[:, h % 2, 0:SEQ], w_ukT[rows, h // 2, :], qT_b[rows, h // 2, :],
                                 start=True, stop=True).then_inc(ql_done, 1)

            def two_tiles(bank, q_of, keys):
                nc.tensor.matmul(bank[:, 0:P], q_of(0), keys[:, 0:P], start=True, stop=True)
                return nc.tensor.matmul(bank[:, P:3 * P], q_of(1), keys, start=True, stop=True)

            for h in range(B_HEADS):
                rows = slice((h % 2) * HD, (h % 2 + 1) * HD)
                need(pe, lg_used, h - 1)
                two_tiles(ps_g[:, h % 2, :], lambda t: iqT[rows, h // 2, t * P:(t + 1) * P], ikT[rows, :]).then_inc(lg_done, 1)
            pe.wait_ge(lg_used, B_HEADS)
            pe.wait_ge(ql_copied, B_HEADS)
            pe.wait_ge(modcol_done, 6)

            for step in range(STEPS):
                h = step
                if h < HEADS:
                    need(pe, s_biased, h - 1)
                    if h < A_HEADS:
                        rows = slice((h % 2) * HD, (h % 2 + 1) * HD)
                        ins = two_tiles(ps_g[:, h % 2, :], lambda t: qT_a[rows, h // 2, t * P:(t + 1) * P],
                                        akT[rows, h // (A_HEADS // A_KV), :])
                    else:
                        ins = two_tiles(ps_g[:, h % 2, :], lambda t: qlatT[:, h - A_HEADS, t * P:(t + 1) * P], ckvT)
                    ins.then_inc(s_done, 1)
                h = step - 2
                if 0 <= h < HEADS:
                    pe.wait_ge(p_ready, h + 1)
                    need(pe, pt_copied, h - 1)
                    for c in range(2):
                        nc.tensor.transpose(ps_u[:, h % 2, c * P:(c + 1) * P], pr[:, h % 2, c * P:(c + 1) * P], ident[:, :])
                    nc.tensor.transpose(ps_u[:, h % 2, 2 * P:3 * P], pr[:, h % 2, 2 * P:3 * P], ident[:, :]).then_inc(pt_done, 1)
                h = step - 3
                if 0 <= h < HEADS:
                    pe.wait_ge(pt_copied, h + 1)
                    if h < A_HEADS:
                        q = h // 2
                        need(pe, o_lo_done, q - 1)
                        kv = AV + (h // (A_HEADS // A_KV)) * HD
                        o = ps_t[(h % 2) * HD:(h % 2 + 1) * HD, q % 2, 0:SEQ]
                        values = [proj[:, t, kv:kv + HD] for t in range(TILES)]
                    else:
                        need(pe, ol_copied, h - A_HEADS - 1)
                        o = ps_y[:, h % 2, 0:SEQ]
                        values = [ckv[:, t, :] for t in range(TILES)]
                    nc.tensor.matmul(o, values[0], pT[:, h % 2, 0:SEQ], start=True, stop=False)
                    ins = nc.tensor.matmul(o[:, P:SEQ], values[1], pT[:, h % 2, SEQ:3 * P], start=False, stop=True)
                    ins.then_inc(pv_done, 1)
                h = step - 5
                if A_HEADS <= h < HEADS:
                    q = h // 2
                    pe.wait_ge(ol_copied, h - A_HEADS + 1)
                    pe.wait_ge(o_lo_done, q - 1)
                    ins = nc.tensor.matmul(ps_t[(h % 2) * HD:(h % 2 + 1) * HD, q % 2, 0:SEQ],
                                           w_uv[:, (h - A_HEADS) * HD:(h - A_HEADS + 1) * HD], olatT[:, h % 2, :], start=True, stop=True)
                    ins.then_inc(uv_done, 1)

            pe.wait_ge(ol_copied, B_HEADS)
            transposes(TP_AB, len(TP))
            pe.wait_ge(tp_copied, len(TP))
            pe.wait_ge(o_lo_done, HEADS // 2)
            for step in range(C_HEADS + 1):
                h = step
                if h < C_HEADS:
                    rows = slice((h % 2) * HD, (h % 2 + 1) * HD)
                    need(pe, r_decayed, h - 1)
                    nc.tensor.matmul(ps_g[:, h % 2, 0:SEQ], ckT[rows, h // 2, 0:P], cqT[rows, h // 2, :], start=True, stop=True)
                    nc.tensor.matmul(ps_g[:, h % 2, SEQ:3 * P], ckT[rows, h // 2, P:SEQ], cqT[rows, h // 2, P:SEQ],
                                     start=True, stop=True).then_inc(r_done, 1)
                h = step - 1
                if h >= 0:
                    pe.wait_ge(r_decayed, h + 1)
                    v = [proj[:, t, CV + h * HD:CV + (h + 1) * HD] for t in range(TILES)]
                    cols = slice(h * HD, (h + 1) * HD)
                    nc.tensor.matmul(ps_t[:, 0, cols], sc[:, h % 2, 0:P], v[0], start=True, stop=True)
                    nc.tensor.matmul(ps_t[:, 1, cols], sc[:, h % 2, P:SEQ], v[0], start=True, stop=False)
                    nc.tensor.matmul(ps_t[:, 1, cols], sc[:, h % 2, SEQ:3 * P], v[1], start=False, stop=True).then_inc(ro_done_head, 1)
            pe.wait_ge(oc_ready, 1)
            for b in range(2):
                for c in range(2):
                    for t in range(TILES):
                        k = 2 * b + c
                        ins = nc.tensor.transpose(ps_y[:, b, c * SEQ + t * P:c * SEQ + (t + 1) * P], cent[:, t, k * P:(k + 1) * P], ident[:, :])
                ins.then_inc(oct_done, 1)

            pe.wait_ge(mix_ready, 1)
            for g in range(4):
                if g == 3:
                    gate_rows(0, ADA_IN)
                out_group(G_OUT + g, xT_hi, xT_lo, 4 * g, 4, Y_OUT + 4 * g)
            transpose_x(2)
            ffn_pe(1)


_INS = ["x", "c", "ada_w", "ada_b", "norm_g", "ffn1_w_in", "ffn1_w_out", "ffn2_w_in", "ffn2_w_out", "mix_w_in", "mix_w_out",
        "swa_sinks", "dsa_kv_norm", "dsa_w_uk", "dsa_w_uv", "ret_norm"]


def shape_constants():
    i = np.arange(P)[:, None].astype(np.float64)
    j = np.arange(P)[None, :].astype(np.float64)
    own = np.where(j <= i, i - j, BIG)
    window = np.where(j > i, i - j + P, BIG)
    gamma = 1.0 - 2.0 ** (-5.0 - np.arange(C_HEADS))
    q = np.arange(SEQ)[None, None, :]
    diff = q - np.arange(P)[:, None, None]
    decays = np.where(diff >= 0, gamma[None, :, None] ** np.maximum(diff, 0), 0.0) * HD ** -0.5
    parts = [np.eye(P), own, window, own, own, i - j + P, own, decays.reshape(P, -1)]
    return np.concatenate(parts, axis=1).astype(np.float32)


def kernel(**inputs):
    import concourse.bacc as _bacc
    from concourse.bass_utils import run_bass_kernel_spmd as _run

    nc = _bacc.Bacc("TRN2", target_bir_lowering=False, num_devices=1)
    arrays, args = {}, []
    given = {name: np.ascontiguousarray(inputs[name]) for name in _INS}
    given["consts"] = shape_constants()
    for name, a in given.items():
        arrays[f"in_{name}"] = a
        args.append(nc.dram_tensor(f"in_{name}", a.shape, mybir.dt.from_np(a.dtype), kind="ExternalInput").ap())
    args.append(nc.dram_tensor("out", (1, SEQ, D), F32, kind="ExternalOutput").ap())
    build(nc, *args)
    r = _run(nc, [arrays], core_ids=[0])
    return r.results[0]["out"]
```

```python
from contextlib import ExitStack

import numpy as np

import concourse.bass as bass
from concourse import mybir

ALU = mybir.AluOpType
ACT = mybir.ActivationFunctionType
F32 = mybir.dt.float32
F32R = mybir.dt.float32r
AX_X = mybir.AxisListType.X

P = 128
SEQ, D, DFF = 256, 2048, 5504
TILES = SEQ // P
KD = D // P
NB = 512
HD = 64
A_HEADS, A_KV, B_HEADS, C_HEADS = 16, 2, 8, 8
KV_RANK = 128
EPS = 1e-6
BIG = 1e30

COLS = (A_HEADS * HD, A_KV * HD, A_KV * HD, B_HEADS * HD, KV_RANK, B_HEADS * HD, HD, B_HEADS,
        C_HEADS * HD, C_HEADS * HD, C_HEADS * HD, C_HEADS * HD)
AQ, AK, AV, BQ, BKV, BIQ, BIK, BIW, CQ, CK, CV, CG = [sum(COLS[:i]) for i in range(len(COLS))]
MIX_IN = sum(COLS)
TOPK = min(256, SEQ // 4)

FBLOCKS = -(-DFF // NB)
TAIL = DFF - (FBLOCKS - 1) * NB
LOOP = 8
PBLOCKS = -(-MIX_IN // NB)
PTAIL = MIX_IN - (PBLOCKS - 1) * NB

FFN_GROUPS = 3 * FBLOCKS
G_FFN = (0, FFN_GROUPS + PBLOCKS + 4)
G_IN = FFN_GROUPS
G_OUT = G_IN + PBLOCKS
Y_FFN = (0, 4 * FBLOCKS + 16)
Y_OUT = 4 * FBLOCKS
PRE_USES = 8
STRIPS = 4
OPENING = 3
ADA_PRE = 32
ADA_FFN = (ADA_PRE, ADA_PRE + 64 + 32)
ADA_IN = ADA_PRE + 64
MODS_PRE = ((0, 1), (1, 2))
MODS_FFN = (((2, 1), (3, 2), (4, 3), (5, 0)), ((8, 3),))
MODS_IN = ((6, 1), (7, 2))


def need(eng, sem, value):
    if isinstance(value, int) and value <= 0:
        return
    eng.wait_ge(sem, value)


def build(nc, x_in, c_in, ada_w, ada_b, norm_g, f1_in, f1_out, f2_in, f2_out, m_in, m_out, sinks_in,
          kvn_in, uk_in, uv_in, rn_in, consts, out):
    ctx = ExitStack()
    with ctx:
        def sb(name, shape, dt=F32):
            return ctx.enter_context(nc.sbuf_tensor(name, shape, dt))

        def sem(name):
            return ctx.enter_context(nc.semaphore(name))

        x_sb = sb("x_sb", [P, TILES, D])
        xT_hi = sb("xT_hi", [P, KD, SEQ], F32R)
        xT_lo = sb("xT_lo", [P, KD, SEQ], F32R)
        w_raw = sb("w_raw", [P, 4, 4, NB])
        w_hi = sb("w_hi", [P, 4, 2, NB], F32R)
        w_lo = sb("w_lo", [P, 4, 2, NB], F32R)
        hT_hi = sb("hT_hi", [P, 4, SEQ], F32R)
        hT_lo = sb("hT_lo", [P, 4, SEQ], F32R)
        ada_raw = sb("ada_raw", [P, 2, D])
        def ada_raw_slot(s):
            return ada_raw[:, s, :]

        work_w = 7056
        arena = sb("arena", [P, 4 * D + work_w])
        acc = arena[:, 0:4 * D].rearrange("p (m d) -> p m d", m=4)
        work = arena[:, 4 * D:4 * D + work_w]
        yacc = work[:, 0:TILES * D].rearrange("p (t d) -> p t d", t=TILES)
        silu = work[:, 4096:5120].rearrange("p (t n) -> p t n", t=TILES)
        hbuf = work[:, 5120:6144].rearrange("p (t n) -> p t n", t=TILES)
        junk = work[:, 4096:6144]
        xT_raw = work[:, 0:KD * SEQ].rearrange("p (k n) -> p k n", n=SEQ)
        first_slots = [ada_raw_slot(0), ada_raw_slot(1), acc[:, 0, :], acc[:, 3, :]]
        proj = arena[:, 3 * D:3 * D + TILES * MIX_IN].rearrange("p (t n) -> p t n", t=TILES)
        assert 3 * D + TILES * MIX_IN <= 4 * D + work_w
        ident = sb("ident", [P, P])
        ones = sb("ones", [P, P])
        dist_a = sb("dist_a", [P, 3 * P])
        dist_b = sb("dist_b", [P, 3 * P])
        kvg = sb("kvg", [P, KV_RANK])
        small_rows = sb("small_rows", [6 * KD, P])
        cond = sb("cond", [P, KD])
        bias1 = sb("bias1", [P, 2, KD])
        gpre = sb("gpre", [P, 3, KD])
        modcol = sb("modcol", [P, 3, 2, KD])
        sink = sb("sink", [P, A_HEADS])
        negsink = sb("negsink", [P, A_HEADS])
        iws = sb("iws", [P, TILES, B_HEADS])
        ss = sb("ss", [P, 8])
        ssy = sb("ssy", [P, TILES, 4])
        diag = sb("diag", [P, TILES, P])
        rbc = sb("rbc", [P, SEQ])
        rstd = sb("rstd", [P, 8])
        neghalf = sb("neghalf", [P, 16])
        stat = sb("stat", [P, 2, 12])
        rstat = sb("rstat", [P, 4, 16])
        top8 = sb("top8", [P, TILES, 8])
        t1 = arena[:, D:3 * D]
        t2 = ada_raw[:, :, :].rearrange("p a n -> p (a n)")
        t3 = w_raw[:, 2:4].rearrange("p a b n -> p (a b n)")
        qT_a = t1[:, 0:2048].rearrange("p (c n) -> p c n", n=SEQ)
        qlatT = w_raw[:, 1].rearrange("p b n -> p (b n)").rearrange("p (c n) -> p c n", n=SEQ)
        qT_b = t1[:, 2048:3072].rearrange("p (c n) -> p c n", n=SEQ)
        iqT = t1[:, 3072:4096].rearrange("p (c n) -> p c n", n=SEQ)
        cqT, ckT = qT_b, iqT
        sc = t2[:, 0:768].rearrange("p (b n) -> p b n", b=2)
        pr = t2[:, 768:1536].rearrange("p (b n) -> p b n", b=2)
        pT = t2[:, 1536:2304].rearrange("p (b n) -> p b n", b=2)
        akT = t2[:, 2304:2816].rearrange("p (c n) -> p c n", n=SEQ)
        ikT = t2[:, 2816:3072]
        ckvT = t2[:, 3072:3328]
        ckv = t2[:, 3328:3584].rearrange("p (t n) -> p t n", t=TILES)
        olatT = t2[:, 3584:4096].rearrange("p (b n) -> p b n", b=2)
        w_uk = t3[:, 0:512]
        w_uv = t3[:, 512:1024]
        w_ukT = t3[:, 1024:1536].rearrange("p (c n) -> p c n", n=P)
        score = t3[:, 1536:1920]
        pick = t3[:, 1920:2304]
        dist_sel = t3[:, 2304:2688]
        rw = t3[:, 2688:3072]
        kdup = t3[:, 3072:3840].rearrange("p (t s n) -> p t s n", t=TILES, s=3)
        decay = t1[:, 0:2048].rearrange("p (h n) -> p h n", n=SEQ)
        ro = t2[:, 768:1792].rearrange("p (t n) -> p t n", t=TILES)
        rnorm = t2[:, 1792:2304]
        cent = t1[:, 0:1024].rearrange("p (t n) -> p t n", t=TILES)
        csq = t1[:, 1024:2048].rearrange("p (t n) -> p t n", t=TILES)
        cgate = t2[:, 3072:4096].rearrange("p (t n) -> p t n", t=TILES)

        ps_g = ctx.enter_context(nc.psum_tensor("ps_g", [P, 2, NB], F32))
        ps_u = ctx.enter_context(nc.psum_tensor("ps_u", [P, 2, NB], F32))
        ps_t = ctx.enter_context(nc.psum_tensor("ps_t", [P, 2, NB], F32))
        ps_y = ctx.enter_context(nc.psum_tensor("ps_y", [P, 2, NB], F32))

        banks = [q[:, i, :] for q in (ps_g, ps_u, ps_t, ps_y) for i in range(2)]

        w_landed = [sem(f"w_landed{s}") for s in range(4)]
        ada_landed = [sem(f"ada_landed{s}") for s in range(4)]
        c_landed, x_landed, const_landed = sem("c_landed"), sem("x_landed"), sem("const_landed")
        gpost_landed, tab_landed, out_landed = sem("gpost_landed"), sem("tab_landed"), sem("out_landed")
        decay_landed, uv_done, ro_done_head = sem("decay_landed"), sem("uv_done"), sem("ro_done_head")
        bias_landed = sem("bias_landed")
        ident_landed, small_done = sem("ident_landed"), sem("small_done")
        cond_ready, acc_zero, consts_set = sem("cond_ready"), sem("acc_zero"), sem("consts_set")
        yacc_zero = sem("yacc_zero")
        hi_done, lo_done, pe_used = sem("hi_done"), sem("lo_done"), sem("pe_used")
        ada_done = sem("ada_done")
        silu_done, h_done = sem("silu_done"), sem("h_done")
        ht_done, ht_hi_done, ht_lo_done = sem("ht_done"), sem("ht_hi_done"), sem("ht_lo_done")
        y_added, y_gated, proj_done = sem("y_added"), sem("y_gated"), sem("proj_done")
        cols_done, modcol_done = sem("cols_done"), sem("modcol_done")
        gbc_done, gates_ready = sem("gbc_done"), sem("gates_ready")
        ysq_done, xsq_done, var_ready, rstd_ready = sem("ysq_done"), sem("xsq_done"), sem("var_ready"), sem("rstd_ready")
        xt_copied = sem("xt_copied")
        x_new, diag_ready, rb_done, rb_copied = sem("x_new"), sem("diag_ready"), sem("rb_done"), sem("rb_copied")
        xt_done, xt_scaled, xt_hi_done, xt_lo_done = sem("xt_done"), sem("xt_scaled"), sem("xt_hi_done"), sem("xt_lo_done")
        dve_chain, act_chain = sem("dve_chain"), sem("act_chain")
        kdup_done, ckvsq_done, tp_done, tp_copied = sem("kdup_done"), sem("ckvsq_done"), sem("tp_done"), sem("tp_copied")
        ukT_done, ukT_copied = sem("ukT_done"), sem("ukT_copied")
        ql_done, ql_copied = sem("ql_done"), sem("ql_copied")
        lg_done, lg_used = sem("lg_done"), sem("lg_used")
        s_done, s_biased, e_done, p_ready = sem("s_done"), sem("s_biased"), sem("e_done"), sem("p_ready")
        pt_done, pt_copied, pv_done = sem("pt_done"), sem("pt_copied"), sem("pv_done")
        ol_copied, o_hi_done, o_lo_done = sem("ol_copied"), sem("o_hi_done"), sem("o_lo_done")
        r_done, r_decayed, ro_copied = sem("r_done"), sem("r_decayed"), sem("ro_copied")
        cent_ready, csq_done, rvar_ready, rrstd_ready = sem("cent_ready"), sem("csq_done"), sem("rvar_ready"), sem("rrstd_ready")
        cgate_done, oc_ready, oct_done = sem("cgate_done"), sem("oc_ready"), sem("oct_done")
        mix_ready = sem("mix_ready")

        win_v = [w[0].rearrange("(k p) n -> p k n", p=P) for w in (f1_in, f2_in)]
        wout_v = [w[0].rearrange("(k p) n -> p k n", p=P) for w in (f1_out, f2_out)]
        min_v = m_in[0].rearrange("(k p) n -> p k n", p=P)
        mout_v = m_out[0].rearrange("(k p) n -> p k n", p=P)
        ada_v = ada_w[0].rearrange("(k p) n -> k p n", p=P)

        def cols_of(a):
            return lambda t: proj[:, t, a:a + P]

        TP = [((cols_of(AQ + 2 * P * b), cols_of(AQ + 2 * P * b + P)), qT_a[:, 2 * b:2 * b + 2, :]) for b in range(4)]
        TP += [((lambda t: kdup[:, t, 0, :], lambda t: kdup[:, t, 1, :]), akT[:, 0:2, :])]
        TP += [((cols_of(BQ + 2 * P * b), cols_of(BQ + 2 * P * b + P)), qT_b[:, 2 * b:2 * b + 2, :]) for b in range(2)]
        TP += [((cols_of(BIQ + 2 * P * b), cols_of(BIQ + 2 * P * b + P)), iqT[:, 2 * b:2 * b + 2, :]) for b in range(2)]
        TP += [((lambda t: kdup[:, t, 2, :], lambda t: ckv[:, t, :]), t2[:, 2816:3328].rearrange("p (c n) -> p c n", n=SEQ))]
        TP_AB = len(TP)
        TP += [((cols_of(CQ + 2 * P * b), cols_of(CQ + 2 * P * b + P)), cqT[:, 2 * b:2 * b + 2, :]) for b in range(2)]
        TP += [((cols_of(CK + 2 * P * b), cols_of(CK + 2 * P * b + P)), ckT[:, 2 * b:2 * b + 2, :]) for b in range(2)]

        HEADS = A_HEADS + B_HEADS
        STEPS = HEADS + 7

        def pair_step(q):
            return 2 * q + (5 if q < A_HEADS // 2 else 7)

        slope = [2.0 ** (-8.0 * (i + 1) / A_HEADS) for i in range(A_HEADS)]
        slope += [2.0 ** (-8.0 * (i + 1) / B_HEADS) for i in range(B_HEADS)]

        def ada_after_lo(n, total, a):
            return (a + 1) * total // n - 1

        def ada_after_w(n, total, a):
            return min(a * total // n + 1, total - 1)

        block = ctx.enter_context(nc.Block())

        @block.sync
        def _(sp):
            def load_group(g, src_of, hooks=None, first=0):
                for s in range(4):
                    dst, src = src_of(s)
                    sp.wait_ge(lo_done, 8 * g - 8 + 2 * s + 2)
                    sp.dma_start(dst, src).then_inc(w_landed[s], 16)
                    if hooks:
                        hooks(first + s)

            def in_cols(view, col, width):
                return lambda s: (w_raw[:, s, :, 0:width], view[:, 4 * s:4 * s + 4, bass.ds(col, width)])

            def out_rows(view, chunk, chunks):
                return lambda s: (w_raw[:, s, 0:chunks, :], view[:, bass.ds(chunk, chunks), s * NB:(s + 1) * NB])

            def ada_hook(mods, base, i, weights):
                n = 2 * len(mods)

                def hook(at):
                    for a in range(n):
                        if ada_after_w(n, weights, a) != at:
                            continue
                        kk, m = divmod(a, len(mods))
                        count = base + n * i + a
                        sp.wait_ge(ada_done, count - 1)
                        sp.dma_start(ada_raw[:, a % 2, :],
                                     ada_v[bass.ds(2 * i + kk, 1), :, mods[m][0] * D:(mods[m][0] + 1) * D]
                                     .rearrange("k p n -> p (k n)")).then_inc(ada_landed[a % 2], 16)
                return hook

            def ffn_loads(f):
                g0, win, wout = G_FFN[f], win_v[f], wout_v[f]
                if f == 1:
                    load_group(g0, in_cols(win, 0, NB))
                    load_group(g0 + 1, in_cols(win, DFF, NB))

                def hidden(j, g, width, hooks):
                    load_group(g, in_cols(win, j * NB, width), hooks, 0)
                    load_group(g + 1, in_cols(win, j * NB + DFF, width), hooks, 4)
                    load_group(g + 2, out_rows(wout, (j - 1) * 4, 4), hooks, 8)

                if f == 0:
                    load_group(g0 + 3, in_cols(win, NB + DFF, NB))
                    load_group(g0 + 4, out_rows(wout, 0, 4))
                else:
                    hidden(1, g0 + 2, NB, None)
                    sp.wait_ge(gates_ready, 2)
                with sp.Fori(0, LOOP) as i:
                    hidden(i + 2, g0 + 5 + 3 * i, NB, ada_hook(MODS_FFN[f], ADA_FFN[f], i, 12))
                hidden(FBLOCKS - 1, g0 + 5 + 3 * LOOP, TAIL, None)
                load_group(g0 + 8 + 3 * LOOP, out_rows(wout, (FBLOCKS - 1) * 4, TAIL // P))

            def load_gpost(n, ada_count):
                sp.wait_ge(ada_done, ada_count)
                sp.dma_start(ada_raw[:, 0, :], norm_g[0, 2 * n + 1:2 * n + 2, :].broadcast_to((P, D))).then_inc(gpost_landed, 16)

            sp.dma_start(small_rows[4 * KD:6 * KD, :], ada_b[0, 0:2 * D].rearrange("(k p) -> k p", p=P)).then_inc(c_landed, 16)
            sp.dma_start(small_rows[3 * KD:4 * KD, :], c_in[0].rearrange("(k p) -> k p", p=P)).then_inc(c_landed, 16)
            for n in range(3):
                sp.dma_start(small_rows[n * KD:(n + 1) * KD, :], norm_g[0, 2 * n].rearrange("(k p) -> k p", p=P)).then_inc(c_landed, 16)
            def first_modulation(s):
                for a in range(8):
                    kg, m = divmod(a, 2)
                    count = 8 * s + a
                    need(sp, ada_done, count - 3)
                    sp.dma_start(first_slots[a % 4].rearrange("p (k n) -> p k n", n=NB),
                                 ada_w[0].rearrange("(k p) n -> p k n", p=P)[:, 4 * kg:4 * kg + 4, m * D + s * NB:m * D + (s + 1) * NB]
                                 ).then_inc(ada_landed[a % 4], 16)

            first_modulation(0)
            for s in range(STRIPS):
                if s + 1 < STRIPS:
                    first_modulation(s + 1)
                for b, col in enumerate((0, DFF, NB)):
                    q = OPENING * s + b
                    need(sp, lo_done, 2 * (q - 4) + 2)
                    sp.dma_start(w_raw[:, q % 4], win_v[0][:, 4 * s:4 * s + 4, col:col + NB]).then_inc(w_landed[q % 4], 16)
            ffn_loads(0)
            load_gpost(0, ADA_IN)
            def pair(i, g, hooks):
                load_group(g, in_cols(min_v, 2 * NB * i, NB), hooks, 0)
                load_group(g + 1, in_cols(min_v, 2 * NB * i + NB, NB), hooks, 4)

            def in_hook(i):
                def hook(at):
                    for a in range(8):
                        if ada_after_w(8, 8, a) != at:
                            continue
                        kk, m = divmod(a, 2)
                        sp.wait_ge(ada_done, ADA_IN + 8 * i + a - 1)
                        sp.dma_start(ada_raw[:, a % 2, :],
                                     ada_v[bass.ds(4 * i + kk, 1), :, MODS_IN[m][0] * D:(MODS_IN[m][0] + 1) * D]
                                     .rearrange("k p n -> p (k n)")).then_inc(ada_landed[a % 2], 16)
                return hook

            def first_hook(at):
                if at == 1:
                    sp.wait_ge(gates_ready, 1)
                    sp.wait_ge(modcol_done, 6)
                in_hook(0)(at)

            pair(0, G_IN, first_hook)
            with sp.Fori(1, PBLOCKS // 2) as i:
                pair(i, G_IN + 2 * i, in_hook(i))
            load_group(G_IN + PBLOCKS - 1, in_cols(min_v, (PBLOCKS - 1) * NB, PTAIL))
            sp.wait_ge(lo_done, 8 * G_OUT)
            sp.dma_start(w_uk, uk_in[0].rearrange("r h d -> r (h d)")).then_inc(tab_landed, 16)
            sp.dma_start(w_uv, uv_in[0].rearrange("r h d -> r (h d)")).then_inc(tab_landed, 16)
            sp.wait_ge(s_done, A_HEADS)
            sp.dma_start(decay.rearrange("p h n -> p (h n)"), consts[:, 896:896 + 2048]).then_inc(decay_landed, 16)
            sp.wait_ge(pv_done, HEADS)
            sp.dma_start(rnorm, rn_in[0:1, :].broadcast_to((P, NB))).then_inc(tab_landed, 16)
            sp.wait_ge(s_biased, HEADS)
            sp.wait_ge(uv_done, B_HEADS)
            for g in range(4):
                load_group(G_OUT + g, out_rows(mout_v, 4 * g, 4))
            load_gpost(1, ADA_FFN[1])
            ffn_loads(1)
            load_gpost(2, ADA_FFN[1] + 16)
            for q in range(2 * TILES):
                t, cols = q // 2, slice((q % 2) * D // 2, (q % 2 + 1) * D // 2)
                sp.wait_ge(x_new, 2 * TILES + q + 1)
                sp.dma_start(out[0, t * P:(t + 1) * P, cols], x_sb[:, t, cols]).then_inc(out_landed, 16)
            sp.wait_ge(out_landed, 16 * 2 * TILES)

        @block.gpsimd
        def _(pool):
            nc.gpsimd.memset(ones[:, :], 1.0).then_inc(consts_set, 1)
            nc.gpsimd.memset(neghalf[:, :], -0.5).then_inc(consts_set, 1)
            pool.wait_ge(consts_set, 2)
            count = [0]

            def start_acc(mod, pos):
                nc.gpsimd.memset(acc[:, pos, :], 0.0).then_inc(acc_zero, 1)
                count[0] += 1
                pool.wait_ge(acc_zero, count[0])
                pool.dma_start(acc[0:1, pos, :], ada_b[0:1, mod * D:(mod + 1) * D]).then_inc(bias_landed, 16)
                pool.wait_ge(bias_landed, 16 * count[0])

            powers = [0]

            def power(lo, hi):
                powers[0] += 1
                pool.wait_ge(var_ready, powers[0])
                nc.gpsimd.tensor_tensor(rstd[:, lo:hi], ss[:, lo:hi], neghalf[:, 0:hi - lo], ALU.pow).then_inc(rstd_ready, 1)

            power(2, 4)
            pool.wait_ge(ada_done, ADA_PRE)
            start_acc(4, 3)
            start_acc(5, 0)
            pool.wait_ge(modcol_done, 4)
            start_acc(2, 1)
            pool.wait_ge(xt_lo_done, 8)
            nc.gpsimd.memset(yacc, 0.0).then_inc(yacc_zero, 1)
            start_acc(3, 2)
            power(0, 2)
            pool.wait_ge(y_gated, 4)
            start_acc(6, 1)
            power(2, 4)
            pool.wait_ge(modcol_done, 6)
            start_acc(7, 2)
            power(4, 6)
            pool.wait_ge(ro_done_head, C_HEADS)
            pool.wait_ge(cgate_done, 1)
            nc.gpsimd.memset(yacc, 0.0).then_inc(yacc_zero, 1)
            pool.wait_ge(rvar_ready, 1)
            nc.gpsimd.tensor_tensor(rstat[:, 2, :], rstat[:, 1, :], neghalf[:, 0:16], ALU.pow).then_inc(rrstd_ready, 1)
            start_acc(8, 3)
            power(0, 2)
            power(2, 4)
            pool.wait_ge(x_new, 2 * TILES)
            nc.gpsimd.memset(yacc, 0.0).then_inc(yacc_zero, 1)
            power(0, 2)

        @block.scalar
        def _(act):
            act.dma_start(ident[:, :], consts[:, 0:128]).then_inc(ident_landed, 16)
            act.dma_start(x_sb[:, :, :], x_in[0].rearrange("(t p) d -> p t d", p=P)).then_inc(x_landed, 16)
            act.dma_start(dist_a[:, :], consts[:, 128:512]).then_inc(const_landed, 16)
            act.dma_start(dist_b[:, :], consts[:, 512:896]).then_inc(const_landed, 16)
            act.dma_start(kvg[:, :], kvn_in[0:1, :].broadcast_to((P, KV_RANK))).then_inc(const_landed, 16)
            act.dma_start(sink[:, :], sinks_in[0:1, :].broadcast_to((P, A_HEADS))).then_inc(const_landed, 16)
            act.wait_ge(small_done, 1)
            nc.scalar.activation(gpre[:, :, :], ps_y[:, 0, 0:3 * KD].rearrange("p (n k) -> p n k", k=KD), ACT.Copy)
            nc.scalar.activation(bias1[:, :, :], ps_y[:, 0, 4 * KD:6 * KD].rearrange("p (n k) -> p n k", k=KD), ACT.Copy)
            nc.scalar.activation(cond[:, :], ps_y[:, 0, 3 * KD:4 * KD], ACT.Silu).then_inc(cond_ready, 1)

            chain = [0]

            def link(ins):
                chain[0] += 1
                ins.then_inc(act_chain, 1)
                act.wait_ge(act_chain, chain[0])

            def hi_group(g, chunks, width, hooks=None, units=range(8)):
                for u in units:
                    s, hf = divmod(u, 2)
                    if hf == 0:
                        act.wait_ge(w_landed[s], 16 + 16 * g)
                    n = min(2, chunks - 2 * hf)
                    need(act, pe_used, 8 * g + u - 3)
                    nc.scalar.activation(w_hi[:, u % 4, 0:n, 0:width],
                                         w_raw[:, s, 2 * hf:2 * hf + n, 0:width], ACT.Copy).then_inc(hi_done, 1)
                    for h in (hooks or {}).get(u, ()):
                        h()

            def silu_of(j, g, width):
                def f():
                    act.wait_ge(pe_used, 8 * g + 8)
                    need(act, h_done, j)
                    nc.scalar.activation(silu[:, :, 0:width], ps_g[:, :, 0:width], ACT.Silu).then_inc(silu_done, 1)
                return f

            def ht_hi(j, chunks):
                def f():
                    act.wait_ge(ht_done, j + 1)
                    nc.scalar.activation(hT_hi[:, 0:chunks, :],
                                         ps_t[:, :, :].rearrange("p b (c n) -> p (b c) n", n=SEQ)[:, 0:chunks, :],
                                         ACT.Copy).then_inc(ht_hi_done, 1)
                return f

            def ffn_act(f):
                g0, j0 = G_FFN[f], f * FBLOCKS
                if f == 1:
                    hi_group(g0, 4, NB, xt_hooks(2 * f), range(4, 8))
                    hi_group(g0 + 1, 4, NB, {2: [silu_of(j0, g0, NB)]})

                def hidden(j, g, width):
                    hi_group(g, 4, width)
                    hi_group(g + 1, 4, width, {2: [silu_of(j0 + j, g, width)], 3: [ht_hi(j0 + j - 1, 4)]})
                    hi_group(g + 2, 4, NB)

                if f == 0:
                    def silu_1():
                        act.wait_ge(h_done, 1)
                        act.wait_ge(pe_used, 2 * OPENING * STRIPS)
                        nc.scalar.activation(silu[:, :, :], ps_t[:, :, :], ACT.Silu).then_inc(silu_done, 1)

                    hi_group(g0 + 3, 4, NB, {2: [silu_1], 4: [ht_hi(j0, 4)]})
                    hi_group(g0 + 4, 4, NB)
                else:
                    hidden(1, g0 + 2, NB)
                with act.Fori(0, LOOP) as i:
                    hidden(i + 2, g0 + 5 + 3 * i, NB)
                hidden(FBLOCKS - 1, g0 + 5 + 3 * LOOP, TAIL)
                hi_group(g0 + 8 + 3 * LOOP, TAIL // P, NB, {3: [ht_hi(j0 + FBLOCKS - 1, TAIL // P)]})

            def y_squares(n, y0):
                for b in range(4):
                    act.wait_ge(y_added, y0 + b + 1)
                    if b >= 2:
                        act.wait_ge(ysq_done, 4 * n + b - 1)
                    for t in range(TILES):
                        ins = nc.scalar.activation(junk[:, (2 * b + t) % 4 * NB:((2 * b + t) % 4 + 1) * NB],
                                                   yacc[:, t, b * NB:(b + 1) * NB], ACT.Square, accum_out=ssy[:, t, b:b + 1])
                    ins.then_inc(ysq_done, 1)

            def x_squares(n):
                for t in range(TILES):
                    if n == 0:
                        act.wait_ge(x_landed, 16)
                    else:
                        act.wait_ge(x_new, TILES * (n - 1) + t + 1)
                        act.wait_ge(ysq_done, 4 * n)
                    nc.scalar.activation(junk, x_sb[:, t, :], ACT.Square, accum_out=ss[:, 2 + t:3 + t]).then_inc(xsq_done, 1)
                    act.wait_ge(xsq_done, 2 * n + t + 1)

            def row_scale(n):
                act.wait_ge(rb_done, n + 1)
                nc.scalar.activation(rbc[:, :], ps_y[:, 1, 0:SEQ], ACT.Copy).then_inc(rb_copied, 1)

            def xt_hi(n, b):
                def f():
                    act.wait_ge(xt_scaled, 8 * n + b + 1)
                    for c in range(2):
                        k = 2 * b + c
                        ins = nc.scalar.activation(xT_hi[:, k, :], junk[:, (k % 8) * SEQ:(k % 8 + 1) * SEQ], ACT.Identity,
                                                   bias=modcol[:, n, 1, k:k + 1])
                    ins.then_inc(xt_hi_done, 1)
                return f

            def xt_hooks(n):
                return {4: [xt_hi(n, 3)], 5: [xt_hi(n, 4)], 6: [xt_hi(n, 5)], 7: [xt_hi(n, 6), xt_hi(n, 7)]}

            def into_part(n, g):
                hi_group(g, 4, NB, None, range(4))
                x_squares(n)
                row_scale(n)
                for b in range(3):
                    xt_hi(n, b)()

            for b in range(8):
                act.wait_ge(xt_done, b + 1)
                nc.scalar.activation(xT_raw[:, 2 * b:2 * b + 2, :], banks[b % 6].rearrange("p (c n) -> p c n", n=SEQ), ACT.Copy).then_inc(xt_copied, 1)
                if b == 3:
                    x_squares(0)
            row_scale(0)
            for s in range(STRIPS):
                if s == 0:
                    xt_hi(0, 0)()
                    xt_hi(0, 1)()
                for i in range(2 * OPENING):
                    v = 2 * OPENING * s + i
                    hi_group(v // 8, 4, NB, None, range(v % 8, v % 8 + 1))
                    if s + 1 < STRIPS and i >= 2 * OPENING - 2:
                        xt_hi(0, 2 * s + i - 2)()
            act.wait_ge(pe_used, 2 * (OPENING * (STRIPS - 1) + 1))
            nc.scalar.activation(silu[:, :, :], ps_g[:, :, :], ACT.Silu).then_inc(silu_done, 1)
            ffn_act(0)
            y_squares(0, Y_FFN[0] + 4 * FBLOCKS - 4)
            into_part(1, G_IN)

            def proj_out(b, pairs, width):
                def f():
                    act.wait_ge(pe_used, 8 * (G_IN + b) + 8)
                    nc.scalar.activation(proj[:, :, bass.ds(b * NB, width)], pairs[:, :, 0:width], ACT.Copy).then_inc(proj_done, 1)
                return f

            hi_group(G_IN, 4, NB, xt_hooks(1), range(4, 8))
            hi_group(G_IN + 1, 4, NB, {2: [proj_out(0, ps_g, NB)]})
            with act.Fori(1, PBLOCKS // 2) as i:
                hi_group(G_IN + 2 * i, 4, NB, {2: [proj_out(2 * i - 1, ps_u, NB)]})
                hi_group(G_IN + 2 * i + 1, 4, NB, {2: [proj_out(2 * i, ps_g, NB)]})
            hi_group(G_IN + PBLOCKS - 1, 4, PTAIL, {2: [proj_out(PBLOCKS - 2, ps_u, NB)]})
            proj_out(PBLOCKS - 1, ps_g, PTAIL)()

            act.wait_ge(proj_done, PBLOCKS)
            act.wait_ge(modcol_done, 8)
            for t in range(TILES):
                act.wait_ge(ada_done, ADA_FFN[1])
                nc.scalar.activation(sc[:, t, 0:KV_RANK], proj[:, t, BKV:BKV + KV_RANK], ACT.Square,
                                     accum_out=ss[:, 4 + t:5 + t]).then_inc(ckvsq_done, 1)

            def copy_transposes(b0, b1):
                for b in range(b0, b1):
                    act.wait_ge(tp_done, b + 1)
                    nc.scalar.activation(TP[b][1], ps_y[:, b % 2, :].rearrange("p (c n) -> p c n", n=SEQ), ACT.Copy).then_inc(tp_copied, 1)

            copy_transposes(0, TP_AB)
            act.wait_ge(ukT_done, 1)
            nc.scalar.activation(w_ukT, ps_y[:, 0, :].rearrange("p (c n) -> p c n", n=P), ACT.Copy).then_inc(ukT_copied, 1)
            for h in range(B_HEADS):
                act.wait_ge(ql_done, h + 1)
                nc.scalar.activation(qlatT[:, h, :], ps_y[:, h % 2, 0:SEQ], ACT.Copy).then_inc(ql_copied, 1)

            def pair_hi(q):
                if q < A_HEADS // 2:
                    act.wait_ge(pv_done, 2 * q + 2)
                else:
                    act.wait_ge(uv_done, 2 * q + 2 - A_HEADS)
                nc.scalar.activation(xT_hi[:, q, :], ps_t[:, q % 2, 0:SEQ], ACT.Copy).then_inc(o_hi_done, 1)

            for step in range(STEPS):
                h = step
                if h < HEADS:
                    st = stat[:, h % 2, :]
                    act.wait_ge(s_biased, h + 1)
                    need(act, pt_done, h - 1)
                    nc.scalar.activation(pr[:, h % 2, 0:P], sc[:, h % 2, 0:P], ACT.Exp, bias=st[:, 2:3], scale=HD ** -0.5,
                                         accum_out=st[:, 4:5])
                    if h < A_HEADS:
                        nc.scalar.activation(st[:, 6:8], st[:, 2:4], ACT.Exp, bias=sink[:, h:h + 1])
                    nc.scalar.activation(pr[:, h % 2, P:], sc[:, h % 2, P:], ACT.Exp, bias=st[:, 3:4], scale=HD ** -0.5,
                                         accum_out=st[:, 5:6]).then_inc(e_done, 1)
                h = step - 2
                if 0 <= h < HEADS:
                    act.wait_ge(pt_done, h + 1)
                    need(act, pv_done, h - 1)
                    nc.scalar.activation(pT[:, h % 2, :], ps_u[:, h % 2, 0:3 * P], ACT.Copy).then_inc(pt_copied, 1)
                h = step - 4 - A_HEADS
                if 0 <= h < B_HEADS:
                    act.wait_ge(pv_done, A_HEADS + h + 1)
                    need(act, uv_done, h - 1)
                    nc.scalar.activation(olatT[:, h % 2, :], ps_y[:, h % 2, 0:SEQ], ACT.Copy).then_inc(ol_copied, 1)
                for q in range(HEADS // 2):
                    if step == pair_step(q):
                        pair_hi(q)

            copy_transposes(TP_AB, len(TP))
            nc.scalar.activation(cgate, proj[:, :, CG:CG + NB], ACT.Silu).then_inc(cgate_done, 1)
            hi_group(G_OUT, 4, NB, None, range(4))
            act.wait_ge(ro_done_head, C_HEADS)
            nc.scalar.activation(ro, ps_t[:, :, :], ACT.Copy).then_inc(ro_copied, 1)

            def centred_squares():
                act.wait_ge(cent_ready, 1)
                nc.scalar.activation(csq, cent, ACT.Square).then_inc(csq_done, 1)

            def retention_hi():
                for b in range(2):
                    act.wait_ge(oct_done, b + 1)
                    nc.scalar.activation(xT_hi[:, 12 + 2 * b:14 + 2 * b, :], ps_g[:, b, :].rearrange("p (c n) -> p c n", n=SEQ),
                                         ACT.Copy).then_inc(o_hi_done, 1)

            hi_group(G_OUT, 4, NB, {4: [centred_squares]}, range(4, 8))
            hi_group(G_OUT + 1, 4, NB)
            hi_group(G_OUT + 2, 4, NB, {3: [retention_hi]})
            hi_group(G_OUT + 3, 4, NB)
            y_squares(1, Y_OUT + 12)
            into_part(2, G_FFN[1])
            ffn_act(1)
            y_squares(2, Y_FFN[1] + 4 * FBLOCKS - 4)

        @block.vector
        def _(dve):
            chain = [0]

            def link(ins):
                chain[0] += 1
                ins.then_inc(dve_chain, 1)
                dve.wait_ge(dve_chain, chain[0])

            def lo_group(g, chunks, width, hooks=None, units=range(8)):
                for u in units:
                    s, hf = divmod(u, 2)
                    n = min(2, chunks - 2 * hf)
                    dve.wait_ge(hi_done, 8 * g + u + 1)
                    nc.vector.tensor_tensor(w_lo[:, u % 4, 0:n, 0:width], w_raw[:, s, 2 * hf:2 * hf + n, 0:width],
                                            w_hi[:, u % 4, 0:n, 0:width].bitcast(F32), ALU.subtract).then_inc(lo_done, 1)
                    for h in (hooks or {}).get(u, ()):
                        h()

            def ada_unit(raw, landed, count, k, pos, done):
                def f():
                    dve.wait_ge(landed[0], landed[1])
                    dve.wait_ge(ada_done, done)
                    nc.vector.scalar_tensor_tensor(acc[:, pos, :], raw, cond[:, bass.ds(k, 1)], acc[:, pos, :],
                                                   ALU.mult, ALU.add).then_inc(ada_done, 1)
                return f

            def ada_hooks(mods, base, i, units, k0, hooks):
                n = 8 if units == 16 else 2 * len(mods)
                for a in range(n):
                    kk, m = divmod(a, len(mods))
                    count = base + n * i + a
                    use = (base - ADA_PRE) // 2 + (n // 2) * i + a // 2
                    unit = ada_unit(ada_raw[:, a % 2, :], (ada_landed[a % 2], 16 * (PRE_USES + use) + 16), count, k0 + kk, mods[m][1], count)
                    hooks.setdefault(ada_after_lo(n, units, a), []).append(unit)
                return hooks

            def y_add(g, idx, n):
                ps = ps_t if n % 2 else ps_y

                def f():
                    dve.wait_ge(pe_used, 8 * g + 2 * n + 2)
                    need(dve, y_added, idx)
                    cols = yacc[:, :, n * NB:(n + 1) * NB]
                    nc.vector.tensor_tensor(cols, ps[:, :, :], cols, ALU.add).then_inc(y_added, 1)
                return f

            def h_mul(j, g, width, used=None):
                def f():
                    dve.wait_ge(silu_done, j + 1)
                    dve.wait_ge(pe_used, 8 * g + 8 if used is None else used)
                    need(dve, ht_done, j)
                    nc.vector.tensor_tensor(hbuf[:, :, 0:width], ps_u[:, :, 0:width], silu[:, :, 0:width],
                                            ALU.mult).then_inc(h_done, 1)
                return f

            def ht_lo(j, chunks):
                def f():
                    dve.wait_ge(ht_hi_done, j + 1)
                    nc.vector.tensor_tensor(hT_lo[:, 0:chunks, :],
                                            ps_t[:, :, :].rearrange("p b (c n) -> p (b c) n", n=SEQ)[:, 0:chunks, :],
                                            hT_hi[:, 0:chunks, :].bitcast(F32), ALU.subtract).then_inc(ht_lo_done, 1)
                return f

            def mod_cols(n, which, pairs):
                def f():
                    for b, ps in enumerate(pairs):
                        dve.wait_ge(cols_done, 4 * n + 2 * which + b + 1)
                        picked = ada_raw[:, 1, b * 1024:(b + 1) * 1024].rearrange("p (k q) -> p k q", q=P)
                        link(nc.vector.tensor_tensor(picked, ps[:, :, :].rearrange("p b (k q) -> p (b k) q", q=P),
                                                     ident[:, :].unsqueeze(1).broadcast_to((P, 8, P)), ALU.mult))
                        ins = nc.vector.reduce_sum(modcol[:, n, 1 - which, 8 * b:8 * b + 8], picked, AX_X)
                        if b == 0 or which == 1:
                            link(ins)
                    if which == 1:
                        ins = nc.vector.scalar_tensor_tensor(modcol[:, n, 0, :], modcol[:, n, 0, :], 1.0, gpre[:, n, :], ALU.add, ALU.mult)
                    ins.then_inc(modcol_done, 1)
                return f

            def gates(n, pos, weight):
                def f():
                    dve.wait_ge(gpost_landed, 16 * n + 16)
                    dve.wait_ge(gbc_done, n + 1)
                    for b, ps in enumerate((ps_g, ps_u)):
                        part = slice(2 * b * NB, 2 * (b + 1) * NB)
                        last = nc.vector.scalar_tensor_tensor(
                            acc[:, pos, part], ps[:, :, :].rearrange("p b n -> p (b n)"), weight, ada_raw[:, 0, part],
                            ALU.mult, ALU.mult)
                    last.then_inc(gates_ready, 1)
                return f

            def ffn_dve(f):
                g0, j0, y0 = G_FFN[f], f * FBLOCKS, Y_FFN[f]
                if f == 1:
                    lo_group(g0, 4, NB, xt_hooks(2 * f), range(4, 8))
                    lo_group(g0 + 1, 4, NB)

                def hidden(j, g, width, hooks):
                    parts = [{}, {}, {}]
                    for at, work_ in hooks.items():
                        parts[at // 8].setdefault(at % 8, []).extend(work_)
                    parts[0].setdefault(0, []).append(y_add(g - 1, y0 + 4 * (j - 2) + 2, 2))
                    parts[0].setdefault(2, []).append(y_add(g - 1, y0 + 4 * (j - 2) + 3, 3))
                    parts[1].setdefault(4, []).append(ht_lo(j0 + j - 1, 4))
                    parts[2].setdefault(2, []).append(h_mul(j0 + j, g + 1, width))
                    parts[2].setdefault(4, []).append(y_add(g + 2, y0 + 4 * (j - 1), 0))
                    parts[2].setdefault(6, []).append(y_add(g + 2, y0 + 4 * (j - 1) + 1, 1))
                    lo_group(g, 4, width, parts[0])
                    lo_group(g + 1, 4, width, parts[1])
                    lo_group(g + 2, 4, NB, parts[2])

                if f == 1:
                    lo_group(g0 + 2, 4, NB, {2: [h_mul(j0, g0 + 1, NB)]})
                hooks = {5 - f: [ht_lo(j0, 4)]}
                if f == 0:
                    hooks[0] = [h_mul(0, 0, NB, 2 * (OPENING * (STRIPS - 1) + 2))]
                lo_group(g0 + 3, 4, NB, hooks)
                lo_group(g0 + 4, 4, NB, {2: [h_mul(j0 + 1, g0 + 3, NB)], 3: [lambda: dve.wait_ge(yacc_zero, 1 + 2 * f)], 4: [y_add(g0 + 4, y0, 0)], 6: [y_add(g0 + 4, y0 + 1, 1)]})
                dve.wait_ge(bias_landed, 16 * (4 if f == 0 else 7))
                with dve.Fori(0, LOOP) as i:
                    hidden(i + 2, g0 + 5 + 3 * i, NB, ada_hooks(MODS_FFN[f], ADA_FFN[f], i, 24, 2 * i, {}))
                last = FBLOCKS - 1
                hidden(last, g0 + 5 + 3 * LOOP, TAIL, {})
                yl, gy = y0 + 4 * last, g0 + 8 + 3 * LOOP
                tail = {0: [y_add(gy - 1, yl - 2, 2)], 2: [y_add(gy - 1, yl - 1, 3)], 3: [ht_lo(j0 + last, TAIL // P)],
                        4: [gates(2 * f, 1 if f == 0 else 3, 0.5)], 5: [y_add(gy, yl, 0)], 7: [y_add(gy, yl + 1, 1)]}
                if f == 0:
                    tail[3] += tail.pop(4)
                    tail[5].append(mod_cols(1, 0, (ps_g, ps_u)))
                    tail[6] = tail[7]
                    tail[7] = [mod_cols(1, 1, (ps_g, ps_u))]
                lo_group(gy, TAIL // P, NB, tail)

            norms = [0]

            def norm_scale(col, width, meanwhile=None):
                nc.vector.tensor_scalar(ss[:, col:col + 2], ss[:, col:col + 2], 1.0 / width, EPS, ALU.mult, ALU.add).then_inc(var_ready, 1)
                norms[0] += 1
                if meanwhile:
                    meanwhile()
                dve.wait_ge(rstd_ready, norms[0])

            def residual(n, pos, g, y0):
                def gated(b):
                    dve.wait_ge(ysq_done, 4 * n + b + 1)
                    cols = slice(b * NB, (b + 1) * NB)
                    nc.vector.tensor_tensor(yacc[:, :, cols], yacc[:, :, cols],
                                            acc[:, pos, cols].unsqueeze(1).broadcast_to((P, TILES, NB)), ALU.mult).then_inc(y_gated, 1)

                y_add(g, y0 + 2, 2)()
                gated(0)
                gated(1)
                gated(2)
                y_add(g, y0 + 3, 3)()
                dve.wait_ge(ysq_done, 4 * n + 4)
                link(nc.vector.reduce_sum(ss[:, 0:2], ssy[:, :, :], AX_X))
                nc.vector.tensor_scalar(ss[:, 0:2], ss[:, 0:2], 1.0 / D, EPS, ALU.mult, ALU.add).then_inc(var_ready, 1)
                norms[0] += 1
                gated(3)
                dve.wait_ge(rstd_ready, norms[0])
                dve.wait_ge(y_gated, 4 * n + 4)
                parts = 1 if n < 2 else 2
                for t in range(TILES):
                    for part in range(parts):
                        cols = slice(part * D // parts, (part + 1) * D // parts)
                        nc.vector.scalar_tensor_tensor(x_sb[:, t, cols], yacc[:, t, cols], rstd[:, t:t + 1], x_sb[:, t, cols],
                                                       ALU.mult, ALU.add).then_inc(x_new, 1)

            def input_scale(n, meanwhile=None):
                dve.wait_ge(xsq_done, 2 * n + 2)
                norm_scale(2, D, meanwhile)
                for t in range(TILES):
                    last = nc.vector.tensor_scalar(diag[:, t, :], ident[:, :], rstd[:, 2 + t:3 + t], None, ALU.mult)
                last.then_inc(diag_ready, 1)

            def xt_scale(n, b):
                def f():
                    if b == 0:
                        dve.wait_ge(rb_copied, n + 1)
                    dve.wait_ge(modcol_done, b // 2 + 1 if n == 0 else 2 * n + 4)
                    dve.wait_ge(xt_done, 8 * n + b + 1)
                    need(dve, xt_lo_done, 8 * n + b - 3 if b >= 4 else 0)
                    for c in range(2):
                        k = 2 * b + c
                        xT = xT_raw[:, k, :] if n == 0 else banks[b][:, c * SEQ:(c + 1) * SEQ]
                        last = nc.vector.scalar_tensor_tensor(junk[:, (k % 8) * SEQ:(k % 8 + 1) * SEQ], xT,
                                                              modcol[:, n, 0, k:k + 1], rbc[:, :], ALU.mult, ALU.mult)
                    last.then_inc(xt_scaled, 1)
                return f

            def xt_lo(n, b):
                def f():
                    dve.wait_ge(xt_hi_done, 8 * n + b + 1)
                    dve.wait_ge(xt_scaled, 8 * n + b + 1)
                    for c in range(2):
                        k = 2 * b + c
                        last = nc.vector.scalar_tensor_tensor(xT_lo[:, k, :], junk[:, (k % 8) * SEQ:(k % 8 + 1) * SEQ], modcol[:, n, 1, k:k + 1],
                                                              xT_hi[:, k, :].bitcast(F32), ALU.add, ALU.subtract)
                    last.then_inc(xt_lo_done, 1)
                return f

            def xt_hooks(n):
                return {4: [xt_scale(n, 4), xt_lo(n, 3)], 5: [xt_scale(n, 5), xt_lo(n, 4)], 6: [xt_scale(n, 6), xt_lo(n, 5)],
                        7: [xt_scale(n, 7), xt_lo(n, 6), xt_lo(n, 7)]}

            def into_part(n, g):
                lo_group(g, 4, NB, None, range(2))
                input_scale(n, lambda: lo_group(g, 4, NB, None, range(2, 3)))
                lo_group(g, 4, NB, None, range(3, 4))
                for b in range(3):
                    xt_scale(n, b)()
                    if b:
                        xt_lo(n, b - 1)()
                xt_scale(n, 3)()
                xt_lo(n, 2)()


            dve.wait_ge(cond_ready, 1)
            dve.wait_ge(const_landed, 16 * 4)
            dve.wait_ge(ident_landed, 16)
            nc.vector.tensor_scalar(negsink[:, :], sink[:, :], -1.0, None, ALU.mult)

            def first_ada(s, kg):
                before = chain[0]
                for i in range(8):
                    k, m = divmod(i, 2)
                    count = 8 * s + 2 * kg + m
                    slot = (2 * kg + m) % 4
                    if k == 0:
                        dve.wait_ge(ada_landed[slot], 16 * (count // 4) + 16)
                        if kg:
                            dve.wait_ge(ada_done, count - 1)
                    else:
                        dve.wait_ge(dve_chain, before + i - 1)
                    part = acc[:, MODS_PRE[m][1], s * NB:(s + 1) * NB]
                    raw, weight = first_slots[slot][:, k * NB:(k + 1) * NB], cond[:, 4 * kg + k:4 * kg + k + 1]
                    if kg == 0 and k == 0:
                        ins = nc.vector.tensor_scalar(part, raw, weight, None, ALU.mult)
                    else:
                        ins = nc.vector.scalar_tensor_tensor(part, raw, weight, part, ALU.mult, ALU.add)
                    if k == 3:
                        ins.then_inc(ada_done, 1)
                    else:
                        ins.then_inc(dve_chain, 1)
                        chain[0] += 1

            def first_cols(s):
                dve.wait_ge(cols_done, s + 1)
                cols = slice(4 * s, 4 * s + 4)
                sums = ps_y[:, 0, 0:2 * KD].rearrange("p (n k) -> p n k", k=KD)[:, :, cols]
                link(nc.vector.tensor_tensor(bias1[:, :, cols], sums, bias1[:, :, cols], ALU.add))
                nc.vector.tensor_copy(modcol[:, 0, 1, cols], bias1[:, 0, cols])
                nc.vector.scalar_tensor_tensor(modcol[:, 0, 0, cols], bias1[:, 1, cols], 1.0, gpre[:, 0, cols],
                                               ALU.add, ALU.mult).then_inc(modcol_done, 1)

            def first_lo(v):
                lo_group(v // 8, 4, NB, None, range(v % 8, v % 8 + 1))

            def first_chunks(s):
                first_cols(s)
                xt_scale(0, 2 * s)()
                xt_scale(0, 2 * s + 1)()
                xt_lo(0, 2 * s)()

            for kg in range(4):
                first_ada(0, kg)
            input_scale(0)
            for kg in range(4):
                first_ada(1, kg)
            first_chunks(0)
            xt_lo(0, 1)()
            for s in range(STRIPS):
                for i in range(2 * OPENING):
                    first_lo(2 * OPENING * s + i)
                    if s + 2 < STRIPS and i < 4:
                        first_ada(s + 2, i)
                    if s + 1 < STRIPS and i == 4:
                        first_chunks(s + 1)
                    if s + 1 < STRIPS and i == 5:
                        xt_lo(0, 2 * s + 3)()
            ffn_dve(0)
            residual(0, 1, G_IN - 1, Y_OUT - 4)
            into_part(1, G_IN)

            dve.wait_ge(bias_landed, 16 * 6)

            def in_pair(i):
                hooks = ada_hooks(MODS_IN, ADA_IN, i, 16, 4 * i, {})
                first = {k: h for k, h in hooks.items() if k < 8}
                if isinstance(i, int):
                    for k, h in xt_hooks(1).items():
                        first.setdefault(k, []).extend(h)
                lo_group(G_IN + 2 * i, 4, NB, first, range(4 if isinstance(i, int) else 0, 8))
                lo_group(G_IN + 2 * i + 1, 4, NB, {k - 8: h for k, h in hooks.items() if k >= 8})

            early = ada_hooks(MODS_IN, ADA_IN, 0, 16, 0, {})
            for k in range(4):
                for h in early.get(k, ()):
                    h()
            in_pair(0)
            with dve.Fori(1, PBLOCKS // 2) as i:
                in_pair(i)
            lo_group(G_IN + PBLOCKS - 1, 4, PTAIL, {2: [mod_cols(2, 0, (ps_t, ps_y))], 7: [mod_cols(2, 1, (ps_t, ps_y))]})

            dve.wait_ge(proj_done, PBLOCKS)
            for n_, a in enumerate((AK, AK + HD, BIK)):
                for dup in range(2):
                    last = nc.vector.tensor_copy(kdup[:, :, n_, dup * HD:(dup + 1) * HD], proj[:, :, a:a + HD])
            last.then_inc(kdup_done, 1)
            nc.vector.tensor_scalar(iws[:, :, :], proj[:, :, BIW:BIW + B_HEADS], B_HEADS ** -0.5, None, ALU.mult)
            dve.wait_ge(ckvsq_done, 2)
            norm_scale(4, KV_RANK)
            for t in range(TILES):
                last = nc.vector.scalar_tensor_tensor(ckv[:, t, :], proj[:, t, BKV:BKV + KV_RANK], rstd[:, 4 + t:5 + t],
                                                      kvg[:, :], ALU.mult, ALU.mult)
            last.then_inc(kdup_done, 1)

            link(nc.vector.tensor_scalar(score, dist_b[:, :], 0.1 * BIG, -1e37, ALU.is_ge, ALU.mult))
            for h in range(B_HEADS):
                dve.wait_ge(lg_done, h + 1)
                nc.vector.tensor_scalar(rw[:, 0:P], ps_g[:, h % 2, 0:P], 0.0, iws[:, 0, h:h + 1], ALU.max, ALU.mult)
                last = nc.vector.tensor_scalar(rw[:, P:3 * P], ps_g[:, h % 2, P:3 * P], 0.0, iws[:, 1, h:h + 1], ALU.max, ALU.mult)
                last.then_inc(lg_used, 1)
                dve.wait_ge(lg_used, h + 1)
                if h == 0:
                    link(nc.vector.tensor_copy(pick, rw))
                else:
                    link(nc.vector.tensor_tensor(pick, pick, rw, ALU.add))
            link(nc.vector.tensor_tensor(pick, pick, score, ALU.add))

            def top_round():
                for t in range(TILES):
                    keys = slice(0, P) if t == 0 else slice(P, 3 * P)
                    last = nc.vector.max(top8[:, t, :], pick[:, keys])
                link(last)
                for t in range(TILES):
                    keys = slice(0, P) if t == 0 else slice(P, 3 * P)
                    last = nc.vector.match_replace(pick[:, keys], top8[:, t, :], pick[:, keys], -3e38)
                link(last)

            def selected_distances():
                link(nc.vector.tensor_scalar(dist_sel, pick, -2e38, BIG, ALU.is_ge, ALU.mult))
                link(nc.vector.tensor_tensor(dist_sel, dist_sel, dist_b[:, :], ALU.max))

            side_work = {s: top_round for s in range(TOPK // 8)}
            side_work[TOPK // 8] = selected_distances

            def pair_lo(q):
                dve.wait_ge(o_hi_done, q + 1)
                nc.vector.tensor_tensor(xT_lo[:, q, :], ps_t[:, q % 2, 0:SEQ], xT_hi[:, q, :].bitcast(F32), ALU.subtract).then_inc(o_lo_done, 1)

            for step in range(STEPS):
                h = step
                if h < HEADS:
                    st = stat[:, h % 2, :]
                    dist = dist_a[:, :] if h < A_HEADS else dist_sel
                    dve.wait_ge(s_done, h + 1)
                    need(dve, e_done, h - 1)
                    link(nc.vector.scalar_tensor_tensor(sc[:, h % 2, :], dist, -slope[h] * HD ** 0.5, ps_g[:, h % 2, 0:3 * P],
                                                        ALU.mult, ALU.add))
                    nc.vector.reduce_max(st[:, 0:1], sc[:, h % 2, 0:P], AX_X)
                    link(nc.vector.reduce_max(st[:, 1:2], sc[:, h % 2, P:3 * P], AX_X))
                    if h < A_HEADS:
                        nc.vector.tensor_scalar(st[:, 2:4], st[:, 0:2], -HD ** -0.5, negsink[:, h:h + 1], ALU.mult, ALU.min).then_inc(s_biased, 1)
                    else:
                        nc.vector.tensor_scalar(st[:, 2:4], st[:, 0:2], -HD ** -0.5, None, ALU.mult).then_inc(s_biased, 1)
                h = step - 1
                if 0 <= h < HEADS:
                    st = stat[:, h % 2, :]
                    dve.wait_ge(e_done, h + 1)
                    if h < A_HEADS:
                        link(nc.vector.tensor_tensor(st[:, 4:6], st[:, 4:6], st[:, 6:8], ALU.add))
                    link(nc.vector.reciprocal(st[:, 8:10], st[:, 4:6]))
                    nc.vector.tensor_scalar(pr[:, h % 2, 0:P], pr[:, h % 2, 0:P], st[:, 8:9], None, ALU.mult)
                    nc.vector.tensor_scalar(pr[:, h % 2, P:], pr[:, h % 2, P:], st[:, 9:10], None, ALU.mult).then_inc(p_ready, 1)
                for q in range(HEADS // 2):
                    if step == pair_step(q):
                        pair_lo(q)
                if step in side_work:
                    side_work[step]()

            dve.wait_ge(decay_landed, 16)
            for h in range(C_HEADS):
                dve.wait_ge(r_done, h + 1)
                need(dve, ro_done_head, h - 1)
                nc.vector.tensor_tensor(sc[:, h % 2, 0:SEQ], ps_g[:, h % 2, 0:SEQ], decay[:, h, :], ALU.mult)
                nc.vector.tensor_tensor(sc[:, h % 2, SEQ:3 * P], ps_g[:, h % 2, SEQ:3 * P], decay[:, h, 0:P], ALU.mult).then_inc(r_decayed, 1)
                if h >= C_HEADS - 4:
                    lo_group(G_OUT, 4, NB, None, range(h - (C_HEADS - 4), h - (C_HEADS - 4) + 1))
            dve.wait_ge(r_decayed, C_HEADS)
            dve.wait_ge(ro_copied, 1)

            ro_h = ro.rearrange("p t (h d) -> p (t h) d", d=HD)
            cent_h = cent.rearrange("p t (h d) -> p (t h) d", d=HD)
            link(nc.vector.reduce_sum(rstat[:, 0, :], ro_h, AX_X))
            link(nc.vector.tensor_scalar(rstat[:, 0, :], rstat[:, 0, :], 1.0 / HD, None, ALU.mult))
            nc.vector.tensor_tensor(cent_h, ro_h, rstat[:, 0, :].unsqueeze(2).broadcast_to((P, 16, HD)), ALU.subtract).then_inc(cent_ready, 1)

            def retention_variance():
                dve.wait_ge(csq_done, 1)
                link(nc.vector.reduce_sum(rstat[:, 1, :], csq.rearrange("p t (h d) -> p (t h) d", d=HD), AX_X))
                nc.vector.tensor_scalar(rstat[:, 1, :], rstat[:, 1, :], 1.0 / HD, EPS, ALU.mult, ALU.add).then_inc(rvar_ready, 1)

            def retention_out():
                dve.wait_ge(tab_landed, 16 * 3)
                dve.wait_ge(rrstd_ready, 1)
                link(nc.vector.tensor_tensor(cent_h, cent_h, rstat[:, 2, :].unsqueeze(2).broadcast_to((P, 16, HD)), ALU.mult))
                for t in range(TILES):
                    last = nc.vector.tensor_tensor(cent[:, t, :], cent[:, t, :], rnorm, ALU.mult)
                link(last)
                dve.wait_ge(cgate_done, 1)
                nc.vector.tensor_tensor(cent, cent, cgate, ALU.mult).then_inc(oc_ready, 1)

            def retention_lo():
                for b in range(2):
                    dve.wait_ge(o_hi_done, HEADS // 2 + b + 1)
                    last = nc.vector.tensor_tensor(xT_lo[:, 12 + 2 * b:14 + 2 * b, :], ps_g[:, b, :].rearrange("p (c n) -> p c n", n=SEQ),
                                                   xT_hi[:, 12 + 2 * b:14 + 2 * b, :].bitcast(F32), ALU.subtract)
                last.then_inc(mix_ready, 1)

            for g in range(4):
                y0 = Y_OUT + 4 * g
                hooks = {5: [y_add(G_OUT + g, y0, 0)], 7: [y_add(G_OUT + g, y0 + 1, 1)]}
                if g:
                    hooks[0] = [y_add(G_OUT + g - 1, y0 - 2, 2)]
                    hooks[2] = [y_add(G_OUT + g - 1, y0 - 1, 3)]
                else:
                    hooks[4] = [retention_variance, lambda: dve.wait_ge(yacc_zero, 2)]
                    hooks[6] = [retention_out]
                if g == 2:
                    hooks[4] = [retention_lo]
                if g == 3:
                    hooks[4] = [gates(1, 0, 1.0)]
                lo_group(G_OUT + g, 4, NB, hooks, range(0 if g else 4, 8))
            residual(1, 0, G_OUT + 3, Y_OUT + 12)
            into_part(2, G_FFN[1])
            ffn_dve(1)
            residual(2, 3, G_FFN[1] + FFN_GROUPS - 1, Y_FFN[1] + 4 * FBLOCKS - 4)

        @block.tensor
        def _(pe):
            def unit(a_hi, a_lo, chunk0, b, n, width, out_of, first, last_unit):
                for t in range(TILES):
                    rows = slice(t * P, (t + 1) * P)
                    for c in range(n):
                        k = chunk0 + c
                        start, stop = first and c == 0, last_unit and c == n - 1
                        o = out_of(t)
                        nc.tensor.matmul(o, a_hi[:, k, rows], w_hi[:, b, c, 0:width], start=start, stop=False)
                        nc.tensor.matmul(o, a_hi[:, k, rows], w_lo[:, b, c, 0:width], start=False, stop=False)
                        ins = nc.tensor.matmul(o, a_lo[:, k, rows], w_hi[:, b, c, 0:width], start=False, stop=stop)
                return ins

            def in_group(g, width, ps, part=None, hooks=None):
                if part is not None:
                    pe.wait_ge(xt_scaled, 8 * part + 2)
                for u in range(8):
                    pe.wait_ge(lo_done, 8 * g + u + 1)
                    if part is not None:
                        pe.wait_ge(xt_lo_done, 8 * part + u + 1)
                    unit(xT_hi, xT_lo, 2 * u, u % 4, 2, width, lambda t: ps[:, t, 0:width], u == 0, u == 7).then_inc(pe_used, 1)
                    for h in (hooks or {}).get(u, ()):
                        h()

            def out_group(g, a_hi, a_lo, chunk0, chunks, y0, blocks=range(4)):
                for n in blocks:
                    ps = ps_t if n % 2 else ps_y
                    need(pe, y_added, y0 + n - 1)
                    for hf in range(2):
                        m = min(2, chunks - 2 * hf)
                        pe.wait_ge(lo_done, 8 * g + 2 * n + hf + 1)
                        ins = unit(a_hi, a_lo, chunk0 + 2 * hf, (2 * n + hf) % 4, m, NB, lambda t: ps[:, t, :], hf == 0, hf == 1)
                        ins.then_inc(pe_used, 1)

            def transpose_h(j, chunks, y_before):
                pe.wait_ge(h_done, j + 1)
                need(pe, y_added, y_before)
                for c in range(chunks):
                    for t in range(TILES):
                        col = (c % 2) * SEQ + t * P
                        ins = nc.tensor.transpose(ps_t[:, c // 2, col:col + P], hbuf[:, t, c * P:(c + 1) * P], ident[:, :])
                ins.then_inc(ht_done, 1)

            def mod_rows(pos, pairs, free, count):
                pe.wait_ge(ada_done, count)
                for b, ps in enumerate(pairs):
                    pe.wait_ge(*free[b])
                    for n in range(2):
                        col = (2 * b + n) * NB
                        ins = nc.tensor.matmul(ps[:, n, :], ones[:, :], acc[:, pos, col:col + NB], start=True, stop=True)
                    ins.then_inc(cols_done, 1)

            def gate_rows(pos, count):
                pe.wait_ge(ada_done, count)
                for n in range(4):
                    ps = (ps_g, ps_u)[n // 2]
                    ins = nc.tensor.matmul(ps[:, n % 2, :], ones[:, :], acc[:, pos, n * NB:(n + 1) * NB], start=True, stop=True)
                ins.then_inc(gbc_done, 1)


            def x_transposes(b, t):
                for c in range(2):
                    k = 2 * b + c
                    ins = nc.tensor.transpose(banks[b][:, c * SEQ + t * P:c * SEQ + (t + 1) * P],
                                              x_sb[:, t, k * P:(k + 1) * P], ident[:, :])
                return ins

            def row_scale(n):
                pe.wait_ge(diag_ready, n + 1)
                for t in range(TILES):
                    ins = nc.tensor.matmul(ps_y[:, 1, t * P:(t + 1) * P], ones[:, :], diag[:, t, :], start=True, stop=True)
                ins.then_inc(rb_done, 1)
                pe.wait_ge(rb_copied, n + 1)

            def transpose_x(n):
                for t in range(TILES):
                    pe.wait_ge(x_new, TILES * (n - 1) + t + 1)
                    for b in range(7):
                        ins = x_transposes(b, t)
                        if t == 1:
                            ins.then_inc(xt_done, 1)
                row_scale(n)
                x_transposes(7, 0)
                x_transposes(7, 1).then_inc(xt_done, 1)

            def ffn_pe(f):
                g0, j0, y0 = G_FFN[f], f * FBLOCKS, Y_FFN[f]
                if f == 1:
                    in_group(g0, NB, ps_g, 2 * f)
                    in_group(g0 + 1, NB, ps_u)

                def hidden(j, g, width):
                    need(pe, silu_done, j0 + j)
                    in_group(g, width, ps_g)
                    transpose_h(j0 + j - 1, 4, y0 + 4 * (j - 1))
                    need(pe, h_done, j0 + j)
                    in_group(g + 1, width, ps_u)
                    pe.wait_ge(ht_lo_done, j0 + j)
                    out_group(g + 2, hT_hi, hT_lo, 0, 4, y0 + 4 * (j - 1))

                if f == 0:
                    pe.wait_ge(h_done, 1)

                    def first_transpose():
                        pe.wait_ge(silu_done, 2)
                        transpose_h(0, 4, 0)

                    in_group(g0 + 3, NB, ps_u, None, {2: [first_transpose]})
                    pe.wait_ge(ht_lo_done, 1)
                    out_group(g0 + 4, hT_hi, hT_lo, 0, 4, y0)
                else:
                    hidden(1, g0 + 2, NB)
                with pe.Fori(0, LOOP) as i:
                    hidden(i + 2, g0 + 5 + 3 * i, NB)
                last = FBLOCKS - 1
                hidden(last, g0 + 5 + 3 * LOOP, TAIL)
                gate_rows(1 if f == 0 else 3, ADA_IN if f == 0 else ADA_FFN[1] + 16)
                transpose_h(j0 + last, TAIL // P, y0 + 4 * last)
                pe.wait_ge(ht_lo_done, j0 + FBLOCKS)
                g, yl = g0 + 8 + 3 * LOOP, y0 + 4 * last
                if f == 0:
                    out_group(g, hT_hi, hT_lo, 0, TAIL // P, yl, range(0, 1))
                    mod_rows(3 - 1, (ps_g, ps_u), ((gates_ready, 1), (gates_ready, 1)), ADA_IN)
                    out_group(g, hT_hi, hT_lo, 0, TAIL // P, yl, range(1, 2))
                    mod_rows(3, (ps_g, ps_u), ((modcol_done, 5), (modcol_done, 5)), ADA_IN)
                    out_group(g, hT_hi, hT_lo, 0, TAIL // P, yl, range(2, 4))
                else:
                    out_group(g, hT_hi, hT_lo, 0, TAIL // P, yl)

            pe.wait_ge(ident_landed, 16)
            pe.wait_ge(c_landed, 16 * 5)
            nc.tensor.transpose(ps_y[:, 0, 0:6 * KD], small_rows[:, :], ident[0:6 * KD, 0:6 * KD]).then_inc(small_done, 1)
            pe.wait_ge(x_landed, 16)
            for b in range(8):
                need(pe, xt_copied, b - 5)
                for c in range(2):
                    for t in range(TILES):
                        k = 2 * b + c
                        ins = nc.tensor.transpose(banks[b % 6][:, c * SEQ + t * P:c * SEQ + (t + 1) * P],
                                                  x_sb[:, t, k * P:(k + 1) * P], ident[:, :])
                ins.then_inc(xt_done, 1)
            pe.wait_ge(consts_set, 1)
            row_scale(0)
            pe.wait_ge(cond_ready, 1)
            pe.wait_ge(xt_copied, 8)
            def first_sums(s):
                pe.wait_ge(ada_done, 8 * s + 8)
                need(pe, modcol_done, s)
                for m in range(2):
                    for k in range(4 * s, 4 * s + 4):
                        ins = nc.tensor.matmul(ps_y[:, 0, m * KD + k:m * KD + k + 1], acc[:, MODS_PRE[m][1], k * P:(k + 1) * P],
                                               ones[:, 0:1], start=True, stop=True)
                ins.then_inc(cols_done, 1)

            first_sums(0)
            for s in range(STRIPS):
                for b, ps in enumerate((ps_g, ps_u, ps_t)):
                    for hf in range(2):
                        if b == 0 and hf == 0 and s + 1 < STRIPS:
                            first_sums(s + 1)
                        v = 2 * (OPENING * s + b) + hf
                        pe.wait_ge(lo_done, v + 1)
                        pe.wait_ge(xt_lo_done, 2 * s + hf + 1)
                        unit(xT_hi, xT_lo, 4 * s + 2 * hf, v % 4, 2, NB, lambda t: ps[:, t, :], s == 0 and hf == 0,
                             s == STRIPS - 1 and hf == 1).then_inc(pe_used, 1)
            ffn_pe(0)
            transpose_x(1)

            in_group(G_IN, NB, ps_g, 1)
            in_group(G_IN + 1, NB, ps_u)
            with pe.Fori(1, PBLOCKS // 2) as i:
                pe.wait_ge(proj_done, 2 * i - 1)
                in_group(G_IN + 2 * i, NB, ps_g)
                pe.wait_ge(proj_done, 2 * i)
                in_group(G_IN + 2 * i + 1, NB, ps_u)
            pe.wait_ge(proj_done, PBLOCKS - 2)
            in_group(G_IN + PBLOCKS - 1, PTAIL, ps_g, None,
                     {0: [lambda: mod_rows(1, (ps_t, ps_y), ((xt_scaled, 16), (xt_scaled, 16)), ADA_FFN[1])],
                      3: [lambda: mod_rows(2, (ps_t, ps_y), ((modcol_done, 7), (modcol_done, 7)), ADA_FFN[1])]})
            pe.wait_ge(modcol_done, 8)

            def transposes(b0, b1):
                for b in range(b0, b1):
                    need(pe, tp_copied, b - 1)
                    if b == 4:
                        pe.wait_ge(kdup_done, 1)
                    if b == TP_AB - 1:
                        pe.wait_ge(kdup_done, 2)
                    for c in range(2):
                        for t in range(TILES):
                            col = c * SEQ + t * P
                            ins = nc.tensor.transpose(ps_y[:, b % 2, col:col + P], TP[b][0][c](t), ident[:, :])
                    ins.then_inc(tp_done, 1)

            pe.wait_ge(proj_done, PBLOCKS)
            transposes(0, TP_AB)
            def two_tiles(bank, q_of, keys):
                nc.tensor.matmul(bank[:, 0:P], q_of(0), keys[:, 0:P], start=True, stop=True)
                return nc.tensor.matmul(bank[:, P:3 * P], q_of(1), keys, start=True, stop=True)

            def index_logits(h):
                rows = slice((h % 2) * HD, (h % 2 + 1) * HD)
                need(pe, lg_used, h - 1)
                two_tiles(ps_g[:, h % 2, :], lambda t: iqT[rows, h // 2, t * P:(t + 1) * P], ikT[rows, :]).then_inc(lg_done, 1)

            pe.wait_ge(tab_landed, 16 * 2)
            pe.wait_ge(tp_copied, TP_AB)
            for h in range(2):
                index_logits(h)
            for c in range(4):
                ins = nc.tensor.transpose(ps_y[:, 0, c * P:(c + 1) * P], w_uk[:, c * P:(c + 1) * P], ident[:, :])
            ins.then_inc(ukT_done, 1)
            pe.wait_ge(ukT_copied, 1)
            for h in range(B_HEADS):
                need(pe, ql_copied, h - 1)
                rows = slice((h % 2) * HD, (h % 2 + 1) * HD)
                nc.tensor.matmul(ps_y[:, h % 2, 0:SEQ], w_ukT[rows, h // 2, :], qT_b[rows, h // 2, :],
                                 start=True, stop=True).then_inc(ql_done, 1)
                if h + 2 < B_HEADS:
                    index_logits(h + 2)
            pe.wait_ge(lg_used, B_HEADS)
            pe.wait_ge(ql_copied, B_HEADS)
            pe.wait_ge(modcol_done, 8)

            def keep_warm(b, n):
                for _ in range(n):
                    nc.tensor.matmul(ps_u[:, b, 3 * P:4 * P], ident[:, :], ident[:, :], start=True, stop=True)

            for step in range(STEPS):
                h = step
                if h < HEADS:
                    need(pe, s_biased, h - 1)
                    if h < A_HEADS:
                        rows = slice((h % 2) * HD, (h % 2 + 1) * HD)
                        ins = two_tiles(ps_g[:, h % 2, :], lambda t: qT_a[rows, h // 2, t * P:(t + 1) * P],
                                        akT[rows, h // (A_HEADS // A_KV), :])
                    else:
                        ins = two_tiles(ps_g[:, h % 2, :], lambda t: qlatT[:, h - A_HEADS, t * P:(t + 1) * P], ckvT)
                    ins.then_inc(s_done, 1)
                h = step - 2
                if 0 <= h < HEADS:
                    need(pe, pt_copied, h - 1)
                    keep_warm(h % 2, 5)
                    pe.wait_ge(p_ready, h + 1)
                    for c in range(2):
                        nc.tensor.transpose(ps_u[:, h % 2, c * P:(c + 1) * P], pr[:, h % 2, c * P:(c + 1) * P], ident[:, :])
                    nc.tensor.transpose(ps_u[:, h % 2, 2 * P:3 * P], pr[:, h % 2, 2 * P:3 * P], ident[:, :]).then_inc(pt_done, 1)
                h = step - 3
                if 0 <= h < HEADS:
                    pe.wait_ge(pt_copied, h + 1)
                    if h < A_HEADS:
                        q = h // 2
                        need(pe, o_lo_done, q - 1)
                        kv = AV + (h // (A_HEADS // A_KV)) * HD
                        o = ps_t[(h % 2) * HD:(h % 2 + 1) * HD, q % 2, 0:SEQ]
                        values = [proj[:, t, kv:kv + HD] for t in range(TILES)]
                    else:
                        need(pe, ol_copied, h - A_HEADS - 1)
                        o = ps_y[:, h % 2, 0:SEQ]
                        values = [ckv[:, t, :] for t in range(TILES)]
                    nc.tensor.matmul(o, values[0], pT[:, h % 2, 0:SEQ], start=True, stop=False)
                    ins = nc.tensor.matmul(o[:, P:SEQ], values[1], pT[:, h % 2, SEQ:3 * P], start=False, stop=True)
                    ins.then_inc(pv_done, 1)
                h = step - 5
                if A_HEADS <= h < HEADS:
                    q = h // 2
                    pe.wait_ge(ol_copied, h - A_HEADS + 1)
                    pe.wait_ge(o_lo_done, q - 1)
                    ins = nc.tensor.matmul(ps_t[(h % 2) * HD:(h % 2 + 1) * HD, q % 2, 0:SEQ],
                                           w_uv[:, (h - A_HEADS) * HD:(h - A_HEADS + 1) * HD], olatT[:, h % 2, :], start=True, stop=True)
                    ins.then_inc(uv_done, 1)

            pe.wait_ge(ol_copied, B_HEADS)
            transposes(TP_AB, len(TP))
            pe.wait_ge(tp_copied, len(TP))
            pe.wait_ge(o_lo_done, HEADS // 2)
            for step in range(C_HEADS + 1):
                h = step
                if h < C_HEADS:
                    rows = slice((h % 2) * HD, (h % 2 + 1) * HD)
                    need(pe, r_decayed, h - 1)
                    nc.tensor.matmul(ps_g[:, h % 2, 0:SEQ], ckT[rows, h // 2, 0:P], cqT[rows, h // 2, :], start=True, stop=True)
                    nc.tensor.matmul(ps_g[:, h % 2, SEQ:3 * P], ckT[rows, h // 2, P:SEQ], cqT[rows, h // 2, P:SEQ],
                                     start=True, stop=True).then_inc(r_done, 1)
                h = step - 1
                if h >= 0:
                    pe.wait_ge(r_decayed, h + 1)
                    v = [proj[:, t, CV + h * HD:CV + (h + 1) * HD] for t in range(TILES)]
                    cols = slice(h * HD, (h + 1) * HD)
                    nc.tensor.matmul(ps_t[:, 0, cols], sc[:, h % 2, 0:P], v[0], start=True, stop=True)
                    nc.tensor.matmul(ps_t[:, 1, cols], sc[:, h % 2, P:SEQ], v[0], start=True, stop=False)
                    nc.tensor.matmul(ps_t[:, 1, cols], sc[:, h % 2, SEQ:3 * P], v[1], start=False, stop=True).then_inc(ro_done_head, 1)

            out_group(G_OUT, xT_hi, xT_lo, 0, 4, Y_OUT, range(0, 1))
            pe.wait_ge(ro_copied, 1)
            out_group(G_OUT, xT_hi, xT_lo, 0, 4, Y_OUT, range(1, 4))
            out_group(G_OUT + 1, xT_hi, xT_lo, 4, 4, Y_OUT + 4)
            pe.wait_ge(oc_ready, 1)
            for b in range(2):
                for c in range(2):
                    for t in range(TILES):
                        k = 2 * b + c
                        ins = nc.tensor.transpose(ps_g[:, b, c * SEQ + t * P:c * SEQ + (t + 1) * P], cent[:, t, k * P:(k + 1) * P], ident[:, :])
                ins.then_inc(oct_done, 1)
            out_group(G_OUT + 2, xT_hi, xT_lo, 8, 4, Y_OUT + 8)
            pe.wait_ge(mix_ready, 1)
            gate_rows(0, ADA_IN)
            out_group(G_OUT + 3, xT_hi, xT_lo, 12, 4, Y_OUT + 12)
            transpose_x(2)
            ffn_pe(1)


_INS = ["x", "c", "ada_w", "ada_b", "norm_g", "ffn1_w_in", "ffn1_w_out", "ffn2_w_in", "ffn2_w_out", "mix_w_in", "mix_w_out",
        "swa_sinks", "dsa_kv_norm", "dsa_w_uk", "dsa_w_uv", "ret_norm"]


def shape_constants():
    i = np.arange(P)[:, None].astype(np.float64)
    j = np.arange(P)[None, :].astype(np.float64)
    own = np.where(j <= i, i - j, BIG)
    window = np.where(j > i, i - j + P, BIG)
    gamma = 1.0 - 2.0 ** (-5.0 - np.arange(C_HEADS))
    q = np.arange(SEQ)[None, None, :]
    diff = q - np.arange(P)[:, None, None]
    decays = np.where(diff >= 0, gamma[None, :, None] ** np.maximum(diff, 0), 0.0) * HD ** -0.5
    parts = [np.eye(P), own, window, own, own, i - j + P, own, decays.reshape(P, -1)]
    return np.concatenate(parts, axis=1).astype(np.float32)


def kernel(**inputs):
    import concourse.bacc as _bacc
    from concourse.bass_utils import run_bass_kernel_spmd as _run

    nc = _bacc.Bacc("TRN2", target_bir_lowering=False, num_devices=1)
    arrays, args = {}, []
    given = {name: np.ascontiguousarray(inputs[name]) for name in _INS}
    given["consts"] = shape_constants()
    for name, a in given.items():
        arrays[f"in_{name}"] = a
        args.append(nc.dram_tensor(f"in_{name}", a.shape, mybir.dt.from_np(a.dtype), kind="ExternalInput").ap())
    args.append(nc.dram_tensor("out", (1, SEQ, D), F32, kind="ExternalOutput").ap())
    build(nc, *args)
    r = _run(nc, [arrays], core_ids=[0])
    return r.results[0]["out"]
```
